# Optimizing a Trainium2 kernel written in Bass

```python
import jax, jax.numpy as jnp
from jax import lax
import numpy as np

D_MODEL = 1024
BATCH = 1
SEQ = 256
DEPTH = 2

N_HEADS = 16
N_KV_GROUPS = 2
HEADS_PER_GROUP = N_HEADS // N_KV_GROUPS
HEAD_DIM = 64
N_KV_PARTS = 6
N_BRANCH = 3
L_CMP = 32
STRIDE_CMP = 16
L_SLC = 64
N_SEL = 16
WINDOW = 512
Q_CHUNK = 64
CONV_WIDTH = 31
FFN_HIDDEN = -(-(8 * D_MODEL) // (3 * 256)) * 256
EPS = 1e-6
NEG = -1e30
FORCE = 1e9


def rmsnorm(x, g):
    xf = x.astype(jnp.float32)
    y = xf * lax.rsqrt(jnp.mean(xf * xf, axis=-1, keepdims=True) + EPS)
    return (y * g.astype(jnp.float32)).astype(x.dtype)

def layernorm(x, g, b):
    xf = x.astype(jnp.float32)
    mu = jnp.mean(xf, axis=-1, keepdims=True)
    var = jnp.mean(jnp.square(xf - mu), axis=-1, keepdims=True)
    y = (xf - mu) * lax.rsqrt(var + EPS)
    return (y * g.astype(jnp.float32) + b.astype(jnp.float32)).astype(x.dtype)

def swiglu_ffn(x, norm_g, w_in, w_out):
    gate, up = jnp.split(rmsnorm(x, norm_g) @ w_in, 2, axis=-1)
    return (jax.nn.silu(gate) * up) @ w_out

def conformer_conv(x, norm_g, pw1_w, pw1_b, dw_w, dw_b, ln_g, ln_b, pw2_w, pw2_b):
    a, b = jnp.split(rmsnorm(x, norm_g) @ pw1_w + pw1_b, 2, axis=-1)
    h = a * jax.nn.sigmoid(b)
    h = lax.conv_general_dilated(
        h, dw_w[:, None, :], window_strides=(1,),
        padding=[(CONV_WIDTH - 1, 0)],
        dimension_numbers=('NWC', 'WIO', 'NWC'),
        feature_group_count=h.shape[-1]) + dw_b
    h = jax.nn.silu(layernorm(h, ln_g, ln_b))
    return h @ pw2_w + pw2_b

def shared_kv(h, kv_norm, w_kv, cmp_pos_k, cmp_pos_v, phi_k_w1, phi_k_w2, phi_v_w1, phi_v_w2):
    B, S, _ = h.shape
    kv = (rmsnorm(h, kv_norm) @ w_kv).reshape(B, S, N_KV_PARTS, N_KV_GROUPS, HEAD_DIM)
    kv = kv.transpose(2, 0, 3, 1, 4)
    k_cmp_raw, v_cmp_raw, k_slc, v_slc, k_win, v_win = kv
    n_cmp = (S - L_CMP) // STRIDE_CMP + 1
    idx = np.arange(n_cmp)[:, None] * STRIDE_CMP + np.arange(L_CMP)[None, :]

    def compress(raw, pos, w1, w2):
        blk = raw[:, :, idx] + pos
        blk = blk.reshape(B, N_KV_GROUPS, n_cmp, L_CMP * HEAD_DIM)
        return jax.nn.silu(blk @ w1) @ w2

    k_cmp = compress(k_cmp_raw, cmp_pos_k, phi_k_w1, phi_k_w2)
    v_cmp = compress(v_cmp_raw, cmp_pos_v, phi_v_w1, phi_v_w2)
    n_slc = S // L_SLC
    k_slc_blk = k_slc.reshape(B, N_KV_GROUPS, n_slc, L_SLC, HEAD_DIM)
    v_slc_blk = v_slc.reshape(B, N_KV_GROUPS, n_slc, L_SLC, HEAD_DIM)
    pad = ((0, 0), (0, 0), (WINDOW, 0), (0, 0))
    k_win_pad = jnp.pad(k_win, pad)
    v_win_pad = jnp.pad(v_win, pad)
    return (k_cmp, v_cmp, k_slc_blk, v_slc_blk, k_win_pad, v_win_pad)

def nsa_attention(x, norm_g, w_in, w_out, kv):
    k_cmp, v_cmp, k_slc_blk, v_slc_blk, k_win_pad, v_win_pad = kv
    B, S, _ = x.shape
    G, Hg, dh = N_KV_GROUPS, HEADS_PER_GROUP, HEAD_DIM
    n_chunk = S // Q_CHUNK
    n_cmp = k_cmp.shape[2]
    n_slc = k_slc_blk.shape[2]
    k_sel = min(N_SEL, n_slc)
    scale = HEAD_DIM ** -0.5

    proj = rmsnorm(x, norm_g) @ w_in
    q = proj[..., :N_HEADS * dh]
    gates = jax.nn.sigmoid(proj[..., N_HEADS * dh:])
    q = q.reshape(B, n_chunk, Q_CHUNK, G, Hg, dh).transpose(1, 0, 3, 4, 2, 5)
    gates = gates.reshape(B, n_chunk, Q_CHUNK, N_BRANCH, G, Hg).transpose(1, 3, 0, 4, 5, 2)
    starts = jnp.arange(n_chunk, dtype=jnp.int32) * Q_CHUNK

    slopes = jnp.asarray(2.0 ** (-8.0 * (np.arange(N_HEADS) + 1) / N_HEADS), jnp.float32)
    slopes = slopes.reshape(G, Hg)[:, :, None, None]
    cmp_end = jnp.arange(n_cmp, dtype=jnp.int32) * STRIDE_CMP + (L_CMP - 1)
    cs = np.arange(n_cmp)[:, None] * STRIDE_CMP
    ss = np.arange(n_slc)[None, :] * L_SLC
    overlap = jnp.asarray((cs <= ss + L_SLC - 1) & (cs + L_CMP - 1 >= ss), jnp.float32)
    blk = jnp.arange(n_slc, dtype=jnp.int32)
    bidx = jnp.arange(B)[:, None, None, None]
    gidx = jnp.arange(G)[None, :, None, None]

    def chunk_fn(args):
        q_c, g_c, c0 = args
        t = c0 + jnp.arange(Q_CHUNK, dtype=jnp.int32)

        dist = (t[:, None] - cmp_end[None, :]).astype(jnp.float32)
        valid = dist >= 0
        s = jnp.einsum('bghqd,bgnd->bghqn', q_c, k_cmp).astype(jnp.float32) * scale
        s = jnp.where(valid, s - slopes * dist, NEG)
        p_cmp = jax.nn.softmax(s, axis=-1) * valid.any(-1, keepdims=True)
        o_cmp = jnp.einsum('bghqn,bgnd->bghqd', p_cmp.astype(v_cmp.dtype), v_cmp)

        imp = jnp.einsum('bghqn,nj->bgqj', p_cmp, overlap)
        t_blk = t // L_SLC
        forced = (blk[None] == 0) | (blk[None] == t_blk[:, None]) | (blk[None] == t_blk[:, None] - 1)
        causal = blk[None] * L_SLC <= t[:, None]
        imp = jnp.where(forced, FORCE, jnp.where(causal, imp, -FORCE))
        _, sel = lax.top_k(imp, k_sel)
        ks = k_slc_blk[bidx, gidx, sel]
        vs = v_slc_blk[bidx, gidx, sel]
        pos = sel[..., None] * L_SLC + jnp.arange(L_SLC, dtype=jnp.int32)
        dist = (t[None, None, :, None, None] - pos).astype(jnp.float32)[:, :, None]
        s = jnp.einsum('bghqd,bgqkld->bghqkl', q_c, ks).astype(jnp.float32) * scale
        s = jnp.where(dist >= 0, s - slopes[..., None] * dist, NEG)
        p = jax.nn.softmax(s.reshape(B, G, Hg, Q_CHUNK, k_sel * L_SLC), axis=-1)
        o_slc = jnp.einsum('bghqm,bgqmd->bghqd', p.astype(vs.dtype),
                           vs.reshape(B, G, Q_CHUNK, k_sel * L_SLC, dh))

        kw = lax.dynamic_slice_in_dim(k_win_pad, c0, WINDOW + Q_CHUNK, axis=2)
        vw = lax.dynamic_slice_in_dim(v_win_pad, c0, WINDOW + Q_CHUNK, axis=2)
        s_pos = c0 - WINDOW + jnp.arange(WINDOW + Q_CHUNK, dtype=jnp.int32)
        dist = (t[:, None] - s_pos[None, :]).astype(jnp.float32)
        ok = (dist >= 0) & (dist < WINDOW) & (s_pos[None, :] >= 0)
        s = jnp.einsum('bghqd,bgmd->bghqm', q_c, kw).astype(jnp.float32) * scale
        s = jnp.where(ok, s - slopes * dist, NEG)
        p = jax.nn.softmax(s, axis=-1)
        o_win = jnp.einsum('bghqm,bgmd->bghqd', p.astype(vw.dtype), vw)

        o = (g_c[0][..., None] * o_cmp + g_c[1][..., None] * o_slc
             + g_c[2][..., None] * o_win)
        return o.transpose(0, 3, 1, 2, 4).reshape(B, Q_CHUNK, N_HEADS * dh).astype(x.dtype)

    out = lax.map(chunk_fn, (q, gates, starts))
    out = out.transpose(1, 0, 2, 3).reshape(B, S, N_HEADS * dh)
    return out @ w_out

def first_inputs(seed: int = 0) -> dict:
    key = jax.random.key(seed)
    ks = jax.random.split(key, 32)
    n_a = DEPTH // 2
    n_b = DEPTH - n_a
    D, F = D_MODEL, FFN_HIDDEN
    f32 = jnp.float32

    def w(k, shape, fan_in):
        return jax.random.normal(k, shape, f32) * fan_in ** -0.5

    def gain(k, shape):
        return 1.0 + 0.05 * jax.random.normal(k, shape, f32)

    def bias(k, shape):
        return 0.02 * jax.random.normal(k, shape, f32)

    return {
        "x": jax.random.normal(ks[0], (BATCH, SEQ, D), f32),
        "a_norm": gain(ks[1], (n_a, D)),
        "a_pw1_w": w(ks[2], (n_a, D, 2 * D), D),
        "a_pw1_b": bias(ks[3], (n_a, 2 * D)),
        "a_dw_w": w(ks[4], (n_a, CONV_WIDTH, D), CONV_WIDTH),
        "a_dw_b": bias(ks[5], (n_a, D)),
        "a_ln_g": gain(ks[6], (n_a, D)),
        "a_ln_b": bias(ks[7], (n_a, D)),
        "a_pw2_w": w(ks[8], (n_a, D, D), D),
        "a_pw2_b": bias(ks[9], (n_a, D)),
        "kv_norm": gain(ks[10], (D,)),
        "w_kv": w(ks[11], (D, N_KV_PARTS * N_KV_GROUPS * HEAD_DIM), D),
        "cmp_pos_k": 0.1 * jax.random.normal(ks[12], (L_CMP, HEAD_DIM), f32),
        "cmp_pos_v": 0.1 * jax.random.normal(ks[13], (L_CMP, HEAD_DIM), f32),
        "phi_k_w1": w(ks[14], (L_CMP * HEAD_DIM, HEAD_DIM), L_CMP * HEAD_DIM),
        "phi_k_w2": w(ks[15], (HEAD_DIM, HEAD_DIM), HEAD_DIM),
        "phi_v_w1": w(ks[16], (L_CMP * HEAD_DIM, HEAD_DIM), L_CMP * HEAD_DIM),
        "phi_v_w2": w(ks[17], (HEAD_DIM, HEAD_DIM), HEAD_DIM),
        "b_norm": gain(ks[18], (n_b, D)),
        "b_w_in": w(ks[19], (n_b, D, N_HEADS * HEAD_DIM + N_BRANCH * N_HEADS), D),
        "b_w_out": w(ks[20], (n_b, N_HEADS * HEAD_DIM, D), N_HEADS * HEAD_DIM),
        "ffn_norm": gain(ks[21], (DEPTH, D)),
        "ffn_w_in": w(ks[22], (DEPTH, D, 2 * F), D),
        "ffn_w_out": w(ks[23], (DEPTH, F, D), F),
        "final_norm": gain(ks[24], (D,)),
    }

def first_block(x, a_norm, a_pw1_w, a_pw1_b, a_dw_w, a_dw_b, a_ln_g, a_ln_b, a_pw2_w, a_pw2_b,
              kv_norm, w_kv, cmp_pos_k, cmp_pos_v, phi_k_w1, phi_k_w2, phi_v_w1, phi_v_w2,
              b_norm, b_w_in, b_w_out, ffn_norm, ffn_w_in, ffn_w_out, final_norm):
    n_a = DEPTH // 2
    h = x
    kv = None
    for layer in range(DEPTH):
        if layer < n_a:
            i = layer
            h = h + conformer_conv(h, a_norm[i], a_pw1_w[i], a_pw1_b[i], a_dw_w[i], a_dw_b[i],
                                   a_ln_g[i], a_ln_b[i], a_pw2_w[i], a_pw2_b[i])
        else:
            j = layer - n_a
            h = h + nsa_attention(h, b_norm[j], b_w_in[j], b_w_out[j], kv)
        h = h + swiglu_ffn(h, ffn_norm[layer], ffn_w_in[layer], ffn_w_out[layer])
        if layer == n_a - 1:
            kv = shared_kv(h, kv_norm, w_kv, cmp_pos_k, cmp_pos_v,
                           phi_k_w1, phi_k_w2, phi_v_w1, phi_v_w2)
    return rmsnorm(h, final_norm)


DEPTH_2 = 1

N_MEM = 256
D_MIX = D_MODEL
ML_HEADS = 4
ML_DH = D_MIX // 2 // ML_HEADS
ML_W = ML_HEADS * ML_DH
ML_CHUNK = 64
CONV_W = 4
FX_HEADS = 8
FX_DH = (D_MIX - ML_W) // FX_HEADS
FX_W = FX_HEADS * FX_DH
Q_BLOCK = 128
X_HEADS = 4
X_DH = D_MODEL // X_HEADS
D_FF = 4 * D_MODEL
IN_SIZES = (2 * ML_W, ML_W, ML_W, ML_HEADS, ML_HEADS, FX_W, FX_W, FX_W, FX_HEADS)
IN_COLS = 4 * ML_W + 2 * ML_HEADS + 3 * FX_W + FX_HEADS


def rmsnorm_2(x, g):
    xf = x.astype(jnp.float32)
    y = xf * lax.rsqrt(jnp.mean(xf * xf, axis=-1, keepdims=True) + EPS)
    return (y * g.astype(jnp.float32)).astype(x.dtype)

def causal_conv(u, w, b):
    S = u.shape[1]
    up = jnp.pad(u, ((0, 0), (CONV_W - 1, 0), (0, 0)))
    out = b
    for j in range(CONV_W):
        out = out + up[:, j:j + S] * w[j]
    return out

def mlstm_chunkwise(q, k, v, ig, lf):
    B, S, H, dh = q.shape
    nc = S // ML_CHUNK
    k = k * (dh ** -0.5)

    def to_chunks(t):
        t = t.reshape((B, nc, ML_CHUNK) + t.shape[2:])
        return jnp.moveaxis(t, (1, 3), (0, 2))

    causal = jnp.tril(jnp.ones((ML_CHUNK, ML_CHUNK), dtype=bool))

    def body(carry, xs):
        C, n, m = carry
        qc, kc, vc, ic, fc = xs
        b = jnp.cumsum(fc, axis=-1)
        g = b[..., -1]
        dmat = b[..., :, None] - b[..., None, :] + ic[..., None, :]
        dmat = jnp.where(causal, dmat, -jnp.inf)
        m_inter = b + m[..., None]
        m_t = jnp.maximum(m_inter, jnp.max(dmat, axis=-1))
        scores = jnp.einsum('bhtd,bhsd->bhts', qc, kc) * jnp.exp(dmat - m_t[..., None])
        inter = jnp.exp(m_inter - m_t)
        num = (jnp.einsum('bhts,bhsd->bhtd', scores, vc)
               + inter[..., None] * jnp.einsum('bhed,bhtd->bhte', C, qc))
        den = scores.sum(-1) + inter * jnp.einsum('bhd,bhtd->bht', n, qc)
        h = num / jnp.maximum(jnp.abs(den), jnp.exp(-m_t))[..., None]
        a = g[..., None] - b + ic
        m_new = jnp.maximum(g + m, jnp.max(a, axis=-1))
        decay = jnp.exp(g + m - m_new)
        wa = jnp.exp(a - m_new[..., None])
        C_new = decay[..., None, None] * C + jnp.einsum('bhs,bhse,bhsd->bhed', wa, vc, kc)
        n_new = decay[..., None] * n + jnp.einsum('bhs,bhsd->bhd', wa, kc)
        return (C_new, n_new, m_new), h

    init = (jnp.zeros((B, H, dh, dh), jnp.float32), jnp.zeros((B, H, dh), jnp.float32),
            jnp.zeros((B, H), jnp.float32))
    _, hs = lax.scan(body, init, (to_chunks(q), to_chunks(k), to_chunks(v), to_chunks(ig), to_chunks(lf)))
    hs = jnp.moveaxis(hs, (0, 2), (1, 3))
    return hs.reshape(B, S, H, dh)

def forgetting_attention(q, k, v, lf):
    B, S, H, dh = q.shape
    nb = S // Q_BLOCK
    cT = jnp.cumsum(lf, axis=1).transpose(0, 2, 1)
    qb = q.reshape(B, nb, Q_BLOCK, H, dh).transpose(1, 0, 2, 3, 4)
    cb = cT.reshape(B, H, nb, Q_BLOCK).transpose(2, 0, 1, 3)
    kpos = jnp.arange(S)
    scale = dh ** -0.5

    def block(args):
        qi, ci, blk = args
        qpos = blk * Q_BLOCK + jnp.arange(Q_BLOCK)
        s = jnp.einsum('bqhd,bkhd->bhqk', qi, k, preferred_element_type=jnp.float32) * scale
        s = s + (ci[..., :, None] - cT[..., None, :])
        s = jnp.where(qpos[:, None] >= kpos[None, :], s, -jnp.inf)
        p = jax.nn.softmax(s, axis=-1)
        return jnp.einsum('bhqk,bkhd->bqhd', p.astype(v.dtype), v)

    out = lax.map(block, (qb, cb, jnp.arange(nb)))
    return out.transpose(1, 0, 2, 3, 4).reshape(B, S, H, dh)

def cross_attention(h, memn, w_q, w_kv, w_o):
    B, S, D = h.shape
    M = memn.shape[1]
    q = (h @ w_q).reshape(B, S, X_HEADS, X_DH)
    k, v = jnp.split(memn @ w_kv, 2, axis=-1)
    k = k.reshape(B, M, X_HEADS, X_DH)
    v = v.reshape(B, M, X_HEADS, X_DH)
    s = jnp.einsum('bqhd,bmhd->bhqm', q, k, preferred_element_type=jnp.float32) * (X_DH ** -0.5)
    p = jax.nn.softmax(s, axis=-1)
    o = jnp.einsum('bhqm,bmhd->bqhd', p.astype(v.dtype), v).reshape(B, S, D)
    return o @ w_o

def second_inputs(seed: int = 0) -> dict:
    key = jax.random.key(seed)
    ks = jax.random.split(key, 24)
    f32 = jnp.float32

    def w(k, shape, fan_in):
        return jax.random.normal(k, shape, f32) * (fan_in ** -0.5)

    def gain(k, shape):
        return 1.0 + 0.1 * jax.random.normal(k, shape, f32)

    def small(k, shape):
        return 0.01 * jax.random.normal(k, shape, f32)

    return {
        "x": jax.random.normal(ks[0], (BATCH, SEQ, D_MODEL), f32),
        "mem": jax.random.normal(ks[1], (BATCH, N_MEM, D_MODEL), f32),
        "ln1": gain(ks[2], (DEPTH_2, D_MODEL)),
        "w_in": w(ks[3], (DEPTH_2, D_MODEL, IN_COLS), D_MODEL),
        "ml_conv_w": w(ks[4], (DEPTH_2, CONV_W, 2 * ML_W), CONV_W),
        "ml_conv_b": small(ks[5], (DEPTH_2, 2 * ML_W)),
        "ml_b_i": small(ks[6], (DEPTH_2, ML_HEADS)),
        "ml_b_f": 3.0 + 0.1 * jax.random.normal(ks[7], (DEPTH_2, ML_HEADS), f32),
        "ml_norm": gain(ks[8], (DEPTH_2, ML_W)),
        "fx_b_f": 3.0 + 0.1 * jax.random.normal(ks[9], (DEPTH_2, FX_HEADS), f32),
        "w_out": w(ks[10], (DEPTH_2, D_MIX, D_MODEL), D_MIX),
        "ln_x": gain(ks[11], (DEPTH_2, D_MODEL)),
        "ln_mem": gain(ks[12], (DEPTH_2, D_MODEL)),
        "w_xq": w(ks[13], (DEPTH_2, D_MODEL, D_MODEL), D_MODEL),
        "w_xkv": w(ks[14], (DEPTH_2, D_MODEL, 2 * D_MODEL), D_MODEL),
        "w_xo": w(ks[15], (DEPTH_2, D_MODEL, D_MODEL), D_MODEL),
        "ln2": gain(ks[16], (DEPTH_2, D_MODEL)),
        "w_ff1": w(ks[17], (DEPTH_2, D_MODEL, D_FF), D_MODEL),
        "w_ff2": w(ks[18], (DEPTH_2, D_FF, D_MODEL), D_FF),
        "ln_f": gain(ks[19], (D_MODEL,)),
    }

def second_block(x, mem, ln1, w_in, ml_conv_w, ml_conv_b, ml_b_i, ml_b_f, ml_norm, fx_b_f, w_out,
              ln_x, ln_mem, w_xq, w_xkv, w_xo, ln2, w_ff1, w_ff2, ln_f):
    B, S, _ = x.shape
    splits = [int(v) for v in np.cumsum(IN_SIZES)[:-1]]
    for l in range(DEPTH_2):
        h = rmsnorm_2(x, ln1[l])
        z = h @ w_in[l]
        ml_qk, ml_v, ml_o, ml_i, ml_f, fx_q, fx_k, fx_v, fx_f = jnp.split(z, splits, axis=-1)

        ml_qk = jax.nn.silu(causal_conv(ml_qk, ml_conv_w[l], ml_conv_b[l]))
        mq, mk = jnp.split(ml_qk.astype(jnp.float32), 2, axis=-1)
        mq = mq.reshape(B, S, ML_HEADS, ML_DH)
        mk = mk.reshape(B, S, ML_HEADS, ML_DH)
        mv = ml_v.astype(jnp.float32).reshape(B, S, ML_HEADS, ML_DH)
        ig = ml_i.astype(jnp.float32) + ml_b_i[l].astype(jnp.float32)
        lf = jax.nn.log_sigmoid(ml_f.astype(jnp.float32) + ml_b_f[l].astype(jnp.float32))
        mh = mlstm_chunkwise(mq, mk, mv, ig, lf)
        mh = mh * lax.rsqrt(jnp.mean(mh * mh, axis=-1, keepdims=True) + EPS)
        mh = mh * ml_norm[l].astype(jnp.float32).reshape(ML_HEADS, ML_DH)
        ml_out = (mh.reshape(B, S, ML_W) * jax.nn.sigmoid(ml_o.astype(jnp.float32))).astype(x.dtype)

        fq = fx_q.reshape(B, S, FX_HEADS, FX_DH)
        fk = fx_k.reshape(B, S, FX_HEADS, FX_DH)
        fv = fx_v.reshape(B, S, FX_HEADS, FX_DH)
        flf = jax.nn.log_sigmoid(fx_f.astype(jnp.float32) + fx_b_f[l].astype(jnp.float32))
        fx_out = forgetting_attention(fq, fk, fv, flf).reshape(B, S, FX_W)

        x = x + jnp.concatenate([ml_out, fx_out], axis=-1) @ w_out[l]

        x = x + cross_attention(rmsnorm_2(x, ln_x[l]), rmsnorm_2(mem, ln_mem[l]), w_xq[l], w_xkv[l], w_xo[l])

        u = jax.nn.relu(rmsnorm_2(x, ln2[l]) @ w_ff1[l])
        x = x + (u * u) @ w_ff2[l]
    return rmsnorm_2(x, ln_f)


def setup_inputs(seed=0):
    out = dict(first_inputs(seed))
    for name, value in second_inputs(seed + 1).items():
        if name != "x":
            out[name + "_2"] = value
    return out


def reference(
    x, a_norm, a_pw1_w, a_pw1_b, a_dw_w, a_dw_b, a_ln_g, a_ln_b, a_pw2_w, a_pw2_b, kv_norm,
    w_kv, cmp_pos_k, cmp_pos_v, phi_k_w1, phi_k_w2, phi_v_w1, phi_v_w2, b_norm, b_w_in, b_w_out,
    ffn_norm, ffn_w_in, ffn_w_out, final_norm, mem_2, ln1_2, w_in_2, ml_conv_w_2, ml_conv_b_2,
    ml_b_i_2, ml_b_f_2, ml_norm_2, fx_b_f_2, w_out_2, ln_x_2, ln_mem_2, w_xq_2, w_xkv_2, w_xo_2,
    ln2_2, w_ff1_2, w_ff2_2, ln_f_2,
):
    x = first_block(
        x, a_norm, a_pw1_w, a_pw1_b, a_dw_w, a_dw_b, a_ln_g, a_ln_b, a_pw2_w, a_pw2_b, kv_norm,
        w_kv, cmp_pos_k, cmp_pos_v, phi_k_w1, phi_k_w2, phi_v_w1, phi_v_w2, b_norm, b_w_in,
        b_w_out, ffn_norm, ffn_w_in, ffn_w_out, final_norm,
    )
    return second_block(
        x, mem_2, ln1_2, w_in_2, ml_conv_w_2, ml_conv_b_2, ml_b_i_2, ml_b_f_2, ml_norm_2,
        fx_b_f_2, w_out_2, ln_x_2, ln_mem_2, w_xq_2, w_xkv_2, w_xo_2, ln2_2, w_ff1_2, w_ff2_2,
        ln_f_2,
    )


_drawn_inputs = setup_inputs


def setup_inputs(seed=0):
    import zlib

    import numpy as np

    out = dict(_drawn_inputs(seed))
    spreads = {}
    factors = {'a_ln_b': 3.12,
     'cmp_pos_k': 8.0,
     'b_norm': 4.921,
     'ml_conv_b_2': 8.0,
     'ml_b_i_2': 64.0,
     'ml_b_f_2': 34.936,
     'fx_b_f_2': 26.168,
     'ln_x_2': 5.077,
     'ln_mem_2': 3.583}
    for name, (base, spread) in spreads.items():
        noise = np.random.default_rng([zlib.crc32(name.encode()), seed]).standard_normal(out[name].shape)
        drawn = base * np.exp(spread * noise) if base else spread * noise
        out[name] = __import__('jax').numpy.asarray(drawn.astype(out[name].dtype))
    for name, factor in factors.items():
        out[name] = (out[name] * factor).astype(out[name].dtype)
    return out
```

```python
from contextlib import ExitStack

import concourse.bass as bass
from concourse import mybir

F32 = mybir.dt.float32
ACT = mybir.ActivationFunctionType
ALU = mybir.AluOpType
AX = mybir.AxisListType

P = 128
S, D = 256, 1024
TT = S // P
KT = D // P
EPS = 1e-6
NEG = -1e30
TAPS, TAPS2 = 31, 4
F = 2816
FC = F // 256
FT = F // P
HEADS, GROUPS, DH = 16, 2, 64
NCMP = 15
MLH, MLD = 4, 128
FXH = 8
XH = 4
D_FF = 4 * D
SLOTS = 5
SLOT = 4096
TAPG = 8
XSCALE = (D // XH) ** -0.5
XKV_BANK = [4, 5, 0, 1, 2, 3, 4, 5]

VECS = [("a_norm", 8), ("a_pw1_b", 16), ("a_dw_b", 8), ("a_ln_g", 8), ("a_ln_b", 8),
        ("kv_norm", 8), ("b_norm", 8), ("ffn_norm", 16), ("final_norm", 8), ("ln1_2", 8),
        ("ml_conv_b_2", 8), ("ln_x_2", 8), ("ln_mem_2", 8), ("ln2_2", 8)]

CONV, FFN0, NSA, FFN1, MID, IN2, MEM, CROSS, FF, LAST = range(10)


def build_kernel(nc, a, out):
    col, n = {}, 0
    for name, rows in VECS:
        col[name] = n
        n += rows
    assert n == P

    ctx = ExitStack()
    with ctx:
        def sb(name, shape):
            return ctx.enter_context(nc.sbuf_tensor(name, shape, F32))

        def sem(name):
            return ctx.enter_context(nc.semaphore(name))

        ring = [sb(f"ring{i}", [P, SLOT]) for i in range(SLOTS)]
        h = sb("h", [P, TT, D])
        scaled = sb("scaled", [P, TT, D])
        xnT = sb("xnT", [P, KT, S])
        xnT2 = sb("xnT2", [P, KT, S])
        act = sb("act", [P, D_FF // P, S])
        actf = act[:, :, :].rearrange("p a b -> p (a b)")
        PAD = TAPS - 1
        u = sb("u", [P, KT, PAD + S])
        v = sb("v", [P, KT, S])
        vf = v[:, :, :].rearrange("p a b -> p (a b)")
        qT = sb("qT", [P, KT, S])
        qTf = qT[:, :, :].rearrange("p a b -> p (a b)")
        gain_mid = sb("gain_mid", [P, D])
        gain_last = sb("gain_last", [P, D])
        gain_ml = sb("gain_ml", [P, MLH * MLD])
        ident = sb("ident", [P, P])
        ones = sb("ones", [P, P])
        mean_w = sb("mean_w", [P, P])
        vecT = sb("vecT", [P, P])
        tapT = sb("tapT", [P, KT, TAPS + TAPS2])
        dist8 = sb("dist8", [P, 3 * P])
        dist8c = sb("dist8c", [P, TT, 16])
        causal = sb("causal", [P, 3 * P])
        causalT = sb("causalT", [P, 3 * P])
        valid = sb("valid", [P, 1])
        nhalf = sb("nhalf", [P, 8])
        posT = sb("posT", [P, 2, 32])
        soft = sb("soft", [P, 2, 800])
        softf = soft[:, :, :].rearrange("p a b -> p (a b)")
        pt = sb("pt", [P, 2, 1024])
        ptf = pt[:, :, :].rearrange("p a b -> p (a b)")
        ssq = sb("ssq", [P, 20])
        msq = sb("msq", [P, 20])
        rstd = sb("rstd", [P, 20])
        gates = sb("gates", [P, TT, 48])
        phi2 = sb("phi2", [P, 2, DH])
        hid = sb("hid", [P, 2, NCMP])
        kcmp = sb("kcmp", [P, GROUPS, NCMP])
        vcmp = sb("vcmp", [NCMP, GROUPS * DH])
        nmax = sb("nmax", [P, 2, 6])
        rsum = sb("rsum", [P, 2, 6])
        coef = sb("coef", [P, 2, 6])
        rcol = sb("rcol", [P, 2, 8])
        den = sb("den", [P, 6, 8])
        expm = sb("expm", [P, TT, 8])
        gate_bias = sb("gate_bias", [FXH, 3])
        bank = [ctx.enter_context(nc.psum_tensor(f"bank{i}", [P, 512], F32)) for i in range(8)]

        vecs = ptf[:, 0:P]
        taps = softf[0:TAPS + TAPS2, 0:D]
        pos = ptf[0:32, 256:512]
        pw2_row = gain_last[0:1, :]
        diag = actf.rearrange("p (g t c) -> p g t c", t=TAPG, c=P)
        NDIAG = 8
        window = actf[:, 0:2 * 32 * NCMP].rearrange("p (b l n) -> p b l n", b=2, l=32)
        BIAS = 416
        biases = actf[:, 1024:1024 + HEADS * BIAS].rearrange("p (h c) -> p h c", c=BIAS)
        k2 = vf[:, 0:1024].rearrange("p (g b k) -> p g b k", g=GROUPS, b=2)
        vtok = vf[:, 1024:1536].rearrange("p (t b c) -> p t b c", t=TT, b=2)
        memk = actf[:, 0:2048].rearrange("p (f m) -> p f m", m=S)
        memv = actf[:, 2048:4096].rearrange("p (t c) -> p t c", t=TT)
        MLV = MLD + 1
        mlv = actf[:, 4096:4096 + TT * MLH * MLV].rearrange("p (t h c) -> p t h c", t=TT, c=MLV)
        mlo = actf[:, 5136:6160].rearrange("p (t c) -> p t c", t=TT)
        fxv = actf[:, 6160:7184].rearrange("p (t c) -> p t c", t=TT)
        row = scaled[0:FXH, :, :].rearrange("p a b -> p (a b)").rearrange("p (r t) -> p r t", t=S)
        num = qTf[:, 0:TT * MLH * MLV].rearrange("p (i c) -> p i c", c=MLV)
        mlsq = u[:, :, :].rearrange("p a b -> p (a b)")[:, 0:TT * MLH * MLD].rearrange("p (i c) -> p i c", c=MLD)
        NSA_PIECES = [slice(256, 271), slice(0, 128), slice(128, 256),
                      slice(272, 287), slice(288, 544), slice(544, 800)]

        slot_loaded = [sem(f"slot_loaded{i}") for i in range(SLOTS)]
        slots_used = sem("slots_used")
        x_loaded = [sem("x_loaded0"), sem("x_loaded1")]
        vecs_loaded = sem("vecs_loaded")
        small_loaded = sem("small_loaded")
        mem_loaded = sem("mem_loaded")
        gains_loaded = sem("gains_loaded")
        last_gain_loaded = sem("last_gain_loaded")
        out_stored = sem("out_stored")
        pool_step = sem("pool_step")
        consts_built = sem("consts_built")
        bias_built = sem("bias_built")
        h_ready = sem("h_ready")
        ss_ready = sem("ss_ready")
        ms_ready = sem("ms_ready")
        rstd_ready = sem("rstd_ready")
        scaled_ready = sem("scaled_ready")
        turned = sem("turned")
        xn_ready = sem("xn_ready")
        acc_done = sem("acc_done")
        out_ready = sem("out_ready")
        pre_turned = sem("pre_turned")
        pre_copied = sem("pre_copied")
        up_done = sem("up_done")
        gate_act = sem("gate_act")
        glu_done = sem("glu_done")
        diag_built = sem("diag_built")
        diag_used = sem("diag_used")
        conv_out = sem("conv_out")
        stat_done = sem("stat_done")
        centred = sem("centred")
        squared = sem("squared")
        std_ready = sem("std_ready")
        rstd_row = sem("rstd_row")
        normed = sem("normed")
        silu_ready = sem("silu_ready")
        pads_zero = sem("pads_zero")
        kv_done = sem("kv_done")
        window_ready = sem("window_ready")
        kv_dve = sem("kv_dve")
        kv_act = sem("kv_act")
        phi_done = sem("phi_done")
        q_done = sem("q_done")
        q_ready = sem("q_ready")
        score_done = sem("score_done")
        shifted = sem("shifted")
        exp_done = sem("exp_done")
        dve_link = sem("dve_link")
        act_link = sem("act_link")
        weighed = sem("weighed")
        p_turned = sem("p_turned")
        pt_dve = sem("pt_dve")
        pt_act = sem("pt_act")
        pv_done = sem("pv_done")
        o_ready = sem("o_ready")
        in2_done = sem("in2_done")
        in2_act = sem("in2_act")
        in2_dve = sem("in2_dve")
        conv4_done = sem("conv4_done")
        qk_ready = sem("qk_ready")
        rows_done = sem("rows_done")
        cols_turned = sem("cols_turned")
        xkv_done = sem("xkv_done")
        xkv_act = sem("xkv_act")
        xkv_dve = sem("xkv_dve")
        ml_score = sem("ml_score")
        ml_shift = sem("ml_shift")
        ml_exp = sem("ml_exp")
        ml_weight = sem("ml_weight")
        ml_num = sem("ml_num")
        ml_copied = sem("ml_copied")
        ml_sq = sem("ml_sq")
        ml_ms = sem("ml_ms")
        ml_rstd = sem("ml_rstd")
        ml_out = sem("ml_out")
        ml_turned = sem("ml_turned")
        ml_ready = sem("ml_ready")

        chunks, first, freed = [], {}, []

        def chunk(stage, parts, by=None):
            first.setdefault(stage, len(chunks))
            chunks.append(parts)
            freed.append(by or (slots_used, 1 + sum(sm is slots_used for sm, _ in freed)))

        def wide(stage, w, start, width, by=None):
            src = w.rearrange("(k p) n -> p k n", p=P)[:, :, start:start + width]
            chunk(stage, [(lambda s: s[:, 0:KT * width].rearrange("p (k n) -> p k n", n=width), src)], by)

        def pair(stage, w, start, other, by):
            src = w.rearrange("(k p) n -> p k n", p=P)
            view = lambda s: s[:, :].rearrange("p (k b n) -> p k b n", k=KT, b=2)
            chunk(stage, [(lambda s, b=b: view(s)[:, :, b, :], src[:, :, c:c + 256])
                          for b, c in enumerate((start, other))], by)

        def tall(stage, w, rows, acc):
            src = w.rearrange("(k p) n -> p k n", p=P)
            for k in range(0, rows // P, 4):
                m = min(4, rows // P - k)
                chunk(stage, [(lambda s, m=m: s[:, 0:m * D].rearrange("p (k n) -> p k n", n=D),
                               src[:, k:k + m, :])], (acc_done, acc) if k + 4 >= rows // P else None)

        for c in range(4):
            pair("pw1", a["a_pw1_w"][0], 256 * c, D + 256 * c, (up_done, c + 1))
        for c in range(2):
            wide("pw2", a["a_pw2_w"][0], 512 * c, 512, (acc_done, 2 * c + 2))
        for c in range(FC):
            pair("ffn0_in", a["ffn_w_in"][0], 256 * c, F + 256 * c, (up_done, 4 + c + 1))
        tall("ffn0_out", a["ffn_w_out"][0], F, 8)
        wide("kv_a", a["w_kv"], 0, 512)
        wide("kv_b", a["w_kv"], 512, 256, (kv_done, 2))
        phis = [a["phi_k_w1"], a["phi_v_w1"]]
        chunk("phi", [(lambda s, g=g, b=b: s[DH * g:DH * g + DH, 2048 * b:2048 * b + 2048]
                       .rearrange("p (l e) -> p l e", e=DH),
                       phis[b].rearrange("(l d) e -> d l e", d=DH)) for g in range(2) for b in range(2)],
              (phi_done, 1))
        for c in range(2):
            wide("q", a["b_w_in"][0], 512 * c, 512, (q_done, 2 * c + 2))
        wide("gates", a["b_w_in"][0], D, 48, (q_done, 5))
        for c in range(2):
            wide("b_out", a["b_w_out"][0], 512 * c, 512, (acc_done, 8 + 2 * c + 2))
        for c in range(FC):
            pair("ffn1_in", a["ffn_w_in"][1], 256 * c, F + 256 * c, (up_done, 4 + FC + c + 1))
        tall("ffn1_out", a["ffn_w_out"][1], F, 16)
        w_in2 = a["w_in_2"][0]
        for c in range(2):
            wide("ml_qk", w_in2, 512 * c, 512, (in2_done, 2 * c + 2))
        wide("ml_v", w_in2, 1024, 512, (in2_done, 5))
        wide("ml_o", w_in2, 1536, 512, (in2_done, 6))
        wide("fx_q", w_in2, 2056, 512, (in2_done, 8))
        wide("fx_k", w_in2, 2568, 512, (in2_done, 10))
        wide("fx_v", w_in2, 3080, 512, (in2_done, 11))
        in2_src = w_in2.rearrange("(k p) n -> p k n", p=P)
        small_gates = lambda s: s[:, 0:KT * 16].rearrange("p (k n) -> p k n", n=16)
        chunk("rows", [(lambda s: small_gates(s)[:, :, 0:8], in2_src[:, :, 2048:2056]),
                       (lambda s: small_gates(s)[:, :, 8:16], in2_src[:, :, 3592:3600])], (in2_done, 12))
        for c in range(2):
            wide("xkv_k", a["w_xkv_2"][0], 512 * c, 512, (xkv_done, 2 * c + 2))
        for c in range(2, 4):
            wide("xkv_v", a["w_xkv_2"][0], 512 * c, 512, (xkv_done, 2 * c + 2))
        for c in range(2):
            wide("out2", a["w_out_2"][0], 512 * c, 512, (acc_done, 16 + 2 * c + 2))
        for c in range(2):
            wide("xq", a["w_xq_2"][0], 512 * c, 512, (q_done, 5 + 2 * c + 2))
        for c in range(2):
            wide("xo", a["w_xo_2"][0], 512 * c, 512, (acc_done, 20 + 2 * c + 2))
        for c in range(8):
            wide("ff1", a["w_ff1_2"][0], 512 * c, 512, (up_done, 4 + 2 * FC + c + 1))
        tall("ff2", a["w_ff2_2"][0], D_FF, 28)

        def loads_through(c):
            return 16 * sum(len(chunks[i]) for i in range(c % SLOTS, c + 1, SLOTS))

        turning = [CONV, FFN0, NSA, FFN1, IN2, MEM, CROSS, FF]
        gains = {CONV: [("a_norm", 0, xnT)], FFN0: [("ffn_norm", 0, xnT)],
                 NSA: [("kv_norm", 0, xnT2), ("b_norm", 0, xnT)], FFN1: [("ffn_norm", 8, xnT)],
                 IN2: [("ln1_2", 0, xnT)], MEM: [("ln_mem_2", 0, qT)], CROSS: [("ln_x_2", 0, xnT)],
                 FF: [("ln2_2", 0, xnT)]}
        xn_before, n = {}, 0
        for k in turning:
            xn_before[k] = n
            n += 4 * len(gains[k])
        h_order = [FFN0, NSA, FFN1, MID, IN2, CROSS, FF, LAST]
        residuals = [FFN0, NSA, FFN1, MID, CROSS, FF, LAST]

        def h_count(k, t):
            return TT * h_order.index(k) + t + 1

        def xn_count(k, which=0):
            return xn_before[k] + 4 * (which + 1)

        def ends(k):
            if k in (NSA, MID, LAST):
                return [(t, c) for t in range(TT) for c in range(2)]
            return [(t, c) for c in range(2) for t in range(TT)]

        def tok(t):
            return slice(P * t, P * t + P)

        block = ctx.enter_context(nc.Block())

        @block.sync
        def _(sp):
            for c, parts in enumerate(chunks):
                if c >= SLOTS:
                    sp.wait_ge(*freed[c - SLOTS])
                for place, src in parts:
                    sp.dma_start(place(ring[c % SLOTS]), src).then_inc(slot_loaded[c % SLOTS], 16)
            for t in range(TT):
                sp.wait_ge(out_ready, t + 1)
                sp.dma_start(out[0].rearrange("(t p) n -> p t n", p=P)[:, t, :],
                             scaled[:, t, :]).then_inc(out_stored, 16)
            sp.wait_ge(out_stored, 32)

        @block.gpsimd
        def _(pool):
            nc.gpsimd.memset(ident[:, :], 0.0).then_inc(pool_step, 1)
            nc.gpsimd.memset(nhalf[:, :], -0.5).then_inc(pool_step, 1)
            nc.gpsimd.memset(mean_w[:, :], 1.0 / D).then_inc(pool_step, 1)
            nc.gpsimd.memset(causal[:, :], 0.0).then_inc(pool_step, 1)
            nc.gpsimd.memset(causalT[:, :], 0.0).then_inc(pool_step, 1)
            nc.gpsimd.memset(valid[:, :], 1.0).then_inc(pool_step, 1)
            nc.gpsimd.memset(ones[:, :], 1.0).then_inc(pool_step, 1)
            nc.gpsimd.iota(dist8[:, 0:P], pattern=[[8, P]], base=0, channel_multiplier=-8,
                           allow_small_or_imprecise_dtypes=True).then_inc(pool_step, 1)
            nc.gpsimd.iota(dist8[:, P:3 * P], pattern=[[8, 2 * P]], base=-8 * P, channel_multiplier=-8,
                           allow_small_or_imprecise_dtypes=True).then_inc(pool_step, 1)
            nc.gpsimd.iota(dist8c[:, :, :], pattern=[[-8 * P, 2], [128, 16]], base=8 * 31,
                           channel_multiplier=-8, allow_small_or_imprecise_dtypes=True).then_inc(pool_step, 1)
            pool.wait_ge(pool_step, 10)
            nc.gpsimd.affine_select(out=ident[:, :], in_=ident[:, :], compare_op=ALU.not_equal, fill=1.0,
                                    base=0, pattern=[[-1, P]], channel_multiplier=1).then_inc(consts_built, 1)

            def mask(m, pattern, base, step):
                nc.gpsimd.affine_select(out=m, in_=m, compare_op=ALU.is_ge, fill=NEG, base=base,
                                        pattern=pattern, channel_multiplier=step).then_inc(consts_built, 1)

            for m in (dist8, causal):
                mask(m[:, 0:P], [[-1, P]], 0, 1)
                mask(m[:, P:3 * P], [[-1, 2 * P]], P, 1)
            mask(dist8c[:, :, :], [[P, 2], [-16, 16]], -31, 1)
            mask(causalT[:, 0:2 * P], [[1, 2 * P]], 0, -1)
            mask(causalT[:, 2 * P:3 * P], [[1, P]], 0, -1)
            nc.gpsimd.affine_select(out=valid[:, :], in_=valid[:, :], compare_op=ALU.is_ge, fill=0.0,
                                    base=-31, pattern=[[0, 1]], channel_multiplier=1).then_inc(consts_built, 1)

            def root(k):
                for t in range(TT):
                    c = TT * k + t
                    pool.wait_ge(ss_ready, c + 1)
                    nc.gpsimd.tensor_scalar(msq[:, c:c + 1], ssq[:, c:c + 1], 1.0 / D, EPS,
                                            ALU.mult, ALU.add).then_inc(ms_ready, 1)
                    pool.wait_ge(ms_ready, c + 1)
                    nc.gpsimd.tensor_tensor(rstd[:, c:c + 1], msq[:, c:c + 1], nhalf[:, 0:1],
                                            ALU.pow).then_inc(rstd_ready, 1)

            for k in (CONV, FFN0, NSA):
                root(k)
            pool.wait_ge(h_ready, h_count(NSA, 1))
            pool.wait_ge(consts_built, 9)
            for i in range(HEADS):
                slope = 2.0 ** (-8.0 * (i + 1) / HEADS)
                nc.gpsimd.tensor_scalar(biases[:, i, 0:3 * P], dist8[:, :], slope, None, ALU.mult)
                nc.gpsimd.tensor_scalar(biases[:, i, 3 * P:3 * P + 32],
                                        dist8c[:, :, :].rearrange("p a b -> p (a b)"), slope, None,
                                        ALU.mult).then_inc(bias_built, 1)
            for k in (FFN1, MID, IN2, MEM):
                root(k)
            pool.wait_ge(ml_sq, 1)
            nc.gpsimd.tensor_scalar(den[:, 4, :], den[:, 3, :], 1.0 / MLD, EPS, ALU.mult,
                                    ALU.add).then_inc(ml_ms, 1)
            pool.wait_ge(ml_ms, 1)
            nc.gpsimd.tensor_tensor(den[:, 5, :], den[:, 4, :], nhalf[:, :], ALU.pow).then_inc(ml_rstd, 1)
            for k in (CROSS, FF, LAST):
                root(k)

        @block.scalar
        def _(sc):
            xs = a["x"][0].rearrange("(t p) n -> p t n", p=P)
            for t in range(TT):
                sc.dma_start(h[:, t, :], xs[:, t, :]).then_inc(x_loaded[t], 16)
            for name, rows in VECS:
                src = a[name]
                src = (src.rearrange("(k p) -> k p", p=P) if len(src.shape) == 1
                       else src.rearrange("a (k p) -> (a k) p", p=P))
                sc.dma_start(vecs[col[name]:col[name] + rows, :], src).then_inc(vecs_loaded, 16)
            sc.dma_start(taps[0:TAPS, :], a["a_dw_w"][0]).then_inc(vecs_loaded, 16)
            sc.dma_start(taps[TAPS:TAPS + TAPS2, :], a["ml_conv_w_2"][0]).then_inc(vecs_loaded, 16)
            for b, name in enumerate(("cmp_pos_k", "cmp_pos_v")):
                for g in range(2):
                    sc.dma_start(pos[:, P * b + DH * g:P * b + DH * g + DH], a[name]).then_inc(vecs_loaded, 16)
            for b, name in enumerate(("phi_k_w2", "phi_v_w2")):
                for g in range(2):
                    sc.dma_start(phi2[DH * g:DH * g + DH, b, :], a[name]).then_inc(small_loaded, 16)
            sc.dma_start(pw2_row, a["a_pw2_b"]).then_inc(small_loaded, 16)
            sc.wait_ge(pads_zero, 1)
            for b, (name, m) in enumerate((("fx_b_f_2", FXH), ("ml_b_f_2", MLH), ("ml_b_i_2", MLH))):
                sc.dma_start(gate_bias[0:m, b:b + 1], a[name].rearrange("a n -> n a")).then_inc(small_loaded, 16)
            sc.dma_start(gain_mid[:, :], a["final_norm"].rearrange("(a n) -> a n", a=1)
                         .broadcast_to([P, D])).then_inc(gains_loaded, 16)
            sc.dma_start(gain_ml[:, :], a["ml_norm_2"].broadcast_to([P, MLH * MLD])).then_inc(gains_loaded, 16)

            def squares(k, src, ready, junk=ptf):
                for t in range(TT):
                    ready(t)
                    nc.scalar.activation(junk[:, D * t:D * t + D], src[:, t, :], ACT.Square,
                                         accum_out=ssq[:, TT * k + t:TT * k + t + 1]).then_inc(ss_ready, 1)

            def h_squares(k):
                squares(k, h, lambda t: sc.wait_ge(h_ready, h_count(k, t)))

            squares(CONV, h, lambda t: sc.wait_ge(x_loaded[t], 16),
                    xnT2[:, :, :].rearrange("p a b -> p (a b)"))

            sc.wait_ge(pre_copied, 1)
            for c in range(4):
                sc.wait_ge(up_done, c + 1)
                if c >= 2:
                    sc.wait_ge(glu_done, 2 * (c - 1))
                for j in range(2):
                    ft = 2 * c + j
                    nc.scalar.activation(softf[:, 512 * (c % 2) + S * j:512 * (c % 2) + S * j + S],
                                         bank[2 * (c % 2) + 1][:, S * j:S * j + S], ACT.Sigmoid,
                                         bias=vecT[:, col["a_pw1_b"] + 8 + ft:col["a_pw1_b"] + 9 + ft]
                                         ).then_inc(gate_act, 1)
            for ft in range(KT):
                sc.wait_ge(diag_used, 4 * (ft + 1))
                nc.scalar.activation(v[:, ft, :], bank[4 + ft % 4][:, 0:S], ACT.Identity,
                                     bias=vecT[:, col["a_dw_b"] + ft:col["a_dw_b"] + ft + 1]).then_inc(conv_out, 1)
            for j in range(2):
                sc.wait_ge(centred, j + 1)
                nc.scalar.activation(actf[:, D * j:D * j + D], vf[:, D * j:D * j + D],
                                     ACT.Square).then_inc(squared, 1)
            sc.wait_ge(rstd_row, 1)
            nc.scalar.activation(softf[:, 0:S], softf[:, 0:S], ACT.Sqrt).then_inc(std_ready, 1)
            for ft in range(KT):
                sc.wait_ge(normed, ft // 4 + 1)
                nc.scalar.activation(v[:, ft, :], v[:, ft, :], ACT.Silu,
                                     bias=vecT[:, col["a_ln_b"] + ft:col["a_ln_b"] + ft + 1],
                                     scale=vecT[:, col["a_ln_g"] + ft:col["a_ln_g"] + ft + 1]
                                     ).then_inc(silu_ready, 1)

            def ffn_silu(which):
                up0, glu0 = 4 + FC * which, 8 + FC * which
                for c in range(FC):
                    sc.wait_ge(up_done, up0 + c + 1)
                    if c >= 2:
                        sc.wait_ge(glu_done, glu0 + c - 1)
                    nc.scalar.activation(softf[:, 512 * (c % 2):512 * (c % 2) + 512], bank[2 * (c % 2)][:, :],
                                         ACT.Silu).then_inc(gate_act, 1)

            h_squares(FFN0)
            sc.dma_start(gain_last[:, :], a["ln_f_2"].rearrange("(a n) -> a n", a=1)
                         .broadcast_to([P, D])).then_inc(last_gain_loaded, 16)
            ffn_silu(0)
            h_squares(NSA)

            sc.wait_ge(kv_done, 2)
            for half in range(2):
                nc.scalar.activation(k2[DH * half:DH * half + DH, 1, :, :].rearrange("p b k -> p (b k)"),
                                     bank[5][DH:P, :], ACT.Copy).then_inc(kv_act, 1)
            sc.wait_ge(phi_done, 1)
            nc.scalar.activation(hid[:, :, :], bank[7][:, 0:32].rearrange("p (b n) -> p b n", b=2)[:, :, 0:NCMP],
                                 ACT.Silu).then_inc(kv_act, 1)
            for b in range(4):
                sc.wait_ge(q_done, b + 1)
                nc.scalar.activation(qTf[:, 512 * b:512 * b + 512], bank[b][:, :], ACT.Copy).then_inc(q_ready, 1)
            sc.wait_ge(q_done, 5)
            nc.scalar.activation(gates[:, :, :].rearrange("p t c -> p (t c)"), bank[4][:, 0:96],
                                 ACT.Sigmoid).then_inc(q_ready, 1)
            sc.wait_ge(phi_done, 2)
            for g in range(GROUPS):
                nc.scalar.activation(kcmp[:, g, :], bank[7 - g][:, 64:64 + NCMP], ACT.Copy)
                nc.scalar.activation(vcmp[:, DH * g:DH * g + DH], bank[7 - g][0:NCMP, P:P + DH],
                                     ACT.Copy).then_inc(kv_act, 1)

            def nsa_exp(i):
                s = soft[:, i % 2, :]
                sc.wait_ge(shifted, i + 1)
                for n, piece in enumerate(NSA_PIECES):
                    x = nc.scalar.activation(s[:, piece], s[:, piece], ACT.Exp, scale=-1.0,
                                             bias=nmax[:, i % 2, n:n + 1], accum_out=rsum[:, i % 2, n:n + 1])
                x.then_inc(exp_done, 1)

            def nsa_evac(i):
                sc.wait_ge(p_turned, i + 1)
                if i >= 2:
                    sc.wait_ge(pv_done, i - 1)
                nc.scalar.activation(pt[:, i % 2, 384:768], bank[5][:, 0:384], ACT.Copy)
                nc.scalar.activation(pt[0:NCMP, i % 2, 768 + P:1024], bank[5][0:NCMP, 384:512],
                                     ACT.Copy).then_inc(pt_act, 1)

            nsa_exp(0)
            for i in range(HEADS):
                if i + 1 < HEADS:
                    nsa_exp(i + 1)
                nsa_evac(i)

            sc.wait_ge(score_done, HEADS)
            mem_src = a["mem_2"][0].rearrange("(t p) n -> p t n", p=P)
            sc.dma_start(qTf.rearrange("p (t n) -> p t n", t=TT), mem_src).then_inc(mem_loaded, 16)
            h_squares(FFN1)
            ffn_silu(1)
            h_squares(MID)
            h_squares(IN2)
            squares(MEM, qTf.rearrange("p (t n) -> p t n", t=TT), lambda t: sc.wait_ge(mem_loaded, 16), actf)

            for b in range(4):
                sc.wait_ge(in2_done, b + 1)
                nc.scalar.activation(u[:, 2 * b:2 * b + 2, PAD:PAD + S],
                                     bank[b][:, :].rearrange("p (f t) -> p f t", f=2),
                                     ACT.Copy).then_inc(in2_act, 1)
            sc.wait_ge(in2_done, 6)
            for t in range(TT):
                nc.scalar.activation(mlo[:, t, :], bank[6 + t][:, :], ACT.Sigmoid).then_inc(in2_act, 1)
            for b in range(4):
                sc.wait_ge(in2_done, 7 + b)
                nc.scalar.activation(xnT2[:, 2 * b:2 * b + 2, :].rearrange("p f t -> p (f t)"),
                                     bank[b][:, :], ACT.Copy).then_inc(in2_act, 1)
            for ft in range(KT):
                sc.wait_ge(conv4_done, ft + 1)
                nc.scalar.activation(v[:, ft, :], v[:, ft, :], ACT.Silu).then_inc(qk_ready, 1)
            sc.wait_ge(rows_done, 1)
            nc.scalar.activation(row[:, 2:4, :], row[:, 2:4, :], ACT.Exp).then_inc(act_link, 1)
            sc.wait_ge(rows_done, 2)
            nc.scalar.activation(row[:, 6:8, :], row[:, 4:6, :], ACT.Ln).then_inc(act_link, 1)
            for b in range(8):
                sc.wait_ge(xkv_done, b + 1)
                dst = memk[:, 2 * b:2 * b + 2, :].rearrange("p f t -> p (f t)") if b < 4 else \
                    memv[:, b % 2, 512 * (b // 2 - 2):512 * (b // 2 - 2) + 512]
                nc.scalar.activation(dst, bank[XKV_BANK[b]][:, :], ACT.Copy).then_inc(xkv_act, 1)
            sc.wait_ge(rows_done, 4)
            nc.scalar.activation(expm[:, :, :], bank[7][:, 16:32].rearrange("p (t n) -> p t n", t=TT),
                                 ACT.Exp).then_inc(act_link, 1)

            for i in range(MLH):
                sc.wait_ge(ml_shift, i + 1)
                w = soft[:, i % 2, :]
                nc.scalar.activation(w[:, 0:S], w[:, 0:S], ACT.Exp, bias=rcol[:, 0, i:i + 1])
                nc.scalar.activation(w[:, S:3 * P], w[:, S:3 * P], ACT.Exp,
                                     bias=rcol[:, 1, i:i + 1]).then_inc(ml_exp, 1)
            sc.wait_ge(ml_copied, MLH + 1)
            nc.scalar.activation(mlsq, num[:, :, 0:MLD], ACT.Square).then_inc(act_link, 1)

            def fx_exp(i):
                n, s = HEADS + i, soft[:, i % 2, :]
                sc.wait_ge(shifted, n + 1)
                nc.scalar.activation(s[:, 0:P], s[:, 0:P], ACT.Exp, scale=-1.0, bias=nmax[:, i % 2, 0:1],
                                     accum_out=rsum[:, i % 2, 0:1])
                nc.scalar.activation(s[:, P:3 * P], s[:, P:3 * P], ACT.Exp, scale=-1.0,
                                     bias=nmax[:, i % 2, 1:2],
                                     accum_out=rsum[:, i % 2, 1:2]).then_inc(exp_done, 1)

            def fx_evac(i):
                n = HEADS + i
                sc.wait_ge(p_turned, n + 1)
                if i < 2:
                    sc.wait_ge(ml_num, MLH)
                else:
                    sc.wait_ge(pv_done, n - 1)
                nc.scalar.activation(pt[:, i % 2, 0:3 * P], bank[6 + i % 2][:, 0:3 * P],
                                     ACT.Copy).then_inc(pt_act, 1)

            fx_exp(0)
            for i in range(FXH):
                if i + 1 < FXH:
                    fx_exp(i + 1)
                fx_evac(i)

            h_squares(CROSS)
            for b in range(4):
                sc.wait_ge(q_done, 6 + b)
                nc.scalar.activation(xnT2[:, 2 * b:2 * b + 2, :].rearrange("p f t -> p (f t)"),
                                     bank[b][:, :], ACT.Copy).then_inc(q_ready, 1)

            def x_exp(i):
                n = HEADS + FXH + i
                sc.wait_ge(shifted, n + 1)
                for t in range(TT):
                    x = nc.scalar.activation(soft[:, i % 2, S * t:S * t + S], bank[4 + i % 2][:, S * t:S * t + S],
                                             ACT.Exp, scale=XSCALE, bias=nmax[:, i % 2, 2 + t:3 + t],
                                             accum_out=rsum[:, i % 2, t:t + 1])
                x.then_inc(exp_done, 1)

            def x_evac(i):
                n = HEADS + FXH + i
                sc.wait_ge(p_turned, n + 1)
                if i >= 2:
                    sc.wait_ge(pv_done, n - 1)
                nc.scalar.activation(pt[:, i % 2, 0:512], bank[6 + i % 2][:, :], ACT.Copy).then_inc(pt_act, 1)

            x_exp(0)
            for i in range(XH):
                if i + 1 < XH:
                    x_exp(i + 1)
                x_evac(i)

            h_squares(FF)
            for c in range(8):
                sc.wait_ge(up_done, 4 + 2 * FC + c + 1)
                for b in range(2):
                    n = 8 + 2 * FC + 2 * c + b
                    if c >= 2:
                        sc.wait_ge(glu_done, n - 3)
                    nc.scalar.activation(ptf[:, 1024 * (c % 2) + 512 * b:1024 * (c % 2) + 512 * b + 512],
                                         bank[2 * (c % 2) + b][:, :], ACT.Relu).then_inc(gate_act, 1)
            h_squares(LAST)

        @block.vector
        def _(ve):
            links = [0]

            def link(x):
                links[0] += 1
                x.then_inc(dve_link, 1)
                ve.wait_ge(dve_link, links[0])

            def scale(k, src):
                for t in range(TT):
                    ve.wait_ge(rstd_ready, TT * k + t + 1)
                    nc.vector.tensor_scalar(scaled[:, t, :], src[:, t, :], rstd[:, TT * k + t:TT * k + t + 1],
                                            None, ALU.mult).then_inc(scaled_ready, 1)

            def take(k, waits=True):
                idx = turning.index(k)
                for name, off, dst in gains[k]:
                    g0 = col[name] + off
                    for t in range(TT):
                        for half in range(2):
                            ve.wait_ge(turned, 4 * idx + 2 * t + half + 1)
                            nc.vector.tensor_tensor(
                                dst[:, 4 * half:4 * half + 4, tok(t)],
                                bank[2 * t + half][:, :].rearrange("p (k c) -> p k c", k=4),
                                vecT[:, g0 + 4 * half:g0 + 4 * half + 4].unsqueeze(2).broadcast_to([P, 4, P]),
                                ALU.mult).then_inc(xn_ready, 1)

            def add(k):
                for n, (t, c) in enumerate(ends(k)):
                    ve.wait_ge(acc_done, 4 * residuals.index(k) + n + 1)
                    part = h[:, t, 512 * c:512 * c + 512]
                    x = nc.vector.tensor_tensor(part, part, bank[4 + 2 * t + c][:, :], ALU.add)
                    if c == 1:
                        x.then_inc(h_ready, 1)

            nc.vector.memset(gate_bias[:, :], 0.0).then_inc(pads_zero, 1)
            nc.vector.memset(u[:, :, 0:PAD], 0.0).then_inc(pads_zero, 1)
            scale(CONV, h)
            ve.wait_ge(pre_turned, 1)
            nc.vector.tensor_copy(vecT[:, :], bank[4][:, 0:P]).then_inc(pre_copied, 1)
            ve.wait_ge(pre_turned, 2)
            nc.vector.tensor_copy(tapT[:, :, :].rearrange("p k c -> p (k c)"),
                                  bank[5][:, 0:KT * (TAPS + TAPS2)]).then_inc(pre_copied, 1)
            ve.wait_ge(pre_turned, 3)
            nc.vector.tensor_copy(posT[:, :, :].rearrange("p b l -> p (b l)"), bank[6][:, 0:64]).then_inc(pre_copied, 1)
            ve.wait_ge(pre_copied, 3)
            ve.wait_ge(consts_built, 1)
            take(CONV)

            def diagonals(g):
                ft, m = g // 4, min(TAPG, TAPS - TAPG * (g % 4))
                if g >= NDIAG:
                    ve.wait_ge(diag_used, g - NDIAG + 1)
                j = TAPG * (g % 4)
                nc.vector.tensor_tensor(diag[:, g % NDIAG, 0:m, :],
                                        ident[:, :].unsqueeze(1).broadcast_to([P, m, P]),
                                        tapT[:, ft, j:j + m].unsqueeze(2).broadcast_to([P, m, P]),
                                        ALU.mult).then_inc(diag_built, 1)

            for g in range(NDIAG):
                diagonals(g)
            for ft in range(KT):
                ve.wait_ge(gate_act, ft + 1)
                c, j = ft // 2, ft % 2
                b = col["a_pw1_b"] + ft
                nc.vector.scalar_tensor_tensor(
                    out=u[:, ft, PAD:PAD + S], in0=bank[2 * (c % 2)][:, S * j:S * j + S], scalar=vecT[:, b:b + 1],
                    in1=softf[:, 512 * (c % 2) + S * j:512 * (c % 2) + S * j + S],
                    op0=ALU.add, op1=ALU.mult).then_inc(glu_done, 1)
            for g in range(NDIAG, 4 * KT):
                diagonals(g)

            ve.wait_ge(stat_done, 1)
            for j in range(2):
                part = v[:, 4 * j:4 * j + 4, :]
                nc.vector.tensor_tensor(part, part, bank[0][:, 0:S].unsqueeze(1).broadcast_to([P, 4, S]),
                                        ALU.subtract).then_inc(centred, 1)
            ve.wait_ge(stat_done, 2)
            nc.vector.tensor_scalar(softf[:, 0:S], bank[1][:, 0:S], EPS, None, ALU.add).then_inc(rstd_row, 1)
            ve.wait_ge(std_ready, 1)
            link(nc.vector.reciprocal(softf[:, S:2 * S], softf[:, 0:S]))
            for j in range(2):
                part = v[:, 4 * j:4 * j + 4, :]
                nc.vector.tensor_tensor(part, part, softf[:, S:2 * S].unsqueeze(1).broadcast_to([P, 4, S]),
                                        ALU.mult).then_inc(normed, 1)

            def norm(k):
                add(k)
                scale(k, h)
                take(k)

            def glu(which):
                for c in range(FC):
                    ve.wait_ge(gate_act, 8 + FC * which + c + 1)
                    nc.vector.tensor_tensor(actf[:, 512 * c:512 * c + 512], bank[2 * (c % 2) + 1][:, :],
                                            softf[:, 512 * (c % 2):512 * (c % 2) + 512],
                                            ALU.mult).then_inc(glu_done, 1)

            norm(FFN0)
            glu(0)
            norm(NSA)

            ve.wait_ge(kv_done, 1)
            for b in range(2):
                raw = bank[4][:, S * b:S * b + S].rearrange("p (n l) -> p l n", l=16)
                for part in range(2):
                    ls = slice(16 * part, 16 * part + 16)
                    nc.vector.tensor_tensor(window[:, b, ls, :], raw[:, :, part:part + NCMP],
                                            posT[:, b, ls].unsqueeze(2).broadcast_to([P, 16, NCMP]),
                                            ALU.add).then_inc(window_ready, 1)
            ve.wait_ge(kv_done, 2)
            for half in range(2):
                nc.vector.tensor_copy(k2[DH * half:DH * half + DH, 0, :, :].rearrange("p b k -> p (b k)"),
                                      bank[5][0:DH, :]).then_inc(kv_dve, 1)
            nc.vector.tensor_copy(vtok[:, :, :, :].rearrange("p t b c -> p (t b c)"),
                                  bank[6][:, :]).then_inc(kv_dve, 1)
            ve.wait_ge(q_ready, 5)
            ve.wait_ge(consts_built, 9)
            link(nc.vector.tensor_scalar(gates[:, 0, 0:HEADS], gates[:, 0, 0:HEADS], valid[:, 0:1], None, ALU.mult))
            gate_of = gates[:, :, :].rearrange("p t (b h) -> p t b h", b=3)

            def nsa_shift(i):
                ve.wait_ge(score_done, i + 1)
                ve.wait_ge(bias_built, i + 1)
                if i >= 2:
                    ve.wait_ge(p_turned, i - 1)
                for n, piece in enumerate(NSA_PIECES):
                    t, branch = n // 3, n % 3
                    if branch == 0:
                        src, bias = bank[i % 2][:, piece], biases[:, i, 3 * P + 16 * t:3 * P + 16 * t + NCMP]
                    elif t == 0:
                        src, bias = bank[i % 2][:, piece], biases[:, i, 0:P]
                    else:
                        src, bias = bank[2 + i % 2][:, S * (branch - 1):S * branch], biases[:, i, P:3 * P]
                    x = nc.vector.tensor_tensor_reduce(out=soft[:, i % 2, piece], in0=src, in1=bias,
                                                       scale=-DH ** -0.5, scalar=3e38, op0=ALU.add, op1=ALU.min,
                                                       accum_out=nmax[:, i % 2, n:n + 1])
                x.then_inc(shifted, 1)

            def nsa_weigh(i):
                ve.wait_ge(exp_done, i + 1)
                b = i % 2
                link(nc.vector.reciprocal(rcol[:, 0, 0:6], rsum[:, b, :]))
                link(nc.vector.tensor_tensor(coef[:, b, :].rearrange("p (t n) -> p t n", t=TT),
                                             rcol[:, 0, 0:6].rearrange("p (t n) -> p t n", t=TT),
                                             gate_of[:, :, :, i], ALU.mult))
                for n, piece in enumerate(NSA_PIECES):
                    x = nc.vector.tensor_scalar(soft[:, b, piece], soft[:, b, piece], coef[:, b, n:n + 1],
                                                None, ALU.mult)
                x.then_inc(weighed, 1)

            def nsa_evac(i):
                ve.wait_ge(p_turned, i + 1)
                if i >= 2:
                    ve.wait_ge(pv_done, i - 1)
                nc.vector.tensor_copy(pt[:, i % 2, 0:384], bank[4][:, 0:384])
                nc.vector.tensor_copy(pt[0:NCMP, i % 2, 768:768 + P], bank[4][0:NCMP, 384:512]).then_inc(pt_dve, 1)

            def nsa_out(ft):
                ve.wait_ge(pv_done, 2 * ft + 2)
                nc.vector.tensor_copy(xnT[:, ft, :], bank[6 + ft % 2][:, 0:S]).then_inc(o_ready, 1)

            nsa_shift(0)
            for i in range(HEADS):
                if i + 1 < HEADS:
                    nsa_shift(i + 1)
                nsa_weigh(i)
                nsa_evac(i)
                if i % 2 == 0 and i:
                    nsa_out(i // 2 - 1)
            nsa_out(HEADS // 2 - 1)

            norm(FFN1)
            glu(1)
            add(MID)
            ve.wait_ge(gains_loaded, 32)
            for t in range(TT):
                ve.wait_ge(rstd_ready, TT * MID + t + 1)
                nc.vector.scalar_tensor_tensor(out=h[:, t, :], in0=h[:, t, :],
                                               scalar=rstd[:, TT * MID + t:TT * MID + t + 1], in1=gain_mid[:, :],
                                               op0=ALU.mult, op1=ALU.mult).then_inc(h_ready, 1)
            scale(IN2, h)
            take(IN2)
            scale(MEM, qTf.rearrange("p (t n) -> p t n", t=TT))
            ve.wait_ge(in2_done, 5)
            for t in range(TT):
                nc.vector.memset(mlv[:, t, :, MLD:MLV], 1.0)
                nc.vector.tensor_copy(mlv[:, t, :, 0:MLD],
                                      bank[4 + t][:, :].rearrange("p (h c) -> p h c", h=MLH)).then_inc(in2_dve, 1)

            before = links[0]
            for group in range(2):
                ve.wait_ge(in2_act, 2 * group + 2)
                for j in range(TAPS2):
                    for f in range(4):
                        ft = 4 * group + f
                        src = u[:, ft, PAD - TAPS2 + 1 + j:PAD - TAPS2 + 1 + j + S]
                        tap = tapT[:, ft, TAPS + j:TAPS + j + 1]
                        if j == 0:
                            b = col["ml_conv_b_2"] + ft
                            x = nc.vector.tensor_scalar(v[:, ft, :], src, tap, vecT[:, b:b + 1], ALU.mult, ALU.add)
                        else:
                            ve.wait_ge(dve_link, before + 12 * group + 4 * (j - 1) + f + 1)
                            x = nc.vector.scalar_tensor_tensor(out=v[:, ft, :], in0=src, scalar=tap, in1=v[:, ft, :],
                                                               op0=ALU.mult, op1=ALU.add)
                        x.then_inc(conv4_done if j == TAPS2 - 1 else dve_link, 1)
            links[0] = before + 24
            ve.wait_ge(in2_act, 6)
            for t in range(TT):
                nc.vector.tensor_tensor(mlo[:, t, :], mlo[:, t, :], gain_ml[:, :], ALU.mult)
            ve.wait_ge(in2_done, 11)
            for t in range(TT):
                nc.vector.tensor_copy(fxv[:, t, :], bank[4 + t][:, :]).then_inc(in2_dve, 1)
            take(MEM)

            ve.wait_ge(in2_done, 12)
            ve.wait_ge(small_loaded, 16 * 8)
            for b in range(2):
                x = nc.vector.tensor_scalar(row[:, b, :], bank[6][0:FXH, S * b:S * b + S], gate_bias[:, b:b + 1],
                                            None, ALU.add)
            link(x)
            nc.vector.scalar_tensor_tensor(out=row[:, 2:4, :], in0=row[:, 0:2, :], scalar=-1.0, in1=row[:, 0:2, :],
                                           op0=ALU.mult, op1=ALU.min).then_inc(rows_done, 1)
            ve.wait_ge(act_link, 1)
            nc.vector.tensor_scalar(row[:, 4:6, :], row[:, 2:4, :], 1.0, None, ALU.add).then_inc(rows_done, 1)
            ve.wait_ge(act_link, 2)
            link(nc.vector.scalar_tensor_tensor(out=row[:, 4:6, :], in0=row[:, 4:6, :], scalar=1.0,
                                                in1=row[:, 2:4, :], op0=ALU.subtract, op1=ALU.subtract))
            link(nc.vector.tensor_tensor(row[:, 6:8, :], row[:, 6:8, :], row[:, 4:6, :], ALU.subtract))
            link(nc.vector.scalar_tensor_tensor(out=row[:, 2:4, :], in0=row[:, 0:2, :], scalar=0.0,
                                                in1=row[:, 6:8, :], op0=ALU.min, op1=ALU.subtract))
            one = ones[0:FXH, 0:1].broadcast_to([FXH, S])
            for b in range(2):
                x = nc.vector.tensor_tensor_scan(row[:, 4 + b, :], one, row[:, 2 + b, :], 0.0, ALU.mult, ALU.add)
            link(x)
            nc.vector.tensor_scalar(row[:, 0, :], row[:, 4, :], -float(DH) ** 0.5, None, ALU.mult)
            link(nc.vector.scalar_tensor_tensor(out=row[:, 1, :], in0=bank[7][0:FXH, 0:S], scalar=gate_bias[:, 2:3],
                                                in1=row[:, 5, :], op0=ALU.add, op1=ALU.subtract))
            link(nc.vector.tensor_tensor_scan(row[:, 6, :], one, row[:, 1, :], 0.0, ALU.mult, ALU.max))
            nc.vector.tensor_scalar(row[:, 7, :], row[:, 6, :], -1.0, None, ALU.mult)
            nc.vector.scalar_tensor_tensor(out=row[:, 2, :], in0=row[:, 5, :], scalar=-1.0, in1=row[:, 6, :],
                                           op0=ALU.mult, op1=ALU.subtract).then_inc(rows_done, 1)
            ve.wait_ge(cols_turned, 1)
            nc.vector.tensor_copy(rcol[:, :, :], bank[7][:, 0:16].rearrange("p (t n) -> p t n", t=TT)
                                  ).then_inc(rows_done, 1)

            def ml_shifted(i):
                ve.wait_ge(ml_score, i + 1)
                ve.wait_ge(consts_built, 9)
                w, m = soft[:, i % 2, :], bank[1 + 2 * (i % 2)]
                nc.vector.tensor_tensor(w[:, 0:S], m[:, 0:S], causalT[:, 0:S], ALU.add)
                nc.vector.tensor_tensor(w[:, S:3 * P], m[:, P:S], causalT[:, S:3 * P], ALU.add).then_inc(ml_shift, 1)

            def ml_weighed(i):
                ve.wait_ge(ml_exp, i + 1)
                if i >= 2:
                    ve.wait_ge(ml_num, i - 1)
                nc.vector.scalar_tensor_tensor(out=pt[:, i % 2, 0:3 * P], in0=bank[2 * (i % 2)][:, 0:3 * P],
                                               scalar=MLD ** -0.5, in1=soft[:, i % 2, 0:3 * P],
                                               op0=ALU.mult, op1=ALU.mult).then_inc(ml_weight, 1)

            numv = num.rearrange("p (t h) c -> p t h c", t=TT)

            def ml_take(i):
                ve.wait_ge(ml_num, i + 1)
                nc.vector.tensor_copy(numv[:, :, i, :], bank[4 + i % 2][:, 0:TT * MLV]
                                      .rearrange("p (t c) -> p t c", t=TT)).then_inc(ml_copied, 1)

            ve.wait_ge(xkv_done, 8)
            ml_shifted(0)
            for i in range(MLH):
                if i + 1 < MLH:
                    ml_shifted(i + 1)
                ml_weighed(i)
                if i:
                    ml_take(i - 1)
            ml_take(MLH - 1)
            ve.wait_ge(act_link, 3)
            ve.wait_ge(ml_copied, MLH)
            d = num[:, :, MLD]
            link(nc.vector.scalar_tensor_tensor(out=den[:, 0, :], in0=d, scalar=-1.0, in1=d, op0=ALU.mult, op1=ALU.max))
            link(nc.vector.tensor_tensor(den[:, 1, :].rearrange("p (t h) -> p t h", t=TT),
                                         den[:, 0, :].rearrange("p (t h) -> p t h", t=TT),
                                         expm[:, :, 0:MLH], ALU.max))
            link(nc.vector.reciprocal(den[:, 2, :], den[:, 1, :]))
            nc.vector.tensor_tensor(num[:, :, 0:MLD], num[:, :, 0:MLD],
                                    den[:, 2, :].unsqueeze(2).broadcast_to([P, 8, MLD]), ALU.mult
                                    ).then_inc(ml_copied, 1)

            def fx_shift(i):
                n = HEADS + i
                ve.wait_ge(score_done, n + 1)
                if i >= 2:
                    ve.wait_ge(p_turned, n - 1)
                s, b = soft[:, i % 2, :], bank[2 * (i % 2)]
                nc.vector.tensor_tensor_reduce(out=s[:, 0:P], in0=b[:, 0:P], in1=causal[:, 0:P],
                                               scale=-DH ** -0.5, scalar=3e38, op0=ALU.add, op1=ALU.min,
                                               accum_out=nmax[:, i % 2, 0:1])
                nc.vector.tensor_tensor_reduce(out=s[:, P:3 * P], in0=b[:, P:3 * P], in1=causal[:, P:3 * P],
                                               scale=-DH ** -0.5, scalar=3e38, op0=ALU.add, op1=ALU.min,
                                               accum_out=nmax[:, i % 2, 1:2]).then_inc(shifted, 1)

            def row_weigh(n, i, pieces):
                ve.wait_ge(exp_done, n + 1)
                link(nc.vector.reciprocal(coef[:, i % 2, 0:2], rsum[:, i % 2, 0:2]))
                for t, piece in enumerate(pieces):
                    x = nc.vector.tensor_scalar(soft[:, i % 2, piece], soft[:, i % 2, piece],
                                                coef[:, i % 2, t:t + 1], None, ALU.mult)
                x.then_inc(weighed, 1)

            def fx_out(j):
                ve.wait_ge(pv_done, HEADS + 2 * j + 2)
                nc.vector.tensor_copy(xnT[:, 4 + j, :], bank[1 + 2 * (j % 2)][:, 0:S]).then_inc(o_ready, 1)

            fx_shift(0)
            for i in range(FXH):
                if i + 1 < FXH:
                    fx_shift(i + 1)
                row_weigh(HEADS + i, i, (slice(0, P), slice(P, 3 * P)))
                if i % 2 == 0 and i:
                    fx_out(i // 2 - 1)
                if i == 1:
                    ve.wait_ge(act_link, 4)
                    nc.vector.tensor_reduce(den[:, 3, :], mlsq, AX.X, ALU.add).then_inc(ml_sq, 1)
                if i == 4:
                    ve.wait_ge(ml_rstd, 1)
                    link(nc.vector.tensor_tensor(num[:, :, 0:MLD], num[:, :, 0:MLD],
                                                 den[:, 5, :].unsqueeze(2).broadcast_to([P, 8, MLD]), ALU.mult))
                    for t in range(TT):
                        nc.vector.tensor_tensor(numv[:, t, :, 0:MLD], numv[:, t, :, 0:MLD],
                                                mlo[:, t, :].rearrange("p (h c) -> p h c", h=MLH),
                                                ALU.mult).then_inc(ml_out, 1)
            fx_out(FXH // 2 - 1)
            for t in range(TT):
                ve.wait_ge(ml_turned, t + 1)
                nc.vector.tensor_copy(xnT[:, 0:MLH, tok(t)],
                                      bank[4 + t][:, :].rearrange("p (h c) -> p h c", h=MLH)).then_inc(ml_ready, 1)

            norm(CROSS)

            def x_shift(i):
                ve.wait_ge(score_done, HEADS + FXH + i + 1)
                link(nc.vector.tensor_reduce(nmax[:, i % 2, 0:2], bank[4 + i % 2][:, :]
                                             .rearrange("p (t m) -> p t m", t=TT), AX.X, ALU.max, negate=True))
                nc.vector.tensor_scalar(nmax[:, i % 2, 2:4], nmax[:, i % 2, 0:2], XSCALE, None,
                                        ALU.mult).then_inc(shifted, 1)

            def x_out(i):
                ve.wait_ge(pv_done, HEADS + FXH + i + 1)
                nc.vector.tensor_copy(xnT[:, 2 * i:2 * i + 2, :].rearrange("p f t -> p (f t)"),
                                      bank[i][:, :]).then_inc(o_ready, 1)

            x_shift(0)
            for i in range(XH):
                if i + 1 < XH:
                    x_shift(i + 1)
                row_weigh(HEADS + FXH + i, i, (slice(0, S), slice(S, 2 * S)))
                if i:
                    x_out(i - 1)
            x_out(XH - 1)

            norm(FF)
            for n in range(16):
                c, b = n // 2, n % 2
                ve.wait_ge(gate_act, 8 + 2 * FC + n + 1)
                nc.vector.scalar_tensor_tensor(
                    out=actf[:, 512 * n:512 * n + 512], in0=bank[2 * (c % 2) + b][:, :], scalar=0.0,
                    in1=ptf[:, 1024 * (c % 2) + 512 * b:1024 * (c % 2) + 512 * b + 512],
                    op0=ALU.max, op1=ALU.mult).then_inc(glu_done, 1)
            add(LAST)
            ve.wait_ge(last_gain_loaded, 16)
            for t in range(TT):
                ve.wait_ge(rstd_ready, TT * LAST + t + 1)
                nc.vector.scalar_tensor_tensor(out=scaled[:, t, :], in0=h[:, t, :],
                                               scalar=rstd[:, TT * LAST + t:TT * LAST + t + 1], in1=gain_last[:, :],
                                               op0=ALU.mult, op1=ALU.mult).then_inc(out_ready, 1)

        @block.tensor
        def _(te):
            mm = nc.tensor.matmul

            def arrived(c):
                te.wait_ge(slot_loaded[c % SLOTS], loads_through(c))

            def slot(c, width):
                return ring[c % SLOTS][:, 0:SLOT // width * width].rearrange("p (k n) -> p k n", n=width)

            def used(x):
                x.then_inc(slots_used, 1)

            def turn(k):
                idx = turning.index(k)
                for t in range(TT):
                    te.wait_ge(scaled_ready, TT * idx + t + 1)
                    for half in range(2):
                        for q in range(4):
                            x = nc.tensor.transpose(bank[2 * t + half][:, P * q:P * q + P],
                                                    scaled[:, t, P * (4 * half + q):P * (4 * half + q) + P],
                                                    ident[:, :])
                        x.then_inc(turned, 1)

            def features(dst, w, c0, src, width=P):
                for kt in range(KT):
                    x = mm(dst, w[:, kt, c0:c0 + width], src[:, kt, :], start=kt == 0, stop=kt == KT - 1)
                return x

            def tokens(dst, w, cols, src, t):
                for kt in range(KT):
                    x = mm(dst, src[:, kt, tok(t)], w[:, kt, cols], start=kt == 0, stop=kt == KT - 1)
                return x

            def residual_wide(stage, src, bias=False):
                for c in range(2):
                    n = first[stage] + c
                    arrived(n)
                    w = slot(n, 512)
                    for t in range(TT):
                        dst = bank[4 + 2 * t + c]
                        if bias:
                            mm(dst[:, :], ones[0:1, :], pw2_row[0:1, 512 * c:512 * c + 512], start=True, stop=False)
                        for kt in range(KT):
                            x = mm(dst[:, :], src[:, kt, tok(t)], w[:, kt, :],
                                   start=kt == 0 and not bias, stop=kt == KT - 1)
                        x.then_inc(acc_done, 1)

            def residual_tall(stage, tiles, glu_before):
                for c in range(-(-tiles // 4)):
                    n = first[stage] + c
                    arrived(n)
                    w = slot(n, D)
                    m = min(4, tiles - 4 * c)
                    te.wait_ge(glu_done, glu_before(4 * c + m - 1))
                    for t in range(TT):
                        for half in range(2):
                            for q in range(m):
                                kt = 4 * c + q
                                x = mm(bank[4 + 2 * t + half][:, :], act[:, kt, tok(t)],
                                       w[:, q, 512 * half:512 * half + 512], start=kt == 0, stop=kt == tiles - 1)
                            if 4 * c + m == tiles:
                                x.then_inc(acc_done, 1)
                    if 4 * c + m < tiles:
                        used(x)

            def gated(stage, up0, used_by, count):
                for c in range(count):
                    n = first[stage] + c
                    arrived(n)
                    if c >= 2:
                        te.wait_ge(glu_done, used_by(c - 2))
                    w = slot(n, 512)
                    for b in range(2):
                        for j in range(2):
                            x = features(bank[2 * (c % 2) + b][:, S * j:S * j + S], w, S * b + P * j, xnT)
                    x.then_inc(up_done, 1)

            te.wait_ge(consts_built, 1)
            turn(CONV)
            te.wait_ge(vecs_loaded, 16 * (len(VECS) + 6))
            nc.tensor.transpose(bank[4][:, 0:P], vecs, ident[:, :]).then_inc(pre_turned, 1)
            m = TAPS + TAPS2
            for k in range(KT):
                x = nc.tensor.transpose(bank[5][:, m * k:m * k + m], taps[:, P * k:P * k + P], ident[0:m, 0:m])
            x.then_inc(pre_turned, 1)
            for b in range(2):
                x = nc.tensor.transpose(bank[6][:, 32 * b:32 * b + 32], pos[:, P * b:P * b + P], ident[0:32, 0:32])
            x.then_inc(pre_turned, 1)
            te.wait_ge(xn_ready, xn_count(CONV))
            gated("pw1", 0, lambda c: 2 * c + 2, 4)

            def mean(ft, dst, src, stage):
                x = mm(dst, mean_w[:, :], src, start=ft == 0, stop=ft == KT - 1)
                if ft == KT - 1:
                    x.then_inc(stat_done, 1)

            for ft in range(KT):
                te.wait_ge(glu_done, ft + 1)
                if ft >= 4:
                    te.wait_ge(conv_out, ft - 3)
                for j in range(TAPS):
                    g = 4 * ft + j // TAPG
                    if j % TAPG == 0:
                        te.wait_ge(diag_built, g + 1)
                    x = mm(bank[4 + ft % 4][:, 0:S], diag[:, g % NDIAG, j % TAPG, :], u[:, ft, j:j + S],
                           start=j == 0, stop=j == TAPS - 1)
                    if j % TAPG == TAPG - 1 or j == TAPS - 1:
                        x.then_inc(diag_used, 1)
                if ft == 1:
                    te.wait_ge(glu_done, 6)
                if ft:
                    te.wait_ge(conv_out, ft)
                    mean(ft - 1, bank[0][:, 0:S], v[:, ft - 1, :], 0)
            te.wait_ge(conv_out, KT)
            mean(KT - 1, bank[0][:, 0:S], v[:, KT - 1, :], 0)
            for ft in range(KT):
                te.wait_ge(squared, ft // 4 + 1)
                mean(ft, bank[1][:, 0:S], act[:, ft, :], 1)
            te.wait_ge(silu_ready, KT)
            te.wait_ge(small_loaded, 16 * 8)
            residual_wide("pw2", v, bias=True)

            def ffn(k, which):
                turn(k)
                te.wait_ge(xn_ready, xn_count(k))
                gated(f"ffn{which}_in", 0, lambda c: 8 + FC * which + c + 1, FC)
                residual_tall(f"ffn{which}_out", FT, lambda kt: 8 + FC * which + kt // 2 + 1)

            ffn(FFN0, 0)

            turn(NSA)
            te.wait_ge(xn_ready, xn_count(NSA, 0))
            n = first["kv_a"]
            arrived(n)
            w = slot(n, 512)
            for j in range(2):
                x = features(bank[4][:, S * j:S * j + S], w, P * j, xnT2)
            x.then_inc(kv_done, 1)
            features(bank[5][:, 0:S], w, 2 * P, xnT2)
            for t in range(TT):
                x = tokens(bank[6][:, S * t:S * t + P], w, slice(3 * P, 4 * P), xnT2, t)
            used(x)
            n = first["kv_b"]
            arrived(n)
            w = slot(n, 256)
            features(bank[5][:, S:2 * S], w, 0, xnT2)
            for t in range(TT):
                x = tokens(bank[6][:, S * t + P:S * t + 2 * P], w, slice(P, 2 * P), xnT2, t)
            x.then_inc(kv_done, 1)
            n = first["phi"]
            arrived(n)
            te.wait_ge(window_ready, 4)
            w = ring[n % SLOTS][:, :].rearrange("p (b l e) -> p b l e", b=2, e=DH)
            for b in range(2):
                for g in range(GROUPS):
                    half = slice(DH * g, DH * g + DH)
                    for l in range(32):
                        x = mm(bank[7][half, 16 * b:16 * b + NCMP], w[half, b, l, :], window[half, b, l, :],
                               start=l == 0, stop=l == 31)
            x.then_inc(phi_done, 1)
            te.wait_ge(xn_ready, xn_count(NSA, 1))
            for c in range(2):
                n = first["q"] + c
                arrived(n)
                w = slot(n, 512)
                for j in range(4):
                    x = features(bank[2 * c + j // 2][:, S * (j % 2):S * (j % 2) + S], w, P * j, xnT)
                    if j % 2:
                        x.then_inc(q_done, 1)
            n = first["gates"]
            arrived(n)
            w = slot(n, 48)
            for t in range(TT):
                x = tokens(bank[4][:, 48 * t:48 * t + 48], w, slice(0, 48), xnT, t)
            x.then_inc(q_done, 1)
            te.wait_ge(kv_act, 3)
            te.wait_ge(small_loaded, 16 * 8)
            te.wait_ge(kv_dve, 3)
            for g in range(GROUPS):
                half = slice(DH * g, DH * g + DH)
                for e in range(2):
                    mm(bank[7 - g][DH * e:DH * e + DH, 64:64 + NCMP], phi2[half, 0, :],
                       hid[half, 0, :], start=True, stop=True)
                x = mm(bank[7 - g][0:NCMP, P:P + DH], hid[half, 1, :], phi2[half, 1, :], start=True, stop=True)
            x.then_inc(phi_done, 1)

            def nsa_score(i):
                if i >= 2:
                    te.wait_ge(shifted, i - 1)
                e, g = slice(DH * (i % 2), DH * (i % 2) + DH), i // (HEADS // GROUPS)
                x, y = bank[i % 2], bank[2 + i % 2]
                q0, q1 = qT[e, i // 2, 0:P], qT[e, i // 2, P:S]
                mm(x[:, 0:2 * P], q0, k2[e, g, :, 0:P], start=True, stop=True)
                mm(x[:, 256:271], q0, kcmp[e, g, :], start=True, stop=True)
                mm(x[:, 272:287], q1, kcmp[e, g, :], start=True, stop=True)
                mm(y[:, :], q1, k2[e, g, :, :].rearrange("p b k -> p (b k)"), start=True,
                   stop=True).then_inc(score_done, 1)

            def nsa_turn(i):
                te.wait_ge(weighed, i + 1)
                if i:
                    te.wait_ge(pt_dve, i)
                    te.wait_ge(pt_act, i)
                s = soft[:, i % 2, :]
                turns = [(4, 0, 0), (4, P, 288), (4, 2 * P, 416), (5, 0, 128), (5, P, 544), (5, 2 * P, 672)]
                for b, at, src in turns:
                    nc.tensor.transpose(bank[b][:, at:at + P], s[:, src:src + P], ident[:, :])
                for t in range(TT):
                    x = nc.tensor.transpose(bank[4 + t][0:NCMP, 384:512],
                                            s[:, 256 + 16 * t:256 + 16 * t + NCMP], ident[:, :])
                x.then_inc(p_turned, 1)

            def nsa_pv(i):
                te.wait_ge(pt_dve, i + 1)
                te.wait_ge(pt_act, i + 1)
                ft, g = i // 2, i // (HEADS // GROUPS)
                if i % 2 == 0 and ft >= 2:
                    te.wait_ge(o_ready, ft - 1)
                dst = bank[6 + ft % 2][DH * (i % 2):DH * (i % 2) + DH, 0:S]
                d = slice(DH * g, DH * g + DH)
                for b in range(2):
                    mm(dst, vtok[:, 0, b, d], pt[:, i % 2, 384 * b:384 * b + S], start=b == 0, stop=False)
                    mm(dst[:, P:S], vtok[:, 1, b, d], pt[:, i % 2, 384 * b + S:384 * b + 384], start=False, stop=False)
                mm(dst, vcmp[:, d], pt[0:NCMP, i % 2, 768:1024], start=False, stop=True).then_inc(pv_done, 1)

            te.wait_ge(q_ready, 5)
            te.wait_ge(kv_act, 5)
            te.wait_ge(kv_dve, 3)
            nsa_score(0)
            nsa_score(1)
            for i in range(HEADS):
                nsa_turn(i)
                if i + 2 < HEADS:
                    nsa_score(i + 2)
                nsa_pv(i)
            te.wait_ge(o_ready, HEADS // 2)
            residual_wide("b_out", xnT)

            ffn(FFN1, 1)

            turn(IN2)
            te.wait_ge(xn_ready, xn_count(IN2))
            for stage, b0, before in (("ml_qk", 0, 0), ("ml_qk", 2, 0)):
                n = first[stage] + b0 // 2
                arrived(n)
                w = slot(n, 512)
                for j in range(4):
                    x = features(bank[b0 + j // 2][:, S * (j % 2):S * (j % 2) + S], w, P * j, xnT)
                    if j % 2:
                        x.then_inc(in2_done, 1)

            def by_token(stage, b0):
                n = first[stage]
                arrived(n)
                w = slot(n, 512)
                for t in range(TT):
                    x = tokens(bank[b0 + t][:, :], w, slice(0, 512), xnT, t)
                x.then_inc(in2_done, 1)

            by_token("ml_v", 4)
            by_token("ml_o", 6)
            for stage, b0 in (("fx_q", 0), ("fx_k", 2)):
                n = first[stage]
                arrived(n)
                w = slot(n, 512)
                te.wait_ge(in2_act, b0 + 2)
                for j in range(4):
                    x = features(bank[b0 + j // 2][:, S * (j % 2):S * (j % 2) + S], w, P * j, xnT)
                    if j % 2:
                        x.then_inc(in2_done, 1)
            te.wait_ge(in2_dve, 2)
            by_token("fx_v", 4)
            n = first["rows"]
            arrived(n)
            te.wait_ge(in2_act, 6)
            w = slot(n, 16)
            features(bank[6][0:8, 0:S], w, 8, xnT, 8)
            features(bank[6][0:8, S:2 * S], w, 4, xnT, 8)
            x = features(bank[7][0:8, 0:S], w, 0, xnT, 8)
            x.then_inc(in2_done, 1)
            te.wait_ge(in2_act, 10)
            turn(MEM)
            te.wait_ge(xn_ready, xn_count(MEM))
            te.wait_ge(in2_dve, 4)
            for c in range(2):
                n = first["xkv_k"] + c
                arrived(n)
                w = slot(n, 512)
                for j in range(4):
                    x = features(bank[XKV_BANK[2 * c + j // 2]][:, S * (j % 2):S * (j % 2) + S], w, P * j, qT)
                    if j % 2:
                        x.then_inc(xkv_done, 1)
            for c in range(2):
                n = first["xkv_v"] + c
                arrived(n)
                w = slot(n, 512)
                if c:
                    te.wait_ge(xkv_act, 2)
                for t in range(TT):
                    x = tokens(bank[XKV_BANK[4 + 2 * c + t]][:, :], w, slice(0, 512), qT, t)
                    x.then_inc(xkv_done, 1)
            te.wait_ge(rows_done, 3)
            for b, r in enumerate((1, 2)):
                for t in range(TT):
                    x = nc.tensor.transpose(bank[7][:, 16 * b + 8 * t:16 * b + 8 * t + 8], row[:, r, tok(t)],
                                            ident[0:FXH, 0:FXH])
            x.then_inc(cols_turned, 1)

            def all_rows(i):
                return ident[0:FXH, i:i + 1].broadcast_to([FXH, P])

            def mlstm_score(i):
                if i >= 2:
                    te.wait_ge(ml_weight, i - 1)
                s, m = bank[2 * (i % 2)], bank[1 + 2 * (i % 2)]
                mm(m[:, 0:S], all_rows(i), row[:, 7, :], start=True, stop=True)
                mm(s[:, 0:S], v[:, 4 + i, 0:P], v[:, i, :], start=True, stop=True)
                mm(s[:, S:3 * P], v[:, 4 + i, P:S], v[:, i, P:S], start=True, stop=True).then_inc(ml_score, 1)

            def mlstm_pv(i):
                te.wait_ge(ml_weight, i + 1)
                if i >= 2:
                    te.wait_ge(ml_copied, i - 1)
                dst, p = bank[4 + i % 2], pt[:, i % 2, :]
                mm(dst[:, 0:MLV], p[:, 0:P], mlv[:, 0, i, :], start=True, stop=True)
                mm(dst[:, MLV:2 * MLV], p[:, P:S], mlv[:, 0, i, :], start=True, stop=False)
                mm(dst[:, MLV:2 * MLV], p[:, S:3 * P], mlv[:, 1, i, :], start=False, stop=True).then_inc(ml_num, 1)

            te.wait_ge(xkv_act, 8)
            te.wait_ge(qk_ready, KT)
            mlstm_score(0)
            mlstm_score(1)
            for i in range(MLH):
                mlstm_pv(i)
                if i + 2 < MLH:
                    mlstm_score(i + 2)

            def fx_score(i):
                n = HEADS + i
                if i < 2:
                    te.wait_ge(ml_weight, MLH)
                else:
                    te.wait_ge(shifted, n - 1)
                e, j = slice(DH * (i % 2), DH * (i % 2) + DH), i // 2
                s = bank[2 * (i % 2)]
                for t, cols, keys in ((0, slice(0, P), slice(0, P)), (1, slice(P, 3 * P), slice(0, S))):
                    mm(s[:, cols], xnT2[e, j, tok(t)], xnT2[e, 4 + j, keys], start=True, stop=False)
                    x = mm(s[:, cols], all_rows(i), row[:, 0, keys], start=False, stop=True)
                x.then_inc(score_done, 1)

            def fx_turn(i):
                n = HEADS + i
                te.wait_ge(weighed, n + 1)
                if i >= 2:
                    te.wait_ge(pt_act, n - 1)
                else:
                    te.wait_ge(act_link, 3)
                    te.wait_ge(rows_done, 4)
                for q in range(3):
                    x = nc.tensor.transpose(bank[6 + i % 2][:, P * q:P * q + P],
                                            soft[:, i % 2, P * q:P * q + P], ident[:, :])
                x.then_inc(p_turned, 1)

            def fx_pv(i):
                n, j = HEADS + i, i // 2
                te.wait_ge(pt_act, n + 1)
                if i % 2 == 0 and j >= 2:
                    te.wait_ge(o_ready, HEADS // 2 + j - 1)
                dst = bank[1 + 2 * (j % 2)][DH * (i % 2):DH * (i % 2) + DH, :]
                d = slice(DH * i, DH * i + DH)
                mm(dst[:, 0:S], fxv[:, 0, d], pt[:, i % 2, 0:S], start=True, stop=False)
                mm(dst[:, P:S], fxv[:, 1, d], pt[:, i % 2, S:3 * P], start=False, stop=True).then_inc(pv_done, 1)

            fx_score(0)
            fx_score(1)
            for i in range(FXH):
                fx_turn(i)
                if i + 2 < FXH:
                    fx_score(i + 2)
                fx_pv(i)
            te.wait_ge(ml_out, TT)
            for t in range(TT):
                for i in range(MLH):
                    x = nc.tensor.transpose(bank[4 + t][:, P * i:P * i + P], num[:, MLH * t + i, 0:MLD], ident[:, :])
                x.then_inc(ml_turned, 1)
            te.wait_ge(ml_ready, TT)
            te.wait_ge(o_ready, HEADS // 2 + FXH // 2)
            residual_wide("out2", xnT)

            turn(CROSS)
            te.wait_ge(xn_ready, xn_count(CROSS))
            for c in range(2):
                n = first["xq"] + c
                arrived(n)
                w = slot(n, 512)
                for j in range(4):
                    x = features(bank[2 * c + j // 2][:, S * (j % 2):S * (j % 2) + S], w, P * j, xnT)
                    if j % 2:
                        x.then_inc(q_done, 1)

            def x_score(i):
                if i >= 2:
                    te.wait_ge(exp_done, HEADS + FXH + i - 1)
                for t in range(TT):
                    for k in range(2):
                        x = mm(bank[4 + i % 2][:, S * t:S * t + S], xnT2[:, 2 * i + k, tok(t)],
                               memk[:, 2 * i + k, :], start=k == 0, stop=k == 1)
                x.then_inc(score_done, 1)

            def x_turn(i):
                n = HEADS + FXH + i
                te.wait_ge(weighed, n + 1)
                if i >= 2:
                    te.wait_ge(pt_act, n - 1)
                for k in range(2):
                    for t in range(TT):
                        x = nc.tensor.transpose(bank[6 + i % 2][:, S * k + P * t:S * k + P * t + P],
                                                soft[:, i % 2, S * t + P * k:S * t + P * k + P], ident[:, :])
                x.then_inc(p_turned, 1)

            def x_pv(i):
                te.wait_ge(pt_act, HEADS + FXH + i + 1)
                for half in range(2):
                    at = S * i + P * half
                    for k in range(2):
                        x = mm(bank[i][:, S * half:S * half + S], memv[:, k, at:at + P],
                               pt[:, i % 2, S * k:S * k + S], start=k == 0, stop=k == 1)
                x.then_inc(pv_done, 1)

            te.wait_ge(q_ready, 9)
            x_score(0)
            x_score(1)
            for i in range(XH):
                x_turn(i)
                if i + 2 < XH:
                    x_score(i + 2)
                x_pv(i)
            te.wait_ge(o_ready, HEADS // 2 + FXH // 2 + XH)
            residual_wide("xo", xnT)

            turn(FF)
            te.wait_ge(xn_ready, xn_count(FF))
            for c in range(8):
                n = first["ff1"] + c
                arrived(n)
                w = slot(n, 512)
                if c >= 2:
                    te.wait_ge(glu_done, 8 + 2 * FC + 2 * c - 2)
                for j in range(4):
                    x = features(bank[2 * (c % 2) + j // 2][:, S * (j % 2):S * (j % 2) + S], w, P * j, xnT)
                x.then_inc(up_done, 1)
            residual_tall("ff2", D_FF // P, lambda kt: 8 + 2 * FC + kt // 2 + 1)


_INS = ["x", "a_norm", "a_pw1_w", "a_pw1_b", "a_dw_w", "a_dw_b", "a_ln_g", "a_ln_b", "a_pw2_w", "a_pw2_b",
        "kv_norm", "w_kv", "cmp_pos_k", "cmp_pos_v", "phi_k_w1", "phi_k_w2", "phi_v_w1", "phi_v_w2", "b_norm",
        "b_w_in", "b_w_out", "ffn_norm", "ffn_w_in", "ffn_w_out", "final_norm", "mem_2", "ln1_2", "w_in_2",
        "ml_conv_w_2", "ml_conv_b_2", "ml_b_i_2", "ml_b_f_2", "ml_norm_2", "fx_b_f_2", "w_out_2", "ln_x_2",
        "ln_mem_2", "w_xq_2", "w_xkv_2", "w_xo_2", "ln2_2", "w_ff1_2", "w_ff2_2", "ln_f_2"]


def kernel(**inputs):
    import numpy as np
    import concourse.bacc as bacc
    from concourse.bass_utils import run_bass_kernel_spmd

    nc = bacc.Bacc("TRN2", target_bir_lowering=False, num_devices=1)
    arrays, aps = {}, {}
    for name in _INS:
        arrays[f"in_{name}"] = np.ascontiguousarray(inputs[name])
        aps[name] = nc.dram_tensor(f"in_{name}", arrays[f"in_{name}"].shape, F32, kind="ExternalInput").ap()
    out = nc.dram_tensor("out", (1, S, D), F32, kind="ExternalOutput").ap()
    build_kernel(nc, aps, out)
    result = run_bass_kernel_spmd(nc, [arrays], core_ids=[0])
    return result.results[0]["out"]
```

```python
from contextlib import ExitStack

import concourse.bass as bass
from concourse import mybir

F32 = mybir.dt.float32
F32R = mybir.dt.float32r
ACT = mybir.ActivationFunctionType
ALU = mybir.AluOpType
AX = mybir.AxisListType

P = 128
S, D = 256, 1024
TT = S // P
KT = D // P
EPS = 1e-6
NEG = -1e30
TAPS, TAPS2 = 31, 4
F = 2816
FC = F // 256
FT = F // P
HEADS, GROUPS, DH = 16, 2, 64
NCMP = 15
MLH, MLD = 4, 128
FXH = 8
XH = 4
D_FF = 4 * D
RAWS, SPLITS = 4, 3
SLOT = 2048
TAPG = 8
XSCALE = (D // XH) ** -0.5
XKV_BANK = [4, 5, 0, 1, 2, 3, 4, 5]

VECS = [("a_norm", 8), ("a_pw1_b", 16), ("a_dw_b", 8), ("a_ln_g", 8), ("a_ln_b", 8),
        ("kv_norm", 8), ("b_norm", 8), ("ffn_norm", 16), ("final_norm", 8), ("ln1_2", 8),
        ("ml_conv_b_2", 8), ("ln_x_2", 8), ("ln_mem_2", 8), ("ln2_2", 8)]

CONV, FFN0, NSA, FFN1, MID, IN2, MEM, CROSS, FF, LAST = range(10)


def build_kernel(nc, a, out):
    col, n = {}, 0
    for name, rows in VECS:
        col[name] = n
        n += rows
    assert n == P

    ctx = ExitStack()
    with ctx:
        def sb(name, shape, dt=F32):
            return ctx.enter_context(nc.sbuf_tensor(name, shape, dt))

        def halves(name, shape):
            return sb(name + "_hi", shape, F32R), sb(name + "_lo", shape, F32R)

        def sem(name):
            return ctx.enter_context(nc.semaphore(name))

        raw = [sb(f"raw{i}", [P, SLOT]) for i in range(RAWS)]
        split_slot = [halves(f"split{i}", [P, SLOT]) for i in range(SPLITS)]
        h = sb("h", [P, TT, D])
        scaled = sb("scaled", [P, TT, D])
        xn = halves("xn", [P, KT, S])
        ffa = halves("ffa", [P, 4, S])
        act = sb("act", [P, 7184])
        actf = act[:, :]
        PAD = TAPS - 1
        u = sb("u", [P, KT, PAD + S])
        v = sb("v", [P, KT, S])
        vf = v[:, :, :].rearrange("p a b -> p (a b)")
        qT = sb("qT", [P, KT, S])
        qTf = qT[:, :, :].rearrange("p a b -> p (a b)")
        gain_row = sb("gain_row", [P, D])
        gain_ml = sb("gain_ml", [P, MLH * MLD])
        ident = sb("ident", [P, P])
        ones = sb("ones", [P, P])
        mean_w = sb("mean_w", [P, P])
        vecT = sb("vecT", [P, P])
        tapT = sb("tapT", [P, KT, TAPS + TAPS2])
        dist8 = sb("dist8", [P, 3 * P])
        dist8c = sb("dist8c", [P, TT, 16])
        causal = sb("causal", [P, 3 * P])
        causalT = sb("causalT", [P, 3 * P])
        valid = sb("valid", [P, 1])
        nhalf = sb("nhalf", [P, 8])
        posT = sb("posT", [P, 2, 32])
        soft = sb("soft", [P, 2, 800])
        softf = soft[:, :, :].rearrange("p a b -> p (a b)")
        pt = sb("pt", [P, 2, 1024])
        ptf = pt[:, :, :].rearrange("p a b -> p (a b)")
        ssq = sb("ssq", [P, 20])
        msq = sb("msq", [P, 20])
        rstd = sb("rstd", [P, 20])
        gates = sb("gates", [P, TT, 48])
        phi2 = sb("phi2", [P, 2, DH])
        hid = sb("hid", [P, 2, NCMP])
        kcmp = sb("kcmp", [P, GROUPS, NCMP])
        vcmp = sb("vcmp", [NCMP, GROUPS * DH])
        nmax = sb("nmax", [P, 2, 6])
        rsum = sb("rsum", [P, 2, 6])
        coef = sb("coef", [P, 2, 6])
        rcol = sb("rcol", [P, 2, 8])
        den = sb("den", [P, 6, 8])
        expm = sb("expm", [P, TT, 8])
        gate_bias = sb("gate_bias", [FXH, 3])
        gtok = sb("gtok", [P, TT, 16])
        bank = [ctx.enter_context(nc.psum_tensor(f"bank{i}", [P, 512], F32)) for i in range(8)]

        vecs = ptf[:, 0:P]
        taps = softf[0:TAPS + TAPS2, 0:D]
        pos = ptf[0:32, 256:512]
        pw2_row = qT[0:1, 0:4, :].rearrange("p a b -> p (a b)")
        CONV_DVE = 5
        NDIAG = 7
        diag = actf[:, 0:NDIAG * TAPG * P].rearrange("p (g t c) -> p g t c", t=TAPG, c=P)
        window = softf[:, 0:2 * 32 * NCMP].rearrange("p (b l n) -> p b l n", b=2, l=32)
        BIAS = 416
        biases = actf[:, 0:HEADS * BIAS].rearrange("p (h c) -> p h c", c=BIAS)
        k2 = vf[:, 0:1024].rearrange("p (g b k) -> p g b k", g=GROUPS, b=2)
        vtok = vf[:, 1024:1536].rearrange("p (t b c) -> p t b c", t=TT, b=2)
        memk = actf[:, 0:2048].rearrange("p (f m) -> p f m", m=S)
        memv = actf[:, 2048:4096].rearrange("p (t c) -> p t c", t=TT)
        MLV = MLD + 1
        mlv = actf[:, 4096:4096 + TT * MLH * MLV].rearrange("p (t h c) -> p t h c", t=TT, c=MLV)
        mlo = actf[:, 5136:6160].rearrange("p (t c) -> p t c", t=TT)
        fxv = actf[:, 6160:7184].rearrange("p (t c) -> p t c", t=TT)
        row = scaled[0:FXH, :, :].rearrange("p a b -> p (a b)").rearrange("p (r t) -> p r t", t=S)
        memraw = actf[:, 0:2048].rearrange("p (t n) -> p t n", t=TT)
        uf = u[:, :, :].rearrange("p a b -> p (a b)")
        num = uf[:, 1024:1024 + TT * MLH * MLV].rearrange("p (i c) -> p i c", c=MLV)
        mlsq = uf[:, 0:TT * MLH * MLD].rearrange("p (i c) -> p i c", c=MLD)
        NSA_PIECES = [slice(256, 271), slice(0, 128), slice(128, 256),
                      slice(272, 287), slice(288, 544), slice(544, 800)]

        raw_loaded = [sem(f"raw_loaded{i}") for i in range(RAWS)]
        split_hi = sem("split_hi")
        split_lo = sem("split_lo")
        slots_used = sem("slots_used")
        x_loaded = [sem("x_loaded0"), sem("x_loaded1")]
        vecs_loaded = sem("vecs_loaded")
        vecs_loaded_pool = sem("vecs_loaded_pool")
        small_loaded = sem("small_loaded")
        mem_loaded = sem("mem_loaded")
        gains_loaded = sem("gains_loaded")
        last_gain_loaded = sem("last_gain_loaded")
        taken = sem("taken")
        xn_hi = sem("xn_hi")
        ffa_hi = sem("ffa_hi")
        ffa_ready = sem("ffa_ready")
        conv_link = sem("conv_link")
        conv_dve = sem("conv_dve")
        silu_hi = sem("silu_hi")
        silu_lo = sem("silu_lo")
        o_hi = sem("o_hi")
        gates_copied = sem("gates_copied")
        out_stored = sem("out_stored")
        pool_step = sem("pool_step")
        consts_built = sem("consts_built")
        bias_built = sem("bias_built")
        h_ready = sem("h_ready")
        ss_ready = sem("ss_ready")
        ms_ready = sem("ms_ready")
        rstd_ready = sem("rstd_ready")
        scaled_ready = sem("scaled_ready")
        turned = sem("turned")
        xn_ready = sem("xn_ready")
        acc_done = sem("acc_done")
        out_ready = sem("out_ready")
        pre_turned = sem("pre_turned")
        pre_copied = sem("pre_copied")
        up_done = sem("up_done")
        gate_act = sem("gate_act")
        glu_done = sem("glu_done")
        diag_built = sem("diag_built")
        diag_used = sem("diag_used")
        conv_out = sem("conv_out")
        stat_done = sem("stat_done")
        centred = sem("centred")
        squared = sem("squared")
        std_ready = sem("std_ready")
        rstd_row = sem("rstd_row")
        normed = sem("normed")
        silu_ready = sem("silu_ready")
        pads_zero = sem("pads_zero")
        kv_done = sem("kv_done")
        window_ready = sem("window_ready")
        kv_dve = sem("kv_dve")
        kv_act = sem("kv_act")
        phi_done = sem("phi_done")
        q_done = sem("q_done")
        q_ready = sem("q_ready")
        score_done = sem("score_done")
        shifted = sem("shifted")
        exp_done = sem("exp_done")
        dve_link = sem("dve_link")
        act_link = sem("act_link")
        weighed = sem("weighed")
        p_turned = sem("p_turned")
        pt_dve = sem("pt_dve")
        pt_act = sem("pt_act")
        pv_done = sem("pv_done")
        o_ready = sem("o_ready")
        in2_done = sem("in2_done")
        in2_act = sem("in2_act")
        in2_dve = sem("in2_dve")
        conv4_done = sem("conv4_done")
        qk_ready = sem("qk_ready")
        rows_done = sem("rows_done")
        cols_turned = sem("cols_turned")
        xkv_done = sem("xkv_done")
        xkv_act = sem("xkv_act")
        xkv_dve = sem("xkv_dve")
        ml_score = sem("ml_score")
        ml_shift = sem("ml_shift")
        ml_exp = sem("ml_exp")
        ml_weight = sem("ml_weight")
        ml_num = sem("ml_num")
        ml_copied = sem("ml_copied")
        ml_sq = sem("ml_sq")
        ml_ms = sem("ml_ms")
        ml_rstd = sem("ml_rstd")
        ml_out = sem("ml_out")
        ml_turned = sem("ml_turned")
        ml_ready = sem("ml_ready")

        chunks, chunk_of, freed, is_split, used_cols = [], {}, [], [], []

        def chunk(stage, parts, by=None, to_split=True, cols=SLOT):
            chunk_of.setdefault(stage, []).append(len(chunks))
            used_cols.append(cols)
            chunks.append(parts)
            freed.append(by or (slots_used, 1 + sum(sm is slots_used for sm, _ in freed)))
            is_split.append(to_split)

        def kn(s, n, k=KT):
            return s[:, 0:k * n].rearrange("p (k n) -> p k n", n=n)

        def by_rows(w):
            return w.rearrange("(k p) n -> p k n", p=P)

        def wide(stage, w, start, width, by=None):
            chunk(stage, [(lambda s: kn(s, width), by_rows(w)[:, :, start:start + width])], by,
                  cols=KT * width)

        def pair(stage, w, start, other, by):
            chunk(stage, [(lambda s, b=b: kn(s, 256)[:, :, P * b:P * b + P], by_rows(w)[:, :, c:c + P])
                          for b, c in enumerate((start, other))], by)

        def half_rows(stage, w, start, by):
            for k in range(2):
                chunk(stage, [(lambda s: kn(s, 512, 4), by_rows(w)[:, 4 * k:4 * k + 4, start:start + 512])],
                      by if k else None)

        def tall(stage, w, k, acc, tiles):
            chunk(stage, [(lambda s: kn(s, D, 2), by_rows(w)[:, k:k + 2, :])],
                  (acc_done, acc) if k + 2 == tiles else None)

        def residual(stage, w, acc):
            for c in range(2):
                half_rows(stage, w, 512 * c, (acc_done, acc + 2 * c + 2))

        UP0 = {"pw1": 0, "ffn0": KT, "ffn1": KT + FT, "ff": KT + 2 * FT}

        for c in range(KT):
            pair("pw1", a["a_pw1_w"][0], P * c, D + P * c, (up_done, c + 1))
        residual("pw2", a["a_pw2_w"][0], 0)

        def ffn_chunks(which, acc):
            stage, w, down = f"ffn{which}", a["ffn_w_in"][which], a["ffn_w_out"][which]
            for g in range(FC + 1):
                if g < FC:
                    for ft in (2 * g, 2 * g + 1):
                        pair(stage + "_in", w, P * ft, F + P * ft, (up_done, UP0[stage] + ft + 1))
                if g:
                    tall(stage + "_out", down, 2 * g - 2, acc, FT)

        ffn_chunks(0, 8)
        for c in range(2):
            wide("kv", a["w_kv"], 256 * c, 256, (kv_done, c + 1))
        wide("kv", a["w_kv"], 512, 256, (kv_done, 3))
        for b, name in enumerate(("phi_k_w1", "phi_v_w1")):
            chunk("phi", [(lambda s, g=g: s[DH * g:DH * g + DH, :].rearrange("p (l e) -> p l e", e=DH),
                           a[name].rearrange("(l d) e -> d l e", d=DH)) for g in range(2)],
                  (phi_done, b + 1), to_split=False)
        for c in range(4):
            wide("q", a["b_w_in"][0], 256 * c, 256, (q_done, c + 1))
        wide("gates", a["b_w_in"][0], D, 48, (q_done, 5))
        residual("b_out", a["b_w_out"][0], 8)
        ffn_chunks(1, 16)
        w_in2 = a["w_in_2"][0]
        for c in range(4):
            wide("ml_qk", w_in2, 256 * c, 256, (in2_done, c + 1))
        half_rows("ml_v", w_in2, 1024, (in2_done, 5))
        half_rows("ml_o", w_in2, 1536, (in2_done, 6))
        for c in range(2):
            wide("fx_q", w_in2, 2056 + 256 * c, 256, (in2_done, 7 + c))
        for c in range(2):
            wide("fx_k", w_in2, 2568 + 256 * c, 256, (in2_done, 9 + c))
        half_rows("fx_v", w_in2, 3080, (in2_done, 11))
        chunk("rows", [(lambda s: kn(s, 16)[:, :, 0:8], by_rows(w_in2)[:, :, 2048:2056]),
                       (lambda s: kn(s, 16)[:, :, 8:16], by_rows(w_in2)[:, :, 3592:3600])], (in2_done, 12), cols=KT * 16)
        for c in range(4):
            wide("xkv_k", a["w_xkv_2"][0], 256 * c, 256, (xkv_done, c + 1))
        for c in range(2):
            half_rows("xkv_v", a["w_xkv_2"][0], D + 512 * c, (xkv_done, 4 + 2 * c + 2))
        residual("out2", a["w_out_2"][0], 16)
        for c in range(4):
            wide("xq", a["w_xq_2"][0], 256 * c, 256, (q_done, 5 + c + 1))
        residual("xo", a["w_xo_2"][0], 20)
        for g in range(17):
            if g < 16:
                wide("ff_in", a["w_ff1_2"][0], 256 * g, 256, (up_done, UP0["ff"] + g + 1))
            if g:
                tall("ff_out", a["w_ff2_2"][0], 2 * g - 2, 28, D_FF // P)

        nth = [sum(is_split[:c]) for c in range(len(chunks))]
        of_split = [c for c in range(len(chunks)) if is_split[c]]

        def loads_through(c):
            return 16 * sum(len(chunks[i]) for i in range(c % RAWS, c + 1, RAWS))

        def splitter(emit):
            at = [0]

            def through(c):
                while at[0] <= min(c, len(chunks) - 1):
                    if is_split[at[0]]:
                        emit(at[0], nth[at[0]])
                    at[0] += 1
            return through

        stage_before = {FFN0: "pw2", NSA: "ffn0_out", FFN1: "b_out", MID: "ffn1_out", CROSS: "out2",
                        FF: "xo", LAST: "ff_out"}

        def last_before(k):
            return chunk_of[stage_before[k]][-1]

        turning = [CONV, FFN0, NSA, FFN1, IN2, MEM, CROSS, FF]
        gains = {CONV: [("a_norm", 0)], FFN0: [("ffn_norm", 0)], NSA: [("kv_norm", 0), ("b_norm", 0)],
                 FFN1: [("ffn_norm", 8)], IN2: [("ln1_2", 0)], MEM: [("ln_mem_2", 0)],
                 CROSS: [("ln_x_2", 0)], FF: [("ln2_2", 0)]}
        xn_before, n = {}, 0
        for k in turning:
            xn_before[k] = n
            n += 4 * len(gains[k])
        h_order = [FFN0, NSA, FFN1, MID, IN2, CROSS, FF, LAST]
        residuals = [FFN0, NSA, FFN1, MID, CROSS, FF, LAST]

        def h_count(k, t):
            return TT * h_order.index(k) + t + 1

        def xn_count(k, which=0):
            return xn_before[k] + 4 * (which + 1)

        def ends(k):
            if k in (NSA, MID, LAST):
                return [(t, c) for t in range(TT) for c in range(2)]
            return [(t, c) for c in range(2) for t in range(TT)]

        def tok(t):
            return slice(P * t, P * t + P)

        block = ctx.enter_context(nc.Block())

        loads = []
        for name, rows in VECS:
            s = a[name]
            loads.append((vecs[col[name]:col[name] + rows, :],
                          s.rearrange("(k p) -> k p", p=P) if len(s.shape) == 1 else
                          s.rearrange("a (k p) -> (a k) p", p=P)))
        loads.append((taps[0:TAPS, :], a["a_dw_w"][0]))
        loads.append((taps[TAPS:TAPS + TAPS2, :], a["ml_conv_w_2"][0]))
        for b, name in enumerate(("cmp_pos_k", "cmp_pos_v")):
            for g in range(2):
                loads.append((pos[:, P * b + DH * g:P * b + DH * g + DH], a[name]))
        pool_loads, act_loads = loads[0::2], loads[1::2]

        @block.sync
        def _(sp):
            for t in range(TT):
                sp.dma_start(h[:, t, :], a["x"][0].rearrange("(t p) n -> p t n", p=P)[:, t, :]
                             ).then_inc(x_loaded[t], 16)
            for c, parts in enumerate(chunks):
                if c >= RAWS:
                    last = c - RAWS
                    if is_split[last]:
                        sp.wait_ge(split_lo, nth[last] + 1)
                    else:
                        sp.wait_ge(*freed[last])
                for place, src in parts:
                    sp.dma_start(place(raw[c % RAWS]), src).then_inc(raw_loaded[c % RAWS], 16)
            for t in range(TT):
                sp.wait_ge(out_ready, t + 1)
                sp.dma_start(out[0].rearrange("(t p) n -> p t n", p=P)[:, t, :],
                             scaled[:, t, :]).then_inc(out_stored, 16)
            sp.wait_ge(out_stored, 32)

        @block.gpsimd
        def _(pool):
            for dst, src in pool_loads:
                pool.dma_start(dst, src).then_inc(vecs_loaded_pool, 16)
            nc.gpsimd.memset(ident[:, :], 0.0).then_inc(pool_step, 1)
            nc.gpsimd.memset(nhalf[:, :], -0.5).then_inc(pool_step, 1)
            nc.gpsimd.memset(mean_w[:, :], 1.0 / D).then_inc(pool_step, 1)
            nc.gpsimd.memset(causal[:, :], 0.0).then_inc(pool_step, 1)
            nc.gpsimd.memset(causalT[:, :], 0.0).then_inc(pool_step, 1)
            nc.gpsimd.memset(valid[:, :], 1.0).then_inc(pool_step, 1)
            nc.gpsimd.memset(ones[:, :], 1.0).then_inc(pool_step, 1)
            nc.gpsimd.iota(dist8[:, 0:P], pattern=[[8, P]], base=0, channel_multiplier=-8,
                           allow_small_or_imprecise_dtypes=True).then_inc(pool_step, 1)
            nc.gpsimd.iota(dist8[:, P:3 * P], pattern=[[8, 2 * P]], base=-8 * P, channel_multiplier=-8,
                           allow_small_or_imprecise_dtypes=True).then_inc(pool_step, 1)
            nc.gpsimd.iota(dist8c[:, :, :], pattern=[[-8 * P, 2], [128, 16]], base=8 * 31,
                           channel_multiplier=-8, allow_small_or_imprecise_dtypes=True).then_inc(pool_step, 1)
            pool.wait_ge(pool_step, 10)
            nc.gpsimd.affine_select(out=ident[:, :], in_=ident[:, :], compare_op=ALU.not_equal, fill=1.0,
                                    base=0, pattern=[[-1, P]], channel_multiplier=1).then_inc(consts_built, 1)

            def mask(m, pattern, base, step):
                nc.gpsimd.affine_select(out=m, in_=m, compare_op=ALU.is_ge, fill=NEG, base=base,
                                        pattern=pattern, channel_multiplier=step).then_inc(consts_built, 1)

            for m in (dist8, causal):
                mask(m[:, 0:P], [[-1, P]], 0, 1)
                mask(m[:, P:3 * P], [[-1, 2 * P]], P, 1)
            mask(dist8c[:, :, :], [[P, 2], [-16, 16]], -31, 1)
            mask(causalT[:, 0:2 * P], [[1, 2 * P]], 0, -1)
            mask(causalT[:, 2 * P:3 * P], [[1, P]], 0, -1)
            nc.gpsimd.affine_select(out=valid[:, :], in_=valid[:, :], compare_op=ALU.is_ge, fill=0.0,
                                    base=-31, pattern=[[0, 1]], channel_multiplier=1).then_inc(consts_built, 1)

            def root(k):
                for t in range(TT):
                    c = TT * k + t
                    pool.wait_ge(ss_ready, c + 1)
                    nc.gpsimd.tensor_scalar(msq[:, c:c + 1], ssq[:, c:c + 1], 1.0 / D, EPS,
                                            ALU.mult, ALU.add).then_inc(ms_ready, 1)
                    pool.wait_ge(ms_ready, c + 1)
                    nc.gpsimd.tensor_tensor(rstd[:, c:c + 1], msq[:, c:c + 1], nhalf[:, 0:1],
                                            ALU.pow).then_inc(rstd_ready, 1)

            for k in (CONV, FFN0):
                root(k)
            pool.wait_ge(h_ready, h_count(FFN0, 1))
            pool.wait_ge(consts_built, 9)
            for i in range(HEADS):
                slope = 2.0 ** (-8.0 * (i + 1) / HEADS)
                nc.gpsimd.tensor_scalar(biases[:, i, 0:3 * P], dist8[:, :], slope, None, ALU.mult)
                nc.gpsimd.tensor_scalar(biases[:, i, 3 * P:3 * P + 32],
                                        dist8c[:, :, :].rearrange("p a b -> p (a b)"), slope, None,
                                        ALU.mult).then_inc(bias_built, 1)
            for k in (NSA, FFN1, MID, IN2, MEM):
                root(k)
            pool.wait_ge(ml_sq, 1)
            nc.gpsimd.tensor_scalar(den[:, 4, :], den[:, 3, :], 1.0 / MLD, EPS, ALU.mult,
                                    ALU.add).then_inc(ml_ms, 1)
            pool.wait_ge(ml_ms, 1)
            nc.gpsimd.tensor_tensor(den[:, 5, :], den[:, 4, :], nhalf[:, :], ALU.pow).then_inc(ml_rstd, 1)
            for k in (CROSS, FF, LAST):
                root(k)

        @block.scalar
        def _(sc):
            for dst, src in act_loads:
                sc.dma_start(dst, src).then_inc(vecs_loaded, 16)
            for b, name in enumerate(("phi_k_w2", "phi_v_w2")):
                for g in range(2):
                    sc.dma_start(phi2[DH * g:DH * g + DH, b, :], a[name]).then_inc(small_loaded, 16)
            sc.dma_start(pw2_row, a["a_pw2_b"]).then_inc(small_loaded, 16)
            sc.wait_ge(pads_zero, 1)
            for b, (name, m) in enumerate((("fx_b_f_2", FXH), ("ml_b_f_2", MLH), ("ml_b_i_2", MLH))):
                sc.dma_start(gate_bias[0:m, b:b + 1], a[name].rearrange("a n -> n a")).then_inc(small_loaded, 16)
            sc.dma_start(gain_row[:, :], a["final_norm"].rearrange("(a n) -> a n", a=1)
                         .broadcast_to([P, D])).then_inc(gains_loaded, 16)
            sc.dma_start(gain_ml[:, :], a["ml_norm_2"].broadcast_to([P, MLH * MLD])).then_inc(gains_loaded, 16)


            def split(c, m):
                sc.wait_ge(raw_loaded[c % RAWS], loads_through(c))
                if m >= SPLITS:
                    sc.wait_ge(*freed[of_split[m - SPLITS]])
                n = used_cols[c]
                nc.scalar.activation(split_slot[m % SPLITS][0][:, 0:n], raw[c % RAWS][:, 0:n],
                                     ACT.Copy).then_inc(split_hi, 1)

            through = splitter(split)

            def squares(k, src, ready):
                for t in range(TT):
                    ready(t)
                    nc.scalar.activation(scaled[:, t, :], src[:, t, :], ACT.Square,
                                         accum_out=ssq[:, TT * k + t:TT * k + t + 1]).then_inc(ss_ready, 1)

            def h_squares(k):
                if k in stage_before:
                    through(last_before(k) + 2)
                squares(k, h, lambda t: sc.wait_ge(h_ready, h_count(k, t)))
                if k in stage_before:
                    through(last_before(k) + 3)

            def take_hi(k, which=0):
                for n in range(4):
                    t, half = n // 2, n % 2
                    sc.wait_ge(taken, xn_before[k] + 4 * which + n + 1)
                    nc.scalar.activation(xn[0][:, 4 * half:4 * half + 4, tok(t)],
                                         ptf[:, 512 * n:512 * n + 512].rearrange("p (k c) -> p k c", k=4),
                                         ACT.Copy).then_inc(xn_hi, 1)

            squares(CONV, h, lambda t: sc.wait_ge(x_loaded[t], 16))
            through(2)
            take_hi(CONV)

            sc.wait_ge(pre_copied, 3)
            sc.wait_ge(consts_built, 1)

            def diagonals(g):
                ft, m = CONV_DVE + g // 4, min(TAPG, TAPS - TAPG * (g % 4))
                if g >= NDIAG:
                    sc.wait_ge(diag_used, g - NDIAG + 1)
                for q in range(m):
                    j = TAPG * (g % 4) + q
                    x = nc.scalar.activation(diag[:, g % NDIAG, q, :], ident[:, :], ACT.Copy,
                                             scale=tapT[:, ft, j:j + 1])
                x.then_inc(diag_built, 1)

            for ft in range(KT):
                through(chunk_of["pw1"][ft] + 2)
                sc.wait_ge(up_done, ft + 1)
                if ft >= 4:
                    sc.wait_ge(glu_done, ft - 3)
                nc.scalar.activation(softf[:, S * (ft % 4):S * (ft % 4) + S], bank[ft % 4][:, S:2 * S], ACT.Sigmoid,
                                     bias=vecT[:, col["a_pw1_b"] + 8 + ft:col["a_pw1_b"] + 9 + ft]
                                     ).then_inc(gate_act, 1)
                if ft < NDIAG:
                    diagonals(ft)
            through(chunk_of["pw2"][2])
            for ft in range(CONV_DVE, KT):
                n = ft - CONV_DVE
                for g in range(NDIAG, 4 * (KT - CONV_DVE)):
                    if (g - NDIAG) // 4 == n:
                        diagonals(g)
                sc.wait_ge(diag_used, 4 * (n + 1))
                nc.scalar.activation(v[:, ft, :], bank[4 + n][:, 0:S], ACT.Identity,
                                     bias=vecT[:, col["a_dw_b"] + ft:col["a_dw_b"] + ft + 1]).then_inc(conv_out, 1)
            for j in range(2):
                sc.wait_ge(centred, j + 1)
                nc.scalar.activation(actf[:, D * j:D * j + D], vf[:, D * j:D * j + D],
                                     ACT.Square).then_inc(squared, 1)
            sc.wait_ge(rstd_row, 1)
            nc.scalar.activation(softf[:, 0:S], softf[:, 0:S], ACT.Sqrt).then_inc(std_ready, 1)
            for ft in range(KT):
                sc.wait_ge(normed, ft // 4 + 1)
                nc.scalar.activation(v[:, ft, :], v[:, ft, :], ACT.Silu,
                                     bias=vecT[:, col["a_ln_b"] + ft:col["a_ln_b"] + ft + 1],
                                     scale=vecT[:, col["a_ln_g"] + ft:col["a_ln_g"] + ft + 1]
                                     ).then_inc(silu_ready, 1)

            def ffn_act(which):
                stage = f"ffn{which}"
                for ft in range(FT):
                    through(chunk_of[stage + "_in"][ft] + 2)
                    n, b = UP0[stage] + ft, slice(S * (ft % 4), S * (ft % 4) + S)
                    sc.wait_ge(up_done, n + 1)
                    nc.scalar.activation(softf[:, b], bank[ft % 4][:, 0:S], ACT.Silu).then_inc(gate_act, 1)
                    sc.wait_ge(glu_done, n + 1)
                    if ft >= 4:
                        sc.wait_ge(*freed[chunk_of[stage + "_out"][ft // 2 - 2]])
                    nc.scalar.activation(ffa[0][:, ft % 4, :], ptf[:, b], ACT.Copy).then_inc(ffa_hi, 1)

            h_squares(FFN0)
            take_hi(FFN0)
            ffn_act(0)
            h_squares(NSA)
            take_hi(NSA)
            sc.wait_ge(kv_done, 3)
            through(chunk_of["q"][0])
            take_hi(NSA, 1)
            through(chunk_of["q"][2])

            for half in range(2):
                nc.scalar.activation(k2[DH * half:DH * half + DH, 1, :, :].rearrange("p b k -> p (b k)"),
                                     bank[5][DH:P, :], ACT.Copy).then_inc(kv_act, 1)
            sc.wait_ge(phi_done, 2)
            nc.scalar.activation(hid[:, :, :], bank[7][:, 0:32].rearrange("p (b n) -> p b n", b=2)[:, :, 0:NCMP],
                                 ACT.Silu).then_inc(kv_act, 1)
            for b in range(4):
                through(chunk_of["q"][b] + 2)
                sc.wait_ge(q_done, b + 1)
                nc.scalar.activation(qTf[:, 512 * b:512 * b + 512], bank[b][:, :], ACT.Copy).then_inc(q_ready, 1)
            through(chunk_of["gates"][0] + 2)
            sc.wait_ge(q_done, 5)
            nc.scalar.activation(gates[:, :, :].rearrange("p t c -> p (t c)"), bank[4][:, 0:96],
                                 ACT.Sigmoid).then_inc(q_ready, 1)
            sc.wait_ge(phi_done, 3)
            for g in range(GROUPS):
                nc.scalar.activation(kcmp[:, g, :], bank[7 - g][:, 64:64 + NCMP], ACT.Copy)
                nc.scalar.activation(vcmp[:, DH * g:DH * g + DH], bank[7 - g][0:NCMP, P:P + DH],
                                     ACT.Copy).then_inc(kv_act, 1)

            def nsa_exp(i):
                s = soft[:, i % 2, :]
                sc.wait_ge(shifted, i + 1)
                for n, piece in enumerate(NSA_PIECES):
                    x = nc.scalar.activation(s[:, piece], s[:, piece], ACT.Exp, scale=-1.0,
                                             bias=nmax[:, i % 2, n:n + 1], accum_out=rsum[:, i % 2, n:n + 1])
                x.then_inc(exp_done, 1)

            def nsa_evac(i):
                sc.wait_ge(p_turned, i + 1)
                if i >= 2:
                    sc.wait_ge(pv_done, i - 1)
                nc.scalar.activation(pt[:, i % 2, 384:768], bank[5][:, 0:384], ACT.Copy)
                nc.scalar.activation(pt[0:NCMP, i % 2, 768 + P:1024], bank[5][0:NCMP, 384:512],
                                     ACT.Copy).then_inc(pt_act, 1)

            def out_hi(pv, dst, src):
                sc.wait_ge(pv_done, pv)
                nc.scalar.activation(dst, src, ACT.Copy).then_inc(o_hi, 1)

            nsa_exp(0)
            through(chunk_of["gates"][0] + 3)
            for i in range(HEADS):
                if i + 1 < HEADS:
                    nsa_exp(i + 1)
                nsa_evac(i)
                if i % 2 == 0 and i:
                    out_hi(i, xn[0][:, i // 2 - 1, :], bank[6 + (i // 2 - 1) % 2][:, 0:S])
            out_hi(HEADS, xn[0][:, HEADS // 2 - 1, :], bank[7][:, 0:S])

            sc.wait_ge(shifted, HEADS)
            mem_src = a["mem_2"][0].rearrange("(t p) n -> p t n", p=P)
            sc.dma_start(memraw, mem_src).then_inc(mem_loaded, 16)
            h_squares(FFN1)
            take_hi(FFN1)
            ffn_act(1)
            h_squares(MID)
            h_squares(IN2)
            sc.dma_start(gain_row[:, :], a["ln_f_2"].rearrange("(a n) -> a n", a=1)
                         .broadcast_to([P, D])).then_inc(last_gain_loaded, 16)
            take_hi(IN2)

            def memory_ready(t):
                sc.wait_ge(mem_loaded, 16)
                sc.wait_ge(turned, 4 * turning.index(IN2) + 4)

            squares(MEM, memraw, memory_ready)

            for b in range(4):
                through(chunk_of["ml_qk"][b] + 2)
                sc.wait_ge(in2_done, b + 1)
                nc.scalar.activation(u[:, 2 * b:2 * b + 2, PAD:PAD + S],
                                     bank[b][:, :].rearrange("p (f t) -> p f t", f=2),
                                     ACT.Copy).then_inc(in2_act, 1)
            through(chunk_of["ml_v"][1] + 2)
            for ft in range(KT):
                sc.wait_ge(conv4_done, ft + 1)
                nc.scalar.activation(v[:, ft, :], v[:, ft, :], ACT.Silu).then_inc(qk_ready, 1)
            through(chunk_of["ml_o"][1] + 2)
            sc.wait_ge(in2_done, 6)
            for t in range(TT):
                nc.scalar.activation(mlo[:, t, :], bank[6 + t][:, :], ACT.Sigmoid).then_inc(in2_act, 1)
            for b in range(4):
                through(chunk_of["fx_q"][0] + b + 2)
                sc.wait_ge(in2_done, 7 + b)
                nc.scalar.activation(qTf[:, 512 * b:512 * b + 512], bank[b][:, :], ACT.Copy).then_inc(in2_act, 1)
            through(chunk_of["rows"][0] + 3)
            take_hi(MEM)
            sc.wait_ge(rows_done, 1)
            nc.scalar.activation(row[:, 2:4, :], row[:, 2:4, :], ACT.Exp).then_inc(act_link, 1)
            through(chunk_of["xkv_k"][3])
            sc.wait_ge(rows_done, 2)
            nc.scalar.activation(row[:, 6:8, :], row[:, 4:6, :], ACT.Ln).then_inc(act_link, 1)
            for b in range(8):
                through((chunk_of["xkv_k"][b] if b < 4 else chunk_of["xkv_v"][2 * (b // 2) - 3]) + 2)
                sc.wait_ge(xkv_done, b + 1)
                dst = memk[:, 2 * b:2 * b + 2, :].rearrange("p f t -> p (f t)") if b < 4 else \
                    memv[:, b % 2, 512 * (b // 2 - 2):512 * (b // 2 - 2) + 512]
                nc.scalar.activation(dst, bank[XKV_BANK[b]][:, :], ACT.Copy).then_inc(xkv_act, 1)
            through(chunk_of["out2"][2])
            sc.wait_ge(rows_done, 4)
            nc.scalar.activation(expm[:, :, :], bank[7][:, 16:32].rearrange("p (t n) -> p t n", t=TT),
                                 ACT.Exp).then_inc(act_link, 1)

            for i in range(MLH):
                sc.wait_ge(ml_shift, i + 1)
                w = soft[:, i % 2, :]
                nc.scalar.activation(w[:, 0:S], w[:, 0:S], ACT.Exp, bias=rcol[:, 0, i:i + 1])
                nc.scalar.activation(w[:, S:3 * P], w[:, S:3 * P], ACT.Exp,
                                     bias=rcol[:, 1, i:i + 1]).then_inc(ml_exp, 1)
            sc.wait_ge(ml_copied, MLH + 1)
            nc.scalar.activation(mlsq, num[:, :, 0:MLD], ACT.Square).then_inc(act_link, 1)

            def fx_exp(i):
                n, s = HEADS + i, soft[:, i % 2, :]
                sc.wait_ge(shifted, n + 1)
                nc.scalar.activation(s[:, 0:P], s[:, 0:P], ACT.Exp, scale=-1.0, bias=nmax[:, i % 2, 0:1],
                                     accum_out=rsum[:, i % 2, 0:1])
                nc.scalar.activation(s[:, P:3 * P], s[:, P:3 * P], ACT.Exp, scale=-1.0,
                                     bias=nmax[:, i % 2, 1:2],
                                     accum_out=rsum[:, i % 2, 1:2]).then_inc(exp_done, 1)

            def fx_evac(i):
                n = HEADS + i
                sc.wait_ge(p_turned, n + 1)
                if i < 2:
                    sc.wait_ge(ml_num, MLH)
                else:
                    sc.wait_ge(pv_done, n - 1)
                nc.scalar.activation(pt[:, i % 2, 0:3 * P], bank[6 + i % 2][:, 0:3 * P],
                                     ACT.Copy).then_inc(pt_act, 1)

            fx_exp(0)
            for i in range(FXH):
                if i + 1 < FXH:
                    fx_exp(i + 1)
                fx_evac(i)
                if i % 2 == 0 and i:
                    out_hi(HEADS + i, xn[0][:, 3 + i // 2, :], bank[1 + 2 * ((i // 2 - 1) % 2)][:, 0:S])
            out_hi(HEADS + FXH, xn[0][:, KT - 1, :], bank[3][:, 0:S])
            for t in range(TT):
                sc.wait_ge(ml_turned, t + 1)
                nc.scalar.activation(xn[0][:, 0:MLH, tok(t)], bank[4 + t][:, :].rearrange("p (h c) -> p h c", h=MLH),
                                     ACT.Copy).then_inc(o_hi, 1)

            h_squares(CROSS)
            take_hi(CROSS)
            for b in range(4):
                through(chunk_of["xq"][b] + 2)
                sc.wait_ge(q_done, 6 + b)
                nc.scalar.activation(qTf[:, 512 * b:512 * b + 512], bank[b][:, :], ACT.Copy).then_inc(q_ready, 1)
            through(chunk_of["xo"][2])

            def x_exp(i):
                n = HEADS + FXH + i
                sc.wait_ge(shifted, n + 1)
                for t in range(TT):
                    x = nc.scalar.activation(soft[:, i % 2, S * t:S * t + S], bank[4 + i % 2][:, S * t:S * t + S],
                                             ACT.Exp, scale=XSCALE, bias=nmax[:, i % 2, 2 + t:3 + t],
                                             accum_out=rsum[:, i % 2, t:t + 1])
                x.then_inc(exp_done, 1)

            def x_evac(i):
                n = HEADS + FXH + i
                sc.wait_ge(p_turned, n + 1)
                if i >= 2:
                    sc.wait_ge(pv_done, n - 1)
                nc.scalar.activation(pt[:, i % 2, 0:512], bank[6 + i % 2][:, :], ACT.Copy).then_inc(pt_act, 1)

            def x_out_hi(i):
                out_hi(HEADS + FXH + i + 1, xn[0][:, 2 * i:2 * i + 2, :].rearrange("p f t -> p (f t)"), bank[i][:, :])

            x_exp(0)
            for i in range(XH):
                if i + 1 < XH:
                    x_exp(i + 1)
                x_evac(i)
                if i:
                    x_out_hi(i - 1)
            x_out_hi(XH - 1)

            h_squares(FF)
            take_hi(FF)
            for g in range(D_FF // S):
                through(chunk_of["ff_in"][g] + 2)
                n = UP0["ff"] + g
                sc.wait_ge(up_done, n + 1)
                nc.scalar.activation(softf[:, 512 * (g % 3):512 * (g % 3) + 512], bank[g % 4][:, :],
                                     ACT.Relu).then_inc(gate_act, 1)
                sc.wait_ge(glu_done, n + 1)
                if g >= 2:
                    sc.wait_ge(*freed[chunk_of["ff_out"][g - 2]])
                nc.scalar.activation(ffa[0][:, 2 * (g % 2):2 * (g % 2) + 2, :].rearrange("p f t -> p (f t)"),
                                     ptf[:, 512 * (g % 4):512 * (g % 4) + 512], ACT.Copy).then_inc(ffa_hi, 1)
            h_squares(LAST)

        @block.vector
        def _(ve):
            links = [0]

            def link(x):
                links[0] += 1
                x.then_inc(dve_link, 1)
                ve.wait_ge(dve_link, links[0])

            def less_hi(dst, src, hi):
                return nc.vector.tensor_tensor(dst, src, hi.bitcast(F32), ALU.subtract)

            def split(c, m):
                ve.wait_ge(split_hi, m + 1)
                n, (hi, lo) = used_cols[c], split_slot[m % SPLITS]
                less_hi(lo[:, 0:n], raw[c % RAWS][:, 0:n], hi[:, 0:n]).then_inc(split_lo, 1)

            through = splitter(split)

            def scale(k, src):
                for t in range(TT):
                    ve.wait_ge(rstd_ready, TT * k + t + 1)
                    nc.vector.tensor_scalar(scaled[:, t, :], src[:, t, :], rstd[:, TT * k + t:TT * k + t + 1],
                                            None, ALU.mult).then_inc(scaled_ready, 1)

            def take(k, which=0):
                idx = turning.index(k)
                name, off = gains[k][which]
                g0, n0 = col[name] + off, xn_before[k] + 4 * which

                def product(n):
                    g = g0 + 4 * (n % 2)
                    ve.wait_ge(turned, 4 * idx + n + 1)
                    nc.vector.tensor_tensor(ptf[:, 512 * n:512 * n + 512].rearrange("p (k c) -> p k c", k=4),
                                            bank[n][:, :].rearrange("p (k c) -> p k c", k=4),
                                            vecT[:, g:g + 4].unsqueeze(2).broadcast_to([P, 4, P]),
                                            ALU.mult).then_inc(taken, 1)

                def lo(n):
                    t, half = n // 2, n % 2
                    piece = (slice(None), slice(4 * half, 4 * half + 4), tok(t))
                    ve.wait_ge(xn_hi, n0 + n + 1)
                    less_hi(xn[1][piece], ptf[:, 512 * n:512 * n + 512].rearrange("p (k c) -> p k c", k=4),
                            xn[0][piece]).then_inc(xn_ready, 1)

                product(0)
                for n in range(4):
                    if n + 1 < 4:
                        product(n + 1)
                    lo(n)

            def add(k):
                last = last_before(k)
                wide_order = ends(k)[1][0] == 1
                through(last + 1 if wide_order else last + 2)
                for n, (t, c) in enumerate(ends(k)):
                    if n == 2:
                        through(last + 2)
                    ve.wait_ge(acc_done, 4 * residuals.index(k) + n + 1)
                    part = h[:, t, 512 * c:512 * c + 512]
                    x = nc.vector.tensor_tensor(part, part, bank[4 + 2 * t + c][:, :], ALU.add)
                    if c == 1:
                        x.then_inc(h_ready, 1)

            nc.vector.memset(gate_bias[:, :], 0.0).then_inc(pads_zero, 1)
            nc.vector.memset(u[:, :, 0:PAD], 0.0).then_inc(pads_zero, 1)
            scale(CONV, h)
            ve.wait_ge(pre_turned, 1)
            nc.vector.tensor_copy(vecT[:, :], bank[4][:, 0:P]).then_inc(pre_copied, 1)
            ve.wait_ge(pre_turned, 2)
            nc.vector.tensor_copy(tapT[:, :, :].rearrange("p k c -> p (k c)"),
                                  bank[5][:, 0:KT * (TAPS + TAPS2)]).then_inc(pre_copied, 1)
            ve.wait_ge(pre_turned, 3)
            nc.vector.tensor_copy(posT[:, :, :].rearrange("p b l -> p (b l)"), bank[6][:, 0:64]).then_inc(pre_copied, 1)
            ve.wait_ge(pre_copied, 3)
            through(2)
            take(CONV)

            def glu_pw1(ft):
                through(chunk_of["pw1"][ft] + 2)
                ve.wait_ge(gate_act, ft + 1)
                b = col["a_pw1_b"] + ft
                nc.vector.scalar_tensor_tensor(
                    out=u[:, ft, PAD:PAD + S], in0=bank[ft % 4][:, 0:S], scalar=vecT[:, b:b + 1],
                    in1=softf[:, S * (ft % 4):S * (ft % 4) + S], op0=ALU.add, op1=ALU.mult).then_inc(glu_done, 1)

            glu_pw1(0)
            glu_pw1(1)
            tasks = [lambda ft=ft: glu_pw1(ft) for ft in range(2, KT)]
            tasks += [lambda j=j: through(chunk_of["pw2"][j]) for j in range(3)]
            ve.wait_ge(glu_done, 2)
            taps_before = 0
            for fts in ((0, 1), (2, 3), (4,)):
                for j in range(TAPS):
                    if j % 4 == 3 and tasks:
                        tasks.pop(0)()
                    for f, ft in enumerate(fts):
                        tap, dst, src = tapT[:, ft, j:j + 1], v[:, ft, :], u[:, ft, j:j + S]
                        b = col["a_dw_b"] + ft
                        if j == 0:
                            ve.wait_ge(glu_done, ft + 1)
                            x = nc.vector.tensor_scalar(dst, src, tap, vecT[:, b:b + 1], ALU.mult, ALU.add)
                        else:
                            ve.wait_ge(conv_link, taps_before + len(fts) * (j - 1) + f + 1)
                            x = nc.vector.scalar_tensor_tensor(out=dst, in0=src, scalar=tap, in1=dst,
                                                               op0=ALU.mult, op1=ALU.add)
                        x.then_inc(conv_dve if j == TAPS - 1 else conv_link, 1)
                taps_before += len(fts) * (TAPS - 1)
            for task in tasks:
                task()

            ve.wait_ge(stat_done, 1)
            for j in range(2):
                part = v[:, 4 * j:4 * j + 4, :]
                nc.vector.tensor_tensor(part, part, bank[0][:, 0:S].unsqueeze(1).broadcast_to([P, 4, S]),
                                        ALU.subtract).then_inc(centred, 1)
            ve.wait_ge(stat_done, 2)
            nc.vector.tensor_scalar(softf[:, 0:S], bank[1][:, 0:S], EPS, None, ALU.add).then_inc(rstd_row, 1)
            ve.wait_ge(std_ready, 1)
            link(nc.vector.reciprocal(softf[:, S:2 * S], softf[:, 0:S]))
            for j in range(2):
                part = v[:, 4 * j:4 * j + 4, :]
                nc.vector.tensor_tensor(part, part, softf[:, S:2 * S].unsqueeze(1).broadcast_to([P, 4, S]),
                                        ALU.mult).then_inc(normed, 1)
            for g in range(4):
                ve.wait_ge(silu_ready, 2 * g + 2)
                part = (slice(None), slice(2 * g, 2 * g + 2))
                nc.vector.tensor_copy(xn[0][part], v[part]).then_inc(silu_hi, 1)
                ve.wait_ge(silu_hi, g + 1)
                less_hi(xn[1][part], v[part], xn[0][part]).then_inc(silu_lo, 1)

            def norm(k):
                add(k)
                scale(k, h)
                through(last_before(k) + 3)
                take(k)

            def glu(which):
                stage = f"ffn{which}"
                for ft in range(FT):
                    through(chunk_of[stage + "_in"][ft] + 2)
                    n, b = UP0[stage] + ft, slice(S * (ft % 4), S * (ft % 4) + S)
                    ve.wait_ge(gate_act, n + 1)
                    nc.vector.tensor_tensor(ptf[:, b], bank[ft % 4][:, S:2 * S], softf[:, b],
                                            ALU.mult).then_inc(glu_done, 1)
                    ve.wait_ge(ffa_hi, FT * which + ft + 1)
                    less_hi(ffa[1][:, ft % 4, :], ptf[:, b], ffa[0][:, ft % 4, :]).then_inc(ffa_ready, 1)

            norm(FFN0)
            glu(0)
            norm(NSA)

            ve.wait_ge(kv_done, 1)
            for b in range(2):
                kv = bank[4][:, S * b:S * b + S].rearrange("p (n l) -> p l n", l=16)
                for part in range(2):
                    ls = slice(16 * part, 16 * part + 16)
                    nc.vector.tensor_tensor(window[:, b, ls, :], kv[:, :, part:part + NCMP],
                                            posT[:, b, ls].unsqueeze(2).broadcast_to([P, 16, NCMP]),
                                            ALU.add).then_inc(window_ready, 1)
            ve.wait_ge(kv_done, 3)
            through(chunk_of["q"][0])
            take(NSA, 1)
            through(chunk_of["q"][2])
            for half in range(2):
                nc.vector.tensor_copy(k2[DH * half:DH * half + DH, 0, :, :].rearrange("p b k -> p (b k)"),
                                      bank[5][0:DH, :]).then_inc(kv_dve, 1)
            nc.vector.tensor_copy(vtok[:, :, :, :].rearrange("p t b c -> p (t b c)"),
                                  bank[6][:, :]).then_inc(kv_dve, 1)
            through(chunk_of["gates"][0] + 2)
            ve.wait_ge(q_ready, 5)
            ve.wait_ge(consts_built, 9)
            link(nc.vector.tensor_scalar(gates[:, 0, 0:HEADS], gates[:, 0, 0:HEADS], valid[:, 0:1], None, ALU.mult))
            gate_of = gates[:, :, :].rearrange("p t (b h) -> p t b h", b=3)

            def nsa_shift(i):
                ve.wait_ge(score_done, i + 1)
                ve.wait_ge(bias_built, i + 1)
                if i >= 2:
                    ve.wait_ge(p_turned, i - 1)
                for n, piece in enumerate(NSA_PIECES):
                    t, branch = n // 3, n % 3
                    if branch == 0:
                        src, bias = bank[i % 2][:, piece], biases[:, i, 3 * P + 16 * t:3 * P + 16 * t + NCMP]
                    elif t == 0:
                        src, bias = bank[i % 2][:, piece], biases[:, i, 0:P]
                    else:
                        src, bias = bank[2 + i % 2][:, S * (branch - 1):S * branch], biases[:, i, P:3 * P]
                    x = nc.vector.tensor_tensor_reduce(out=soft[:, i % 2, piece], in0=src, in1=bias,
                                                       scale=-DH ** -0.5, scalar=3e38, op0=ALU.add, op1=ALU.min,
                                                       accum_out=nmax[:, i % 2, n:n + 1])
                x.then_inc(shifted, 1)

            def nsa_weigh(i):
                ve.wait_ge(exp_done, i + 1)
                b = i % 2
                link(nc.vector.reciprocal(rcol[:, 0, 0:6], rsum[:, b, :]))
                link(nc.vector.tensor_tensor(coef[:, b, :].rearrange("p (t n) -> p t n", t=TT),
                                             rcol[:, 0, 0:6].rearrange("p (t n) -> p t n", t=TT),
                                             gate_of[:, :, :, i], ALU.mult))
                for n, piece in enumerate(NSA_PIECES):
                    x = nc.vector.tensor_scalar(soft[:, b, piece], soft[:, b, piece], coef[:, b, n:n + 1],
                                                None, ALU.mult)
                x.then_inc(weighed, 1)

            def nsa_evac(i):
                ve.wait_ge(p_turned, i + 1)
                if i >= 2:
                    ve.wait_ge(pv_done, i - 1)
                nc.vector.tensor_copy(pt[:, i % 2, 0:384], bank[4][:, 0:384])
                nc.vector.tensor_copy(pt[0:NCMP, i % 2, 768:768 + P], bank[4][0:NCMP, 384:512]).then_inc(pt_dve, 1)

            def nsa_out(ft):
                ve.wait_ge(o_hi, ft + 1)
                less_hi(xn[1][:, ft, :], bank[6 + ft % 2][:, 0:S], xn[0][:, ft, :]).then_inc(o_ready, 1)

            nsa_shift(0)
            through(chunk_of["gates"][0] + 3)
            for i in range(HEADS):
                if i + 1 < HEADS:
                    nsa_shift(i + 1)
                nsa_weigh(i)
                nsa_evac(i)
                if i % 2 == 0 and i:
                    nsa_out(i // 2 - 1)
            nsa_out(HEADS // 2 - 1)

            norm(FFN1)
            glu(1)
            add(MID)
            ve.wait_ge(gains_loaded, 32)
            for t in range(TT):
                ve.wait_ge(rstd_ready, TT * MID + t + 1)
                nc.vector.scalar_tensor_tensor(out=h[:, t, :], in0=h[:, t, :],
                                               scalar=rstd[:, TT * MID + t:TT * MID + t + 1], in1=gain_row[:, :],
                                               op0=ALU.mult, op1=ALU.mult).then_inc(h_ready, 1)
            scale(IN2, h)
            through(last_before(MID) + 3)
            take(IN2)
            scale(MEM, memraw)
            before = links[0]
            for group in range(2):
                through(chunk_of["ml_qk"][2 * group + 1] + 2)
                ve.wait_ge(in2_act, 2 * group + 2)
                for j in range(TAPS2):
                    for f in range(4):
                        ft = 4 * group + f
                        src = u[:, ft, PAD - TAPS2 + 1 + j:PAD - TAPS2 + 1 + j + S]
                        tap = tapT[:, ft, TAPS + j:TAPS + j + 1]
                        if j == 0:
                            b = col["ml_conv_b_2"] + ft
                            x = nc.vector.tensor_scalar(v[:, ft, :], src, tap, vecT[:, b:b + 1], ALU.mult, ALU.add)
                        else:
                            ve.wait_ge(dve_link, before + 12 * group + 4 * (j - 1) + f + 1)
                            x = nc.vector.scalar_tensor_tensor(out=v[:, ft, :], in0=src, scalar=tap, in1=v[:, ft, :],
                                                               op0=ALU.mult, op1=ALU.add)
                        x.then_inc(conv4_done if j == TAPS2 - 1 else dve_link, 1)
            links[0] = before + 24
            through(chunk_of["ml_v"][1] + 2)
            ve.wait_ge(in2_done, 5)
            for t in range(TT):
                nc.vector.memset(mlv[:, t, :, MLD:MLV], 1.0)
                nc.vector.tensor_copy(mlv[:, t, :, 0:MLD],
                                      bank[4 + t][:, :].rearrange("p (h c) -> p h c", h=MLH)).then_inc(in2_dve, 1)

            through(chunk_of["ml_o"][1] + 2)
            ve.wait_ge(in2_act, 6)
            for t in range(TT):
                nc.vector.tensor_tensor(mlo[:, t, :], mlo[:, t, :], gain_ml[:, :], ALU.mult)
            through(chunk_of["fx_v"][1] + 2)
            ve.wait_ge(in2_done, 11)
            for t in range(TT):
                nc.vector.tensor_copy(fxv[:, t, :], bank[4 + t][:, :]).then_inc(in2_dve, 1)
            through(chunk_of["rows"][0] + 2)
            ve.wait_ge(in2_done, 12)
            nc.vector.tensor_copy(gtok[:, :, :].rearrange("p t c -> p (t c)"), bank[6][:, 0:32]).then_inc(gates_copied, 1)
            through(chunk_of["rows"][0] + 3)
            take(MEM)

            ve.wait_ge(in2_done, 13)
            ve.wait_ge(small_loaded, 16 * 8)
            for b in range(2):
                x = nc.vector.tensor_scalar(row[:, b, :], bank[6][0:FXH, S * b:S * b + S], gate_bias[:, b:b + 1],
                                            None, ALU.add)
            link(x)
            nc.vector.scalar_tensor_tensor(out=row[:, 2:4, :], in0=row[:, 0:2, :], scalar=-1.0, in1=row[:, 0:2, :],
                                           op0=ALU.mult, op1=ALU.min).then_inc(rows_done, 1)
            through(chunk_of["xkv_k"][3])
            ve.wait_ge(act_link, 1)
            nc.vector.tensor_scalar(row[:, 4:6, :], row[:, 2:4, :], 1.0, None, ALU.add).then_inc(rows_done, 1)
            ve.wait_ge(act_link, 2)
            link(nc.vector.scalar_tensor_tensor(out=row[:, 4:6, :], in0=row[:, 4:6, :], scalar=1.0,
                                                in1=row[:, 2:4, :], op0=ALU.subtract, op1=ALU.subtract))
            link(nc.vector.tensor_tensor(row[:, 6:8, :], row[:, 6:8, :], row[:, 4:6, :], ALU.subtract))
            link(nc.vector.scalar_tensor_tensor(out=row[:, 2:4, :], in0=row[:, 0:2, :], scalar=0.0,
                                                in1=row[:, 6:8, :], op0=ALU.min, op1=ALU.subtract))
            one = ones[0:FXH, 0:1].broadcast_to([FXH, S])
            for b in range(2):
                x = nc.vector.tensor_tensor_scan(row[:, 4 + b, :], one, row[:, 2 + b, :], 0.0, ALU.mult, ALU.add)
            link(x)
            nc.vector.tensor_scalar(row[:, 0, :], row[:, 4, :], -float(DH) ** 0.5, None, ALU.mult)
            link(nc.vector.scalar_tensor_tensor(out=row[:, 1, :], in0=bank[7][0:FXH, 0:S], scalar=gate_bias[:, 2:3],
                                                in1=row[:, 5, :], op0=ALU.add, op1=ALU.subtract))
            link(nc.vector.tensor_tensor_scan(row[:, 6, :], one, row[:, 1, :], 0.0, ALU.mult, ALU.max))
            nc.vector.tensor_scalar(row[:, 7, :], row[:, 6, :], -1.0, None, ALU.mult)
            nc.vector.scalar_tensor_tensor(out=row[:, 2, :], in0=row[:, 5, :], scalar=-1.0, in1=row[:, 6, :],
                                           op0=ALU.mult, op1=ALU.subtract).then_inc(rows_done, 1)
            through(chunk_of["xkv_v"][3] + 2)
            ve.wait_ge(cols_turned, 1)
            nc.vector.tensor_copy(rcol[:, :, :], bank[7][:, 0:16].rearrange("p (t n) -> p t n", t=TT)
                                  ).then_inc(rows_done, 1)

            def ml_shifted(i):
                ve.wait_ge(ml_score, i + 1)
                ve.wait_ge(consts_built, 9)
                w, m = soft[:, i % 2, :], bank[1 + 2 * (i % 2)]
                nc.vector.tensor_tensor(w[:, 0:S], m[:, 0:S], causalT[:, 0:S], ALU.add)
                nc.vector.tensor_tensor(w[:, S:3 * P], m[:, P:S], causalT[:, S:3 * P], ALU.add).then_inc(ml_shift, 1)

            def ml_weighed(i):
                ve.wait_ge(ml_exp, i + 1)
                if i >= 2:
                    ve.wait_ge(ml_num, i - 1)
                nc.vector.scalar_tensor_tensor(out=pt[:, i % 2, 0:3 * P], in0=bank[2 * (i % 2)][:, 0:3 * P],
                                               scalar=MLD ** -0.5, in1=soft[:, i % 2, 0:3 * P],
                                               op0=ALU.mult, op1=ALU.mult).then_inc(ml_weight, 1)

            numv = num.rearrange("p (t h) c -> p t h c", t=TT)

            def ml_take(i):
                ve.wait_ge(ml_num, i + 1)
                nc.vector.tensor_copy(numv[:, :, i, :], bank[4 + i % 2][:, 0:TT * MLV]
                                      .rearrange("p (t c) -> p t c", t=TT)).then_inc(ml_copied, 1)

            through(chunk_of["out2"][2])
            ml_shifted(0)
            for i in range(MLH):
                if i + 1 < MLH:
                    ml_shifted(i + 1)
                ml_weighed(i)
                if i:
                    ml_take(i - 1)
            ml_take(MLH - 1)
            ve.wait_ge(act_link, 3)
            ve.wait_ge(ml_copied, MLH)
            d = num[:, :, MLD]
            link(nc.vector.scalar_tensor_tensor(out=den[:, 0, :], in0=d, scalar=-1.0, in1=d, op0=ALU.mult, op1=ALU.max))
            link(nc.vector.tensor_tensor(den[:, 1, :].rearrange("p (t h) -> p t h", t=TT),
                                         den[:, 0, :].rearrange("p (t h) -> p t h", t=TT),
                                         expm[:, :, 0:MLH], ALU.max))
            link(nc.vector.reciprocal(den[:, 2, :], den[:, 1, :]))
            nc.vector.tensor_tensor(num[:, :, 0:MLD], num[:, :, 0:MLD],
                                    den[:, 2, :].unsqueeze(2).broadcast_to([P, 8, MLD]), ALU.mult
                                    ).then_inc(ml_copied, 1)

            def fx_shift(i):
                n = HEADS + i
                ve.wait_ge(score_done, n + 1)
                if i >= 2:
                    ve.wait_ge(p_turned, n - 1)
                s, b = soft[:, i % 2, :], bank[2 * (i % 2)]
                nc.vector.tensor_tensor_reduce(out=s[:, 0:P], in0=b[:, 0:P], in1=causal[:, 0:P],
                                               scale=-DH ** -0.5, scalar=3e38, op0=ALU.add, op1=ALU.min,
                                               accum_out=nmax[:, i % 2, 0:1])
                nc.vector.tensor_tensor_reduce(out=s[:, P:3 * P], in0=b[:, P:3 * P], in1=causal[:, P:3 * P],
                                               scale=-DH ** -0.5, scalar=3e38, op0=ALU.add, op1=ALU.min,
                                               accum_out=nmax[:, i % 2, 1:2]).then_inc(shifted, 1)

            def row_weigh(n, i, pieces):
                ve.wait_ge(exp_done, n + 1)
                link(nc.vector.reciprocal(coef[:, i % 2, 0:2], rsum[:, i % 2, 0:2]))
                for t, piece in enumerate(pieces):
                    x = nc.vector.tensor_scalar(soft[:, i % 2, piece], soft[:, i % 2, piece],
                                                coef[:, i % 2, t:t + 1], None, ALU.mult)
                x.then_inc(weighed, 1)

            def fx_out(j):
                ve.wait_ge(o_hi, HEADS // 2 + j + 1)
                less_hi(xn[1][:, 4 + j, :], bank[1 + 2 * (j % 2)][:, 0:S], xn[0][:, 4 + j, :]).then_inc(o_ready, 1)

            fx_shift(0)
            for i in range(FXH):
                if i + 1 < FXH:
                    fx_shift(i + 1)
                row_weigh(HEADS + i, i, (slice(0, P), slice(P, 3 * P)))
                if i % 2 == 0 and i:
                    fx_out(i // 2 - 1)
                if i == 1:
                    ve.wait_ge(act_link, 4)
                    nc.vector.tensor_reduce(den[:, 3, :], mlsq, AX.X, ALU.add).then_inc(ml_sq, 1)
                if i == 4:
                    ve.wait_ge(ml_rstd, 1)
                    link(nc.vector.tensor_tensor(num[:, :, 0:MLD], num[:, :, 0:MLD],
                                                 den[:, 5, :].unsqueeze(2).broadcast_to([P, 8, MLD]), ALU.mult))
                    for t in range(TT):
                        nc.vector.tensor_tensor(numv[:, t, :, 0:MLD], numv[:, t, :, 0:MLD],
                                                mlo[:, t, :].rearrange("p (h c) -> p h c", h=MLH),
                                                ALU.mult).then_inc(ml_out, 1)
            fx_out(FXH // 2 - 1)
            for t in range(TT):
                ve.wait_ge(o_hi, HEADS // 2 + FXH // 2 + t + 1)
                less_hi(xn[1][:, 0:MLH, tok(t)], bank[4 + t][:, :].rearrange("p (h c) -> p h c", h=MLH),
                        xn[0][:, 0:MLH, tok(t)]).then_inc(ml_ready, 1)

            norm(CROSS)
            through(chunk_of["xo"][2])

            def x_shift(i):
                ve.wait_ge(score_done, HEADS + FXH + i + 1)
                link(nc.vector.tensor_reduce(nmax[:, i % 2, 0:2], bank[4 + i % 2][:, :]
                                             .rearrange("p (t m) -> p t m", t=TT), AX.X, ALU.max, negate=True))
                nc.vector.tensor_scalar(nmax[:, i % 2, 2:4], nmax[:, i % 2, 0:2], XSCALE, None,
                                        ALU.mult).then_inc(shifted, 1)

            def x_out(i):
                ve.wait_ge(o_hi, HEADS // 2 + FXH // 2 + TT + i + 1)
                less_hi(xn[1][:, 2 * i:2 * i + 2, :].rearrange("p f t -> p (f t)"), bank[i][:, :],
                        xn[0][:, 2 * i:2 * i + 2, :].rearrange("p f t -> p (f t)")).then_inc(o_ready, 1)

            x_shift(0)
            for i in range(XH):
                if i + 1 < XH:
                    x_shift(i + 1)
                row_weigh(HEADS + FXH + i, i, (slice(0, S), slice(S, 2 * S)))
                if i:
                    x_out(i - 1)
            x_out(XH - 1)

            norm(FF)
            for g in range(D_FF // S):
                through(chunk_of["ff_in"][g] + 2)
                n, b = UP0["ff"] + g, slice(512 * (g % 4), 512 * (g % 4) + 512)
                ve.wait_ge(gate_act, n + 1)
                nc.vector.scalar_tensor_tensor(out=ptf[:, b], in0=bank[g % 4][:, :], scalar=0.0,
                                               in1=softf[:, 512 * (g % 3):512 * (g % 3) + 512],
                                               op0=ALU.max, op1=ALU.mult).then_inc(glu_done, 1)
                f = (slice(None), slice(2 * (g % 2), 2 * (g % 2) + 2))
                ve.wait_ge(ffa_hi, 2 * FT + g + 1)
                less_hi(ffa[1][f].rearrange("p f t -> p (f t)"), ptf[:, b],
                        ffa[0][f].rearrange("p f t -> p (f t)")).then_inc(ffa_ready, 1)
            add(LAST)
            ve.wait_ge(last_gain_loaded, 16)
            for t in range(TT):
                ve.wait_ge(rstd_ready, TT * LAST + t + 1)
                nc.vector.scalar_tensor_tensor(out=scaled[:, t, :], in0=h[:, t, :],
                                               scalar=rstd[:, TT * LAST + t:TT * LAST + t + 1], in1=gain_row[:, :],
                                               op0=ALU.mult, op1=ALU.mult).then_inc(out_ready, 1)

        @block.tensor
        def _(te):
            mm = nc.tensor.matmul

            turn_of = [0]

            def weights(stage, n, k, unsplit=False):
                c = chunk_of[stage][n]
                assert c == turn_of[0]
                turn_of[0] += 1
                if not is_split[c]:
                    te.wait_ge(raw_loaded[c % RAWS], loads_through(c))
                    return c, raw[c % RAWS]
                te.wait_ge(split_lo, nth[c] + 1)
                return c, [kn(s, used_cols[c] // k, k) for s in split_slot[nth[c] % SPLITS]]

            def used(c, x):
                x.then_inc(freed[c][0], 1)

            def mm3(dst, left, right, start, stop):
                mm(dst, left[0], right[0], start=start, stop=False)
                mm(dst, left[0], right[1], start=False, stop=False)
                return mm(dst, left[1], right[0], start=False, stop=stop)

            def part(pair, *index):
                return [x[index] for x in pair]

            ALL = slice(None)

            def turn(k):
                idx = turning.index(k)
                for t in range(TT):
                    te.wait_ge(scaled_ready, TT * idx + t + 1)
                    for half in range(2):
                        for q in range(4):
                            x = nc.tensor.transpose(bank[2 * t + half][:, P * q:P * q + P],
                                                    scaled[:, t, P * (4 * half + q):P * (4 * half + q) + P],
                                                    ident[:, :])
                        x.then_inc(turned, 1)

            def features(dst, w, c0):
                for kt in range(KT):
                    x = mm3(dst, part(w, ALL, kt, slice(c0, c0 + P)), part(xn, ALL, kt, ALL),
                            kt == 0, kt == KT - 1)
                return x

            def tokens(dst, w, cols, t, k0=0, k1=KT, first=True):
                for kt in range(k0, k1):
                    x = mm3(dst, part(xn, ALL, kt, tok(t)), part(w, ALL, kt - k0, cols),
                            kt == 0 and first, kt == KT - 1)
                return x

            def feature_pair(stage, n, b, before=None):
                c, w = weights(stage, n, KT)
                if before:
                    te.wait_ge(*before)
                for j in range(2):
                    x = features(bank[b][:, S * j:S * j + S], w, P * j)
                used(c, x)

            def by_token(stage, n, b0, b1, each=None):
                for half in range(2):
                    c, w = weights(stage, n + half, 4)
                    for t, b in enumerate((b0, b1)):
                        x = tokens(bank[b][:, :], w, ALL, t, 4 * half, 4 * half + 4)
                        if half and each:
                            x.then_inc(each, 1)
                    if not (half and each):
                        used(c, x)

            def residual_product(stage, bias=False, ready=None):
                for col_half in range(2):
                    for half in range(2):
                        c, w = weights(stage, 2 * col_half + half, 4)
                        if col_half == 0 and ready:
                            te.wait_ge(*ready[half])
                        for t in range(TT):
                            dst = bank[4 + 2 * t + col_half][:, :]
                            if bias and half == 0:
                                mm(dst, ones[0:1, :], pw2_row[0:1, 512 * col_half:512 * col_half + 512],
                                   start=True, stop=False)
                            x = tokens(dst, w, ALL, t, 4 * half, 4 * half + 4, first=not bias)
                            if half:
                                x.then_inc(acc_done, 1)
                        if half == 0:
                            used(c, x)

            def down(stage, g, count, ready):
                c, w = weights(stage, g, 2)
                te.wait_ge(ffa_ready, ready)
                for t in range(TT):
                    for half in range(2):
                        for q in range(2):
                            kt = 2 * g + q
                            x = mm3(bank[4 + 2 * t + half][:, :], part(ffa, ALL, kt % 4, tok(t)),
                                    part(w, ALL, q, slice(512 * half, 512 * half + 512)),
                                    kt == 0, kt == count - 1)
                        if kt == count - 1:
                            x.then_inc(acc_done, 1)
                if 2 * g + 2 < count:
                    used(c, x)

            te.wait_ge(consts_built, 1)
            turn(CONV)
            te.wait_ge(vecs_loaded, 16 * len(act_loads))
            te.wait_ge(vecs_loaded_pool, 16 * len(pool_loads))
            nc.tensor.transpose(bank[4][:, 0:P], vecs, ident[:, :]).then_inc(pre_turned, 1)
            m = TAPS + TAPS2
            for k in range(KT):
                x = nc.tensor.transpose(bank[5][:, m * k:m * k + m], taps[:, P * k:P * k + P], ident[0:m, 0:m])
            x.then_inc(pre_turned, 1)
            for b in range(2):
                x = nc.tensor.transpose(bank[6][:, 32 * b:32 * b + 32], pos[:, P * b:P * b + P], ident[0:32, 0:32])
            x.then_inc(pre_turned, 1)
            te.wait_ge(xn_ready, xn_count(CONV))
            for ft in range(KT):
                feature_pair("pw1", ft, ft % 4, (glu_done, ft - 3) if ft >= 4 else None)

            def mean(ft, dst, src, stage):
                x = mm(dst, mean_w[:, :], src, start=ft == 0, stop=ft == KT - 1)
                if ft == KT - 1:
                    x.then_inc(stat_done, 1)

            for ft in range(CONV_DVE, KT):
                n = ft - CONV_DVE
                te.wait_ge(glu_done, ft + 1)
                te.wait_ge(pads_zero, 2)
                for j in range(TAPS):
                    g = 4 * n + j // TAPG
                    if j % TAPG == 0:
                        te.wait_ge(diag_built, g + 1)
                    x = mm(bank[4 + n][:, 0:S], diag[:, g % NDIAG, j % TAPG, :], u[:, ft, j:j + S],
                           start=j == 0, stop=j == TAPS - 1)
                    if j % TAPG == TAPG - 1 or j == TAPS - 1:
                        x.then_inc(diag_used, 1)
            te.wait_ge(glu_done, KT)
            for n in range(KT - CONV_DVE):
                te.wait_ge(conv_out, n + 1)
                mm(bank[0][:, 0:S], mean_w[:, :], v[:, CONV_DVE + n, :], start=n == 0, stop=False)
            for ft in range(CONV_DVE):
                te.wait_ge(conv_dve, ft + 1)
                x = mm(bank[0][:, 0:S], mean_w[:, :], v[:, ft, :], start=False, stop=ft == CONV_DVE - 1)
            x.then_inc(stat_done, 1)
            for ft in range(KT):
                te.wait_ge(squared, ft // 4 + 1)
                x = mm(bank[1][:, 0:S], mean_w[:, :], actf[:, S * ft:S * ft + S], start=ft == 0, stop=ft == KT - 1)
            x.then_inc(stat_done, 1)
            te.wait_ge(small_loaded, 16 * 8)
            residual_product("pw2", bias=True, ready=[(silu_lo, 2), (silu_lo, 4)])

            def ffn(k, which):
                stage = f"ffn{which}"
                turn(k)
                te.wait_ge(xn_ready, xn_count(k))
                for g in range(FC + 1):
                    if g < FC:
                        for ft in (2 * g, 2 * g + 1):
                            feature_pair(stage + "_in", ft, ft % 4,
                                         (glu_done, UP0[stage] + ft - 3) if ft >= 4 else None)
                    if g:
                        down(stage + "_out", g - 1, FT, FT * which + 2 * g)

            ffn(FFN0, 0)

            turn(NSA)
            te.wait_ge(xn_ready, xn_count(NSA, 0))
            feature_pair("kv", 0, 4)
            for n in range(2):
                c, w = weights("kv", 1 + n, KT)
                features(bank[5][:, S * n:S * n + S], w, 0)
                for t in range(TT):
                    x = tokens(bank[6][:, S * t + P * n:S * t + P * n + P], w, slice(P, 2 * P), t)
                used(c, x)
            te.wait_ge(window_ready, 4)
            for b in range(2):
                c, w = weights("phi", b, 1)
                w = w[:, :].rearrange("p (l e) -> p l e", e=DH)
                for g in range(GROUPS):
                    half = slice(DH * g, DH * g + DH)
                    for l in range(32):
                        x = mm(bank[7][half, 16 * b:16 * b + NCMP], w[half, l, :], window[half, b, l, :],
                               start=l == 0, stop=l == 31)
                used(c, x)
            te.wait_ge(xn_ready, xn_count(NSA, 1))
            for b in range(4):
                feature_pair("q", b, b)
            c, w = weights("gates", 0, KT)
            for t in range(TT):
                x = tokens(bank[4][:, 48 * t:48 * t + 48], w, ALL, t)
            used(c, x)
            te.wait_ge(kv_act, 3)
            te.wait_ge(small_loaded, 16 * 8)
            te.wait_ge(kv_dve, 3)
            for g in range(GROUPS):
                half = slice(DH * g, DH * g + DH)
                for e in range(2):
                    mm(bank[7 - g][DH * e:DH * e + DH, 64:64 + NCMP], phi2[half, 0, :],
                       hid[half, 0, :], start=True, stop=True)
                x = mm(bank[7 - g][0:NCMP, P:P + DH], hid[half, 1, :], phi2[half, 1, :], start=True, stop=True)
            x.then_inc(phi_done, 1)

            def nsa_score(i):
                if i >= 2:
                    te.wait_ge(shifted, i - 1)
                e, g = slice(DH * (i % 2), DH * (i % 2) + DH), i // (HEADS // GROUPS)
                x, y = bank[i % 2], bank[2 + i % 2]
                q0, q1 = qT[e, i // 2, 0:P], qT[e, i // 2, P:S]
                mm(x[:, 0:2 * P], q0, k2[e, g, :, 0:P], start=True, stop=True)
                mm(x[:, 256:271], q0, kcmp[e, g, :], start=True, stop=True)
                mm(x[:, 272:287], q1, kcmp[e, g, :], start=True, stop=True)
                mm(y[:, :], q1, k2[e, g, :, :].rearrange("p b k -> p (b k)"), start=True,
                   stop=True).then_inc(score_done, 1)

            def nsa_turn(i):
                te.wait_ge(weighed, i + 1)
                if i:
                    te.wait_ge(pt_dve, i)
                    te.wait_ge(pt_act, i)
                s = soft[:, i % 2, :]
                turns = [(4, 0, 0), (4, P, 288), (4, 2 * P, 416), (5, 0, 128), (5, P, 544), (5, 2 * P, 672)]
                for b, at, src in turns:
                    nc.tensor.transpose(bank[b][:, at:at + P], s[:, src:src + P], ident[:, :])
                for t in range(TT):
                    x = nc.tensor.transpose(bank[4 + t][0:NCMP, 384:512],
                                            s[:, 256 + 16 * t:256 + 16 * t + NCMP], ident[:, :])
                x.then_inc(p_turned, 1)

            def nsa_pv(i):
                te.wait_ge(pt_dve, i + 1)
                te.wait_ge(pt_act, i + 1)
                ft, g = i // 2, i // (HEADS // GROUPS)
                if i % 2 == 0 and ft >= 2:
                    te.wait_ge(o_ready, ft - 1)
                dst = bank[6 + ft % 2][DH * (i % 2):DH * (i % 2) + DH, 0:S]
                d = slice(DH * g, DH * g + DH)
                for b in range(2):
                    mm(dst, vtok[:, 0, b, d], pt[:, i % 2, 384 * b:384 * b + S], start=b == 0, stop=False)
                    mm(dst[:, P:S], vtok[:, 1, b, d], pt[:, i % 2, 384 * b + S:384 * b + 384], start=False, stop=False)
                mm(dst, vcmp[:, d], pt[0:NCMP, i % 2, 768:1024], start=False, stop=True).then_inc(pv_done, 1)

            te.wait_ge(q_ready, 5)
            te.wait_ge(kv_act, 5)
            te.wait_ge(kv_dve, 3)
            nsa_score(0)
            nsa_score(1)
            for i in range(HEADS):
                nsa_turn(i)
                if i + 2 < HEADS:
                    nsa_score(i + 2)
                nsa_pv(i)
            te.wait_ge(o_ready, HEADS // 2)
            residual_product("b_out")

            ffn(FFN1, 1)

            turn(IN2)
            te.wait_ge(xn_ready, xn_count(IN2))
            for b in range(4):
                feature_pair("ml_qk", b, b)
            by_token("ml_v", 0, 4, 5)
            by_token("ml_o", 0, 6, 7)
            for b in range(4):
                feature_pair("fx_q" if b < 2 else "fx_k", b % 2, b, (in2_act, b + 1))
            te.wait_ge(in2_dve, 2)
            by_token("fx_v", 0, 4, 5)
            te.wait_ge(in2_act, 6)
            c, w = weights("rows", 0, KT)
            for t in range(TT):
                x = tokens(bank[6][:, 16 * t:16 * t + 16], w, ALL, t)
            used(c, x)
            te.wait_ge(in2_act, 10)
            turn(MEM)
            te.wait_ge(gates_copied, 1)
            for dst, c0 in ((bank[6][0:FXH, 0:S], 8), (bank[6][0:FXH, S:2 * S], 4), (bank[7][0:FXH, 0:S], 0)):
                for t in range(TT):
                    x = nc.tensor.transpose(dst[:, tok(t)], gtok[:, t, c0:c0 + 8], ident[:, :])
            x.then_inc(in2_done, 1)
            te.wait_ge(xn_ready, xn_count(MEM))
            te.wait_ge(in2_dve, 4)
            for b in range(4):
                feature_pair("xkv_k", b, XKV_BANK[b])
            for half in range(2):
                if half:
                    te.wait_ge(xkv_act, 2)
                by_token("xkv_v", 2 * half, XKV_BANK[4 + 2 * half], XKV_BANK[5 + 2 * half], each=xkv_done)
            te.wait_ge(rows_done, 3)
            for b, r in enumerate((1, 2)):
                for t in range(TT):
                    x = nc.tensor.transpose(bank[7][:, 16 * b + 8 * t:16 * b + 8 * t + 8], row[:, r, tok(t)],
                                            ident[0:FXH, 0:FXH])
            x.then_inc(cols_turned, 1)

            def all_rows(i):
                return ident[0:FXH, i:i + 1].broadcast_to([FXH, P])

            def mlstm_score(i):
                if i >= 2:
                    te.wait_ge(ml_weight, i - 1)
                s, m = bank[2 * (i % 2)], bank[1 + 2 * (i % 2)]
                mm(m[:, 0:S], all_rows(i), row[:, 7, :], start=True, stop=True)
                mm(s[:, 0:S], v[:, 4 + i, 0:P], v[:, i, :], start=True, stop=True)
                mm(s[:, S:3 * P], v[:, 4 + i, P:S], v[:, i, P:S], start=True, stop=True).then_inc(ml_score, 1)

            def mlstm_pv(i):
                te.wait_ge(ml_weight, i + 1)
                if i >= 2:
                    te.wait_ge(ml_copied, i - 1)
                dst, p = bank[4 + i % 2], pt[:, i % 2, :]
                mm(dst[:, 0:MLV], p[:, 0:P], mlv[:, 0, i, :], start=True, stop=True)
                mm(dst[:, MLV:2 * MLV], p[:, P:S], mlv[:, 0, i, :], start=True, stop=False)
                mm(dst[:, MLV:2 * MLV], p[:, S:3 * P], mlv[:, 1, i, :], start=False, stop=True).then_inc(ml_num, 1)

            te.wait_ge(xkv_act, 8)
            te.wait_ge(qk_ready, KT)
            mlstm_score(0)
            mlstm_score(1)
            for i in range(MLH):
                mlstm_pv(i)
                if i + 2 < MLH:
                    mlstm_score(i + 2)

            def fx_score(i):
                n = HEADS + i
                if i < 2:
                    te.wait_ge(ml_weight, MLH)
                else:
                    te.wait_ge(shifted, n - 1)
                e, j = slice(DH * (i % 2), DH * (i % 2) + DH), i // 2
                s = bank[2 * (i % 2)]
                for t, cols, keys in ((0, slice(0, P), slice(0, P)), (1, slice(P, 3 * P), slice(0, S))):
                    mm(s[:, cols], qT[e, j, tok(t)], qT[e, 4 + j, keys], start=True, stop=False)
                    x = mm(s[:, cols], all_rows(i), row[:, 0, keys], start=False, stop=True)
                x.then_inc(score_done, 1)

            def fx_turn(i):
                n = HEADS + i
                te.wait_ge(weighed, n + 1)
                if i >= 2:
                    te.wait_ge(pt_act, n - 1)
                else:
                    te.wait_ge(act_link, 3)
                    te.wait_ge(rows_done, 4)
                for q in range(3):
                    x = nc.tensor.transpose(bank[6 + i % 2][:, P * q:P * q + P],
                                            soft[:, i % 2, P * q:P * q + P], ident[:, :])
                x.then_inc(p_turned, 1)

            def fx_pv(i):
                n, j = HEADS + i, i // 2
                te.wait_ge(pt_act, n + 1)
                if i % 2 == 0 and j >= 2:
                    te.wait_ge(o_ready, HEADS // 2 + j - 1)
                dst = bank[1 + 2 * (j % 2)][DH * (i % 2):DH * (i % 2) + DH, :]
                d = slice(DH * i, DH * i + DH)
                mm(dst[:, 0:S], fxv[:, 0, d], pt[:, i % 2, 0:S], start=True, stop=False)
                mm(dst[:, P:S], fxv[:, 1, d], pt[:, i % 2, S:3 * P], start=False, stop=True).then_inc(pv_done, 1)

            fx_score(0)
            fx_score(1)
            for i in range(FXH):
                fx_turn(i)
                if i + 2 < FXH:
                    fx_score(i + 2)
                fx_pv(i)
            te.wait_ge(ml_out, TT)
            for t in range(TT):
                for i in range(MLH):
                    x = nc.tensor.transpose(bank[4 + t][:, P * i:P * i + P], num[:, MLH * t + i, 0:MLD], ident[:, :])
                x.then_inc(ml_turned, 1)
            te.wait_ge(ml_ready, TT)
            te.wait_ge(o_ready, HEADS // 2 + FXH // 2)
            residual_product("out2")

            turn(CROSS)
            te.wait_ge(xn_ready, xn_count(CROSS))
            for b in range(4):
                feature_pair("xq", b, b)

            def x_score(i):
                if i >= 2:
                    te.wait_ge(exp_done, HEADS + FXH + i - 1)
                for t in range(TT):
                    for k in range(2):
                        x = mm(bank[4 + i % 2][:, S * t:S * t + S], qT[:, 2 * i + k, tok(t)],
                               memk[:, 2 * i + k, :], start=k == 0, stop=k == 1)
                x.then_inc(score_done, 1)

            def x_turn(i):
                n = HEADS + FXH + i
                te.wait_ge(weighed, n + 1)
                if i >= 2:
                    te.wait_ge(pt_act, n - 1)
                for k in range(2):
                    for t in range(TT):
                        x = nc.tensor.transpose(bank[6 + i % 2][:, S * k + P * t:S * k + P * t + P],
                                                soft[:, i % 2, S * t + P * k:S * t + P * k + P], ident[:, :])
                x.then_inc(p_turned, 1)

            def x_pv(i):
                te.wait_ge(pt_act, HEADS + FXH + i + 1)
                for half in range(2):
                    at = S * i + P * half
                    for k in range(2):
                        x = mm(bank[i][:, S * half:S * half + S], memv[:, k, at:at + P],
                               pt[:, i % 2, S * k:S * k + S], start=k == 0, stop=k == 1)
                x.then_inc(pv_done, 1)

            te.wait_ge(q_ready, 9)
            x_score(0)
            x_score(1)
            for i in range(XH):
                x_turn(i)
                if i + 2 < XH:
                    x_score(i + 2)
                x_pv(i)
            te.wait_ge(o_ready, HEADS // 2 + FXH // 2 + XH)
            residual_product("xo")

            turn(FF)
            te.wait_ge(xn_ready, xn_count(FF))
            for g in range(D_FF // S + 1):
                if g < D_FF // S:
                    feature_pair("ff_in", g, g % 4, (glu_done, UP0["ff"] + g - 3) if g >= 4 else None)
                if g:
                    down("ff_out", g - 1, D_FF // P, 2 * FT + g)



_INS = ["x", "a_norm", "a_pw1_w", "a_pw1_b", "a_dw_w", "a_dw_b", "a_ln_g", "a_ln_b", "a_pw2_w", "a_pw2_b",
        "kv_norm", "w_kv", "cmp_pos_k", "cmp_pos_v", "phi_k_w1", "phi_k_w2", "phi_v_w1", "phi_v_w2", "b_norm",
        "b_w_in", "b_w_out", "ffn_norm", "ffn_w_in", "ffn_w_out", "final_norm", "mem_2", "ln1_2", "w_in_2",
        "ml_conv_w_2", "ml_conv_b_2", "ml_b_i_2", "ml_b_f_2", "ml_norm_2", "fx_b_f_2", "w_out_2", "ln_x_2",
        "ln_mem_2", "w_xq_2", "w_xkv_2", "w_xo_2", "ln2_2", "w_ff1_2", "w_ff2_2", "ln_f_2"]


def kernel(**inputs):
    import numpy as np
    import concourse.bacc as bacc
    from concourse.bass_utils import run_bass_kernel_spmd

    nc = bacc.Bacc("TRN2", target_bir_lowering=False, num_devices=1)
    arrays, aps = {}, {}
    for name in _INS:
        arrays[f"in_{name}"] = np.ascontiguousarray(inputs[name])
        aps[name] = nc.dram_tensor(f"in_{name}", arrays[f"in_{name}"].shape, F32, kind="ExternalInput").ap()
    out = nc.dram_tensor("out", (1, S, D), F32, kind="ExternalOutput").ap()
    build_kernel(nc, aps, out)
    result = run_bass_kernel_spmd(nc, [arrays], core_ids=[0])
    return result.results[0]["out"]
```

```python
from contextlib import ExitStack

import concourse.bass as bass
from concourse import mybir

F32 = mybir.dt.float32
F32R = mybir.dt.float32r
ACT = mybir.ActivationFunctionType
ALU = mybir.AluOpType
AX = mybir.AxisListType

P = 128
S, D = 256, 1024
TT = S // P
KT = D // P
EPS = 1e-6
NEG = -1e30
TAPS, TAPS2 = 31, 4
F = 2816
FC = F // 256
FT = F // P
HEADS, GROUPS, DH = 16, 2, 64
NCMP = 15
MLH, MLD = 4, 128
FXH = 8
XH = 4
D_FF = 4 * D
RAWS, SPLITS = 4, 3
SLOT = 2048
TAPG = 8
XSCALE = (D // XH) ** -0.5
Q_BANK = [0, 1, 4, 5]
XKV_BANK = [0, 1, 2, 3, 4, 5, 6, 4]

VECS = [("a_norm", 8), ("a_pw1_b", 16), ("a_dw_b", 8), ("a_ln_g", 8), ("a_ln_b", 8),
        ("kv_norm", 8), ("b_norm", 8), ("ffn_norm", 16), ("final_norm", 8), ("ln1_2", 8),
        ("ml_conv_b_2", 8), ("ln_x_2", 8), ("ln_mem_2", 8), ("ln2_2", 8)]

CONV, FFN0, NSA, FFN1, MID, IN2, MEM, CROSS, FF, LAST = range(10)


def build_kernel(nc, a, out):
    col, n = {}, 0
    for name, rows in VECS:
        col[name] = n
        n += rows
    assert n == P

    ctx = ExitStack()
    with ctx:
        def sb(name, shape, dt=F32):
            return ctx.enter_context(nc.sbuf_tensor(name, shape, dt))

        def halves(name, shape):
            return sb(name + "_hi", shape, F32R), sb(name + "_lo", shape, F32R)

        def sem(name):
            return ctx.enter_context(nc.semaphore(name))

        raw = [sb(f"raw{i}", [P, SLOT]) for i in range(RAWS)]
        split_slot = [halves(f"split{i}", [P, SLOT]) for i in range(SPLITS)]
        h = sb("h", [P, TT, D])
        scaled = sb("scaled", [P, TT, D])
        xn = halves("xn", [P, KT, S])
        ffa = halves("ffa", [P, 4, S])
        act = sb("act", [P, 7184])
        actf = act[:, :]
        PAD = TAPS - 1
        u = sb("u", [P, KT, PAD + S])
        v = sb("v", [P, KT, S])
        vf = v[:, :, :].rearrange("p a b -> p (a b)")
        qT = sb("qT", [P, KT, S])
        qTf = qT[:, :, :].rearrange("p a b -> p (a b)")
        gain_row = sb("gain_row", [P, D])
        gain_ml = sb("gain_ml", [P, MLH * MLD])
        ident = sb("ident", [P, P])
        ones = sb("ones", [P, P])
        mean_w = sb("mean_w", [P, P])
        vecT = sb("vecT", [P, P])
        tapT = sb("tapT", [P, KT, TAPS + TAPS2])
        dist8 = sb("dist8", [P, 3 * P])
        dist8c = sb("dist8c", [P, TT, 16])
        causal = sb("causal", [P, 3 * P])
        causalT = sb("causalT", [P, 3 * P])
        valid = sb("valid", [P, 1])
        nhalf = sb("nhalf", [P, 8])
        eps_col = sb("eps_col", [P, 1])
        posT = sb("posT", [P, 2, 32])
        soft = sb("soft", [P, 3, 800])
        softf = soft[:, :, :].rearrange("p a b -> p (a b)")
        pt = sb("pt", [P, 2, 1024])
        ptf = pt[:, :, :].rearrange("p a b -> p (a b)")
        ssq = sb("ssq", [P, 20])
        msq = sb("msq", [P, 20])
        root_diag = sb("root_diag", [P, TT, P])
        rstd = sb("rstd", [P, 20])
        gates = sb("gates", [P, TT, 48])
        phi2 = sb("phi2", [DH, 2, DH])
        hid = sb("hid", [DH, 2, GROUPS * NCMP])
        kcmp = sb("kcmp", [P, GROUPS, NCMP])
        vcmp = sb("vcmp", [NCMP, GROUPS * DH])
        nmax = sb("nmax", [P, 2, 6])
        rsum = sb("rsum", [P, 2, 6])
        coef = sb("coef", [P, 2, 6])
        rcol = sb("rcol", [P, 2, 8])
        den = dist8[:, 0:48].rearrange("p (r n) -> p r n", n=8)
        expm = dist8[:, 48:64].rearrange("p (t n) -> p t n", t=TT)
        gate_bias = sb("gate_bias", [FXH, 3])
        gtok = dist8[:, 64:96].rearrange("p (t n) -> p t n", t=TT)
        bank = [ctx.enter_context(nc.psum_tensor(f"bank{i}", [P, 512], F32)) for i in range(8)]

        vecs = ptf[:, 0:P]
        taps = vf[0:TAPS + TAPS2, 0:D]
        pos = ptf[0:32, 256:512]
        pw2_row = qT[0:1, 0:4, :].rearrange("p a b -> p (a b)")
        CONV_DVE, SHARED, SHARED_TAPS = 4, 4, 28
        pe_taps = {ft: list(range(SHARED_TAPS if ft == SHARED else 0, TAPS)) for ft in range(CONV_DVE, KT)}
        groups = [(ft, js[i:i + TAPG]) for ft, js in pe_taps.items() for i in range(0, len(js), TAPG)]
        NDIAG = 7
        diag = actf[:, 0:NDIAG * TAPG * P].rearrange("p (g t c) -> p g t c", t=TAPG, c=P)
        window = ptf[:, 0:2 * 32 * 2 * NCMP].rearrange("p (b l g n) -> p b l g n", b=2, l=32, g=GROUPS)
        BIAS = 416
        biases = actf[:, 0:HEADS * BIAS].rearrange("p (h c) -> p h c", c=BIAS)
        k2 = vf[:, 0:1024].rearrange("p (g b k) -> p g b k", g=GROUPS, b=2)
        vtok = vf[:, 1024:1536].rearrange("p (t b c) -> p t b c", t=TT, b=2)
        memk = actf[:, 0:2048].rearrange("p (f m) -> p f m", m=S)
        memv = actf[:, 2048:4096].rearrange("p (t c) -> p t c", t=TT)
        MLV = MLD + 1
        mlv = actf[:, 4096:4096 + TT * MLH * MLV].rearrange("p (t h c) -> p t h c", t=TT, c=MLV)
        mlo = actf[:, 5136:6160].rearrange("p (t c) -> p t c", t=TT)
        fxv = actf[:, 6160:7184].rearrange("p (t c) -> p t c", t=TT)
        row = scaled[0:FXH, :, :].rearrange("p a b -> p (a b)").rearrange("p (r t) -> p r t", t=S)
        memraw = actf[:, 0:2048].rearrange("p (t n) -> p t n", t=TT)
        uf = u[:, :, :].rearrange("p a b -> p (a b)")
        num = uf[:, 1024:1024 + TT * MLH * MLV].rearrange("p (i c) -> p i c", c=MLV)
        mlsq = uf[:, 0:TT * MLH * MLD].rearrange("p (i c) -> p i c", c=MLD)
        NSA_PIECES = [slice(256, 271), slice(0, 128), slice(128, 256),
                      slice(272, 287), slice(288, 544), slice(544, 800)]

        raw_loaded = [sem(f"raw_loaded{i}") for i in range(RAWS)]
        split_hi = sem("split_hi")
        split_lo = sem("split_lo")
        split_lo_pool = sem("split_lo_pool")
        slots_used = sem("slots_used")
        x_loaded = [sem("x_loaded0"), sem("x_loaded1")]
        vecs_loaded = sem("vecs_loaded")
        taps_loaded = sem("taps_loaded")
        vecs_loaded_pool = sem("vecs_loaded_pool")
        vecs_loaded_sp = sem("vecs_loaded_sp")
        small_loaded = sem("small_loaded")
        mem_loaded = sem("mem_loaded")
        gains_loaded = sem("gains_loaded")
        last_gain_loaded = sem("last_gain_loaded")
        xn_hi = sem("xn_hi")
        ffa_hi = sem("ffa_hi")
        ffa_ready = sem("ffa_ready")
        conv_link = sem("conv_link")
        conv_dve = sem("conv_dve")
        silu_hi = sem("silu_hi")
        silu_lo = sem("silu_lo")
        o_hi = sem("o_hi")
        gates_copied = sem("gates_copied")
        out_stored = sem("out_stored")
        pool_step = sem("pool_step")
        consts_built = sem("consts_built")
        bias_built = sem("bias_built")
        h_ready = sem("h_ready")
        ss_ready = sem("ss_ready")
        ms_ready = sem("ms_ready")
        rstd_ready = sem("rstd_ready")
        root_diag_ready = sem("root_diag_ready")
        turned = sem("turned")
        xn_ready = sem("xn_ready")
        acc_done = sem("acc_done")
        out_ready = sem("out_ready")
        pre_turned = sem("pre_turned")
        pre_copied = sem("pre_copied")
        up_done = sem("up_done")
        gate_act = sem("gate_act")
        glu_done = sem("glu_done")
        diag_built = sem("diag_built")
        diag_used = sem("diag_used")
        conv_out = sem("conv_out")
        stat_done = sem("stat_done")
        centred = sem("centred")
        squared = sem("squared")
        squares_summed = sem("squares_summed")
        halved = sem("halved")
        std_ready = sem("std_ready")
        normed = sem("normed")
        silu_ready = sem("silu_ready")
        pads_zero = sem("pads_zero")
        kv_done = sem("kv_done")
        window_zero = sem("window_zero")
        window_ready = sem("window_ready")
        kv_dve = sem("kv_dve")
        kv_act = sem("kv_act")
        phi_done = sem("phi_done")
        q_done = sem("q_done")
        q_ready = sem("q_ready")
        score_done = sem("score_done")
        shifted = sem("shifted")
        exp_done = sem("exp_done")
        dve_link = sem("dve_link")
        act_link = sem("act_link")
        inverse_ready = sem("inverse_ready")
        coef_ready = sem("coef_ready")
        weighed = sem("weighed")
        p_turned = sem("p_turned")
        pt_dve = sem("pt_dve")
        pt_act = sem("pt_act")
        pv_done = sem("pv_done")
        o_ready = sem("o_ready")
        in2_done = sem("in2_done")
        in2_act = sem("in2_act")
        in2_dve = sem("in2_dve")
        conv4_done = sem("conv4_done")
        qk_ready = sem("qk_ready")
        rows_done = sem("rows_done")
        cols_turned = sem("cols_turned")
        xkv_done = sem("xkv_done")
        xkv_act = sem("xkv_act")
        ml_score = sem("ml_score")
        ml_shift = sem("ml_shift")
        ml_exp = sem("ml_exp")
        ml_weight = sem("ml_weight")
        ml_num = sem("ml_num")
        ml_copied = sem("ml_copied")
        ml_sq = sem("ml_sq")
        ml_ms = sem("ml_ms")
        ml_rstd = sem("ml_rstd")
        ml_out = sem("ml_out")
        ml_turned = sem("ml_turned")
        ml_ready = sem("ml_ready")

        chunks, chunk_of, freed, is_split, used_cols = [], {}, [], [], []

        def chunk(stage, parts, by=None, to_split=True, cols=SLOT):
            chunk_of.setdefault(stage, []).append(len(chunks))
            used_cols.append(cols)
            chunks.append(parts)
            freed.append(by or (slots_used, 1 + sum(sm is slots_used for sm, _ in freed)))
            is_split.append(to_split)

        def kn(s, n, k=KT):
            return s[:, 0:k * n].rearrange("p (k n) -> p k n", n=n)

        def by_rows(w):
            return w.rearrange("(k p) n -> p k n", p=P)

        def wide(stage, w, start, width, by=None):
            chunk(stage, [(lambda s: kn(s, width), by_rows(w)[:, :, start:start + width])], by,
                  cols=KT * width)

        def pair(stage, w, start, other, by):
            chunk(stage, [(lambda s, b=b: kn(s, 256)[:, :, P * b:P * b + P], by_rows(w)[:, :, c:c + P])
                          for b, c in enumerate((start, other))], by)

        def half_rows(stage, w, start, by):
            for k in range(2):
                chunk(stage, [(lambda s: kn(s, 512, 4), by_rows(w)[:, 4 * k:4 * k + 4, start:start + 512])],
                      by if k else None)

        def tall(stage, w, k, acc, tiles):
            chunk(stage, [(lambda s: kn(s, D, 2), by_rows(w)[:, k:k + 2, :])],
                  (acc_done, acc) if k + 2 == tiles else None)

        def residual(stage, w, acc):
            for c in range(2):
                half_rows(stage, w, 512 * c, (acc_done, acc + 2 * c + 2))

        UP0 = {"pw1": 0, "ffn0": KT, "ffn1": KT + FT, "ff": KT + 2 * FT}

        for c in range(KT):
            pair("pw1", a["a_pw1_w"][0], P * c, D + P * c, (up_done, c + 1))
        residual("pw2", a["a_pw2_w"][0], 0)

        def ffn_chunks(which, acc):
            stage, w, down = f"ffn{which}", a["ffn_w_in"][which], a["ffn_w_out"][which]
            for g in range(FC + 1):
                if g < FC:
                    for ft in (2 * g, 2 * g + 1):
                        pair(stage + "_in", w, P * ft, F + P * ft, (up_done, UP0[stage] + ft + 1))
                if g:
                    tall(stage + "_out", down, 2 * g - 2, acc, FT)

        ffn_chunks(0, 8)
        wide("kv", a["w_kv"], 0, 256, (kv_done, 1))
        pair("kv", a["w_kv"], 2 * P, 4 * P, (kv_done, 2))
        pair("kv", a["w_kv"], 3 * P, 5 * P, (kv_done, 3))
        for b, name in enumerate(("phi_k_w1", "phi_v_w1")):
            chunk("phi", [(lambda s, g=g: s[DH * g:DH * g + DH, :].rearrange("p (l e) -> p l e", e=DH),
                           a[name].rearrange("(l d) e -> d l e", d=DH)) for g in range(2)],
                  (phi_done, b + 1), to_split=False)
        wide("gates", a["b_w_in"][0], D, 48, (q_done, 1))
        for c in range(4):
            wide("q", a["b_w_in"][0], 256 * c, 256, (q_done, c + 2))
        residual("b_out", a["b_w_out"][0], 8)
        ffn_chunks(1, 16)
        w_in2 = a["w_in_2"][0]
        for c in range(4):
            wide("ml_qk", w_in2, 256 * c, 256, (in2_done, c + 1))
        half_rows("ml_v", w_in2, 1024, (in2_done, 5))
        half_rows("ml_o", w_in2, 1536, (in2_done, 6))
        for c in range(2):
            wide("fx_q", w_in2, 2056 + 256 * c, 256, (in2_done, 7 + c))
        for c in range(2):
            wide("fx_k", w_in2, 2568 + 256 * c, 256, (in2_done, 9 + c))
        half_rows("fx_v", w_in2, 3080, (in2_done, 11))
        chunk("rows", [(lambda s: kn(s, 16)[:, :, 0:8], by_rows(w_in2)[:, :, 2048:2056]),
                       (lambda s: kn(s, 16)[:, :, 8:16], by_rows(w_in2)[:, :, 3592:3600])], (in2_done, 12),
              cols=KT * 16)
        for c in range(4):
            wide("xkv_k", a["w_xkv_2"][0], 256 * c, 256, (xkv_done, c + 1))
        for c in range(2):
            half_rows("xkv_v", a["w_xkv_2"][0], D + 512 * c, (xkv_done, 4 + 2 * c + 2))
        residual("out2", a["w_out_2"][0], 16)
        for c in range(4):
            wide("xq", a["w_xq_2"][0], 256 * c, 256, (q_done, 5 + c + 1))
        residual("xo", a["w_xo_2"][0], 20)
        for g in range(17):
            if g < 16:
                wide("ff_in", a["w_ff1_2"][0], 256 * g, 256, (up_done, UP0["ff"] + g + 1))
            if g:
                tall("ff_out", a["w_ff2_2"][0], 2 * g - 2, 28, D_FF // P)

        nth = [sum(is_split[:c]) for c in range(len(chunks))]
        of_split = [c for c in range(len(chunks)) if is_split[c]]

        def loads_through(c):
            return 16 * sum(len(chunks[i]) for i in range(c % RAWS, c + 1, RAWS))

        by_pool = [chunk_of["pw1"][3], chunk_of["pw1"][6]] + chunk_of["pw2"][0:3]

        def lo_count(c):
            if c in by_pool:
                return split_lo_pool, by_pool.index(c) + 1
            return split_lo, sum(is_split[i] and i not in by_pool for i in range(c + 1))

        def splitter(emit):
            at = [0]

            def through(c):
                while at[0] <= min(c, len(chunks) - 1):
                    if is_split[at[0]]:
                        emit(at[0], nth[at[0]])
                    at[0] += 1
            return through

        stage_before = {FFN0: "pw2", NSA: "ffn0_out", FFN1: "b_out", MID: "ffn1_out", CROSS: "out2",
                        FF: "xo", LAST: "ff_out"}

        def last_before(k):
            return chunk_of[stage_before[k]][-1]

        turning = [CONV, FFN0, NSA, FFN1, IN2, MEM, CROSS, FF]
        gains = {CONV: [("a_norm", 0)], FFN0: [("ffn_norm", 0)], NSA: [("kv_norm", 0), ("b_norm", 0)],
                 FFN1: [("ffn_norm", 8)], IN2: [("ln1_2", 0)], MEM: [("ln_mem_2", 0)],
                 CROSS: [("ln_x_2", 0)], FF: [("ln2_2", 0)]}
        xn_before, n = {}, 0
        for k in turning:
            xn_before[k] = n
            n += 4 * len(gains[k])
        h_order = [FFN0, NSA, FFN1, MID, IN2, CROSS, FF, LAST]
        residuals = [FFN0, NSA, FFN1, MID, CROSS, FF, LAST]

        def h_count(k, t):
            return TT * h_order.index(k) + t + 1

        def ends(k):
            if k in (NSA, MID, LAST):
                return [(t, c) for t in range(TT) for c in range(2)]
            return [(t, c) for c in range(2) for t in range(TT)]

        def tok(t):
            return slice(P * t, P * t + P)

        block = ctx.enter_context(nc.Block())

        vec_loads, tap_loads = [], []
        for name, rows in VECS:
            s = a[name]
            vec_loads.append((vecs[col[name]:col[name] + rows, :],
                              s.rearrange("(k p) -> k p", p=P) if len(s.shape) == 1 else
                              s.rearrange("a (k p) -> (a k) p", p=P)))
        tap_loads.append((taps[0:TAPS, :], a["a_dw_w"][0]))
        tap_loads.append((taps[TAPS:TAPS + TAPS2, :], a["ml_conv_w_2"][0]))
        for b, name in enumerate(("cmp_pos_k", "cmp_pos_v")):
            for g in range(2):
                tap_loads.append((pos[:, P * b + DH * g:P * b + DH * g + DH], a[name]))
        pool_loads, act_loads, sp_loads = vec_loads[0:3], vec_loads[3:9], vec_loads[9:]

        @block.sync
        def _(sp):
            for t in range(TT):
                sp.dma_start(h[:, t, :], a["x"][0].rearrange("(t p) n -> p t n", p=P)[:, t, :]
                             ).then_inc(x_loaded[t], 16)
            for c, parts in enumerate(chunks):
                if c >= RAWS:
                    last = c - RAWS
                    if is_split[last]:
                        sp.wait_ge(*lo_count(last))
                    else:
                        sp.wait_ge(*freed[last])
                for place, src in parts:
                    sp.dma_start(place(raw[c % RAWS]), src).then_inc(raw_loaded[c % RAWS], 16)
                if c == 0:
                    for dst, src in sp_loads:
                        sp.dma_start(dst, src).then_inc(vecs_loaded_sp, 16)
                    for dst, src in tap_loads:
                        sp.dma_start(dst, src).then_inc(taps_loaded, 16)
            for t in range(TT):
                sp.wait_ge(out_ready, t + 1)
                sp.dma_start(out[0].rearrange("(t p) n -> p t n", p=P)[:, t, :],
                             scaled[:, t, :]).then_inc(out_stored, 16)
            sp.wait_ge(out_stored, 32)

        @block.gpsimd
        def _(pool):
            nc.gpsimd.memset(ident[:, :], 0.0).then_inc(pool_step, 1)
            nc.gpsimd.memset(nhalf[:, :], -0.5).then_inc(pool_step, 1)
            nc.gpsimd.memset(eps_col[:, :], EPS).then_inc(pool_step, 1)
            pool.wait_ge(pool_step, 3)
            nc.gpsimd.affine_select(out=ident[:, :], in_=ident[:, :], compare_op=ALU.not_equal, fill=1.0,
                                    base=0, pattern=[[-1, P]], channel_multiplier=1).then_inc(consts_built, 1)
            for dst, src in pool_loads:
                pool.dma_start(dst, src).then_inc(vecs_loaded_pool, 16)

            def root(k):
                for t in range(TT):
                    c = TT * k + t
                    pool.wait_ge(ss_ready, c + 1)
                    nc.gpsimd.tensor_scalar(msq[:, c:c + 1], ssq[:, c:c + 1], EPS, None,
                                            ALU.add).then_inc(ms_ready, 1)
                    pool.wait_ge(ms_ready, c + 1)
                    nc.gpsimd.tensor_tensor(rstd[:, c:c + 1], msq[:, c:c + 1], nhalf[:, 0:1],
                                            ALU.pow).then_inc(rstd_ready, 1)

            root(CONV)
            nc.gpsimd.memset(mean_w[:, :], 1.0 / D).then_inc(pool_step, 1)
            nc.gpsimd.memset(causal[:, :], 0.0).then_inc(pool_step, 1)
            nc.gpsimd.memset(causalT[:, :], 0.0).then_inc(pool_step, 1)
            nc.gpsimd.memset(valid[:, :], 1.0).then_inc(pool_step, 1)
            nc.gpsimd.memset(ones[:, :], 1.0).then_inc(pool_step, 1)
            nc.gpsimd.iota(dist8[:, 0:P], pattern=[[8, P]], base=0, channel_multiplier=-8,
                           allow_small_or_imprecise_dtypes=True).then_inc(pool_step, 1)
            nc.gpsimd.iota(dist8[:, P:3 * P], pattern=[[8, 2 * P]], base=-8 * P, channel_multiplier=-8,
                           allow_small_or_imprecise_dtypes=True).then_inc(pool_step, 1)
            nc.gpsimd.iota(dist8c[:, :, :], pattern=[[-8 * P, 2], [128, 16]], base=8 * 31,
                           channel_multiplier=-8, allow_small_or_imprecise_dtypes=True).then_inc(pool_step, 1)
            pool.wait_ge(pool_step, 11)

            def mask(m, pattern, base, step):
                nc.gpsimd.affine_select(out=m, in_=m, compare_op=ALU.is_ge, fill=NEG, base=base,
                                        pattern=pattern, channel_multiplier=step).then_inc(consts_built, 1)

            for m in (dist8, causal):
                mask(m[:, 0:P], [[-1, P]], 0, 1)
                mask(m[:, P:3 * P], [[-1, 2 * P]], P, 1)
            mask(dist8c[:, :, :], [[P, 2], [-16, 16]], -31, 1)
            mask(causalT[:, 0:2 * P], [[1, 2 * P]], 0, -1)
            mask(causalT[:, 2 * P:3 * P], [[1, P]], 0, -1)
            nc.gpsimd.affine_select(out=valid[:, :], in_=valid[:, :], compare_op=ALU.is_ge, fill=0.0,
                                    base=-31, pattern=[[0, 1]], channel_multiplier=1).then_inc(consts_built, 1)

            for c in by_pool:
                m = nth[c]
                pool.wait_ge(split_hi, m + 1)
                hi, lo = split_slot[m % SPLITS]
                nc.gpsimd.tensor_tensor(lo[:, :], raw[c % RAWS][:, :], hi[:, :].bitcast(F32),
                                        ALU.subtract).then_inc(split_lo_pool, 1)
            root(FFN0)
            pool.wait_ge(h_ready, h_count(FFN0, 1))
            pool.wait_ge(consts_built, 9)
            for i in range(HEADS):
                slope = 2.0 ** (-8.0 * (i + 1) / HEADS)
                nc.gpsimd.tensor_scalar(biases[:, i, 0:3 * P], dist8[:, :], slope, None, ALU.mult)
                nc.gpsimd.tensor_scalar(biases[:, i, 3 * P:3 * P + 32],
                                        dist8c[:, :, :].rearrange("p a b -> p (a b)"), slope, None,
                                        ALU.mult).then_inc(bias_built, 1)
            pool.wait_ge(h_ready, h_count(NSA, 0))
            nc.gpsimd.memset(ptf[:, 0:2 * 32 * 2 * NCMP], 0.0).then_inc(window_zero, 1)
            for k in (NSA, FFN1, MID, IN2, MEM):
                root(k)
            pool.wait_ge(ml_sq, 1)
            nc.gpsimd.tensor_scalar(den[:, 4, :], den[:, 3, :], 1.0 / MLD, EPS, ALU.mult,
                                    ALU.add).then_inc(ml_ms, 1)
            pool.wait_ge(ml_ms, 1)
            nc.gpsimd.tensor_tensor(den[:, 5, :], den[:, 4, :], nhalf[:, :], ALU.pow).then_inc(ml_rstd, 1)
            for k in (CROSS, FF, LAST):
                root(k)

        @block.scalar
        def _(sc):
            for dst, src in act_loads:
                sc.dma_start(dst, src).then_inc(vecs_loaded, 16)
            def split(c, m):
                sc.wait_ge(raw_loaded[c % RAWS], loads_through(c))
                if m >= SPLITS:
                    sc.wait_ge(*freed[of_split[m - SPLITS]])
                n = used_cols[c]
                nc.scalar.activation(split_slot[m % SPLITS][0][:, 0:n], raw[c % RAWS][:, 0:n],
                                     ACT.Copy).then_inc(split_hi, 1)

            through = splitter(split)

            def squares(k, src, ready, together=False):
                idx = turning.index(k) if k in turning else None

                def diagonal(t):
                    if idx:
                        sc.wait_ge(turned, 4 * idx)
                    sc.wait_ge(rstd_ready, TT * k + t + 1)
                    nc.scalar.activation(root_diag[:, t, :], ident[:, :], ACT.Copy,
                                         scale=rstd[:, TT * k + t:TT * k + t + 1]).then_inc(root_diag_ready, 1)

                for t in range(TT):
                    ready(t)
                    nc.scalar.activation(scaled[:, t, :], src[:, t, :], ACT.Square, scale=D ** -0.5,
                                         accum_out=ssq[:, TT * k + t:TT * k + t + 1]).then_inc(ss_ready, 1)
                    if idx is not None and not together:
                        diagonal(t)
                for t in range(TT if together else 0):
                    diagonal(t)

            def h_squares(k):
                if k in stage_before:
                    through(last_before(k) + 2)
                squares(k, h, lambda t: sc.wait_ge(h_ready, h_count(k, t)))

            def take_hi(k, which=0):
                name, off = gains[k][which]
                for n in range(4):
                    if which == 0:
                        sc.wait_ge(turned, 4 * turning.index(k) + n + 1)
                    for kt in (2 * n, 2 * n + 1):
                        g = col[name] + off + kt
                        x = nc.scalar.activation(xn[0][:, kt, :], bank[n][:, S * (kt % 2):S * (kt % 2) + S], ACT.Copy,
                                                 scale=vecT[:, g:g + 1])
                    x.then_inc(xn_hi, 1)
                if k in stage_before and which == 0:
                    through(last_before(k) + 3)

            sc.wait_ge(consts_built, 1)
            squares(CONV, h, lambda t: sc.wait_ge(x_loaded[t], 16), together=True)
            through(0)
            sc.wait_ge(pre_copied, 1)
            take_hi(CONV)

            def diagonals(g):
                ft, js = groups[g]
                if g >= NDIAG:
                    sc.wait_ge(diag_used, g - NDIAG + 1)
                for q, j in enumerate(js):
                    x = nc.scalar.activation(diag[:, g % NDIAG, q, :], ident[:, :], ACT.Copy,
                                             scale=tapT[:, ft, j:j + 1])
                x.then_inc(diag_built, 1)

            for ft in range(KT):
                through(chunk_of["pw1"][ft] + 2)
                sc.wait_ge(up_done, ft + 1)
                if ft >= 4:
                    sc.wait_ge(glu_done, ft - 3)
                nc.scalar.activation(softf[:, S * (ft % 4):S * (ft % 4) + S], bank[ft % 4][:, S:2 * S], ACT.Sigmoid,
                                     bias=vecT[:, col["a_pw1_b"] + 8 + ft:col["a_pw1_b"] + 9 + ft]
                                     ).then_inc(gate_act, 1)
                if ft == 0:
                    sc.wait_ge(pre_copied, 3)
                if ft < NDIAG:
                    diagonals(ft)
            through(chunk_of["pw2"][2])
            for b, name in enumerate(("phi_k_w2", "phi_v_w2")):
                sc.dma_start(phi2[:, b, :], a[name]).then_inc(small_loaded, 16)
            sc.dma_start(pw2_row, a["a_pw2_b"]).then_inc(small_loaded, 16)
            sc.wait_ge(pads_zero, 1)
            for b, (name, m) in enumerate((("fx_b_f_2", FXH), ("ml_b_f_2", MLH), ("ml_b_i_2", MLH))):
                sc.dma_start(gate_bias[0:m, b:b + 1], a[name].rearrange("a n -> n a")).then_inc(small_loaded, 16)
            sc.dma_start(gain_row[:, :], a["final_norm"].rearrange("(a n) -> a n", a=1)
                         .broadcast_to([P, D])).then_inc(gains_loaded, 16)
            sc.dma_start(gain_ml[:, :], a["ml_norm_2"].broadcast_to([P, MLH * MLD])).then_inc(gains_loaded, 16)
            built = NDIAG
            for ft in range(CONV_DVE, KT):
                tile_end = max(g for g in range(len(groups)) if groups[g][0] == ft) + 1
                while built < min(tile_end + NDIAG, len(groups)):
                    diagonals(built)
                    built += 1
                if ft != SHARED:
                    sc.wait_ge(diag_used, tile_end)
                    nc.scalar.activation(v[:, ft, :], bank[ft][:, 0:S], ACT.Identity,
                                         bias=vecT[:, col["a_dw_b"] + ft:col["a_dw_b"] + ft + 1]
                                         ).then_inc(conv_out, 1)
            for j in range(2):
                sc.wait_ge(centred, j + 1)
                nc.scalar.activation(actf[:, D * j:D * j + D], vf[:, D * j:D * j + D],
                                     ACT.Square).then_inc(squared, 1)
            sc.wait_ge(stat_done, 2)
            nc.scalar.activation(softf[:, 0:S], bank[1][:, 0:S], ACT.Sqrt, bias=eps_col[:, :]).then_inc(std_ready, 1)
            for ft in range(KT):
                sc.wait_ge(normed, ft // 2 + 1)
                nc.scalar.activation(v[:, ft, :], v[:, ft, :], ACT.Silu,
                                     bias=vecT[:, col["a_ln_b"] + ft:col["a_ln_b"] + ft + 1],
                                     scale=vecT[:, col["a_ln_g"] + ft:col["a_ln_g"] + ft + 1]
                                     ).then_inc(silu_ready, 1)

            def ffn_act(which):
                stage = f"ffn{which}"
                for ft in range(FT):
                    through(chunk_of[stage + "_in"][ft] + 2)
                    n, b = UP0[stage] + ft, slice(S * (ft % 4), S * (ft % 4) + S)
                    sc.wait_ge(up_done, n + 1)
                    nc.scalar.activation(softf[:, b], bank[ft % 4][:, 0:S], ACT.Silu).then_inc(gate_act, 1)
                    sc.wait_ge(glu_done, n + 1)
                    if ft >= 4:
                        sc.wait_ge(*freed[chunk_of[stage + "_out"][ft // 2 - 2]])
                    nc.scalar.activation(ffa[0][:, ft % 4, :], ptf[:, b], ACT.Copy).then_inc(ffa_hi, 1)

            h_squares(FFN0)
            take_hi(FFN0)
            ffn_act(0)
            h_squares(NSA)
            take_hi(NSA)

            def nsa_exp(i):
                s = soft[:, i % 3, :]
                sc.wait_ge(shifted, i + 1)
                for n, piece in enumerate(NSA_PIECES):
                    x = nc.scalar.activation(s[:, piece], s[:, piece], ACT.Exp, scale=-1.0,
                                             bias=nmax[:, i % 2, n:n + 1], accum_out=rsum[:, i % 2, n:n + 1])
                x.then_inc(exp_done, 1)

            sc.wait_ge(kv_done, 3)
            take_hi(NSA, 1)
            through(chunk_of["q"][0])

            for half in range(2):
                nc.scalar.activation(k2[DH * half:DH * half + DH, 1, :, :].rearrange("p b k -> p (b k)"),
                                     bank[5][DH:P, :], ACT.Copy).then_inc(kv_act, 1)
            through(chunk_of["q"][1])
            sc.wait_ge(phi_done, 2)
            nc.scalar.activation(hid[:, :, :].rearrange("p b n -> p (b n)"), bank[7][0:DH, 0:4 * NCMP],
                                 ACT.Silu).then_inc(kv_act, 1)
            sc.wait_ge(q_done, 1)
            nc.scalar.activation(gates[:, :, :].rearrange("p t c -> p (t c)"), bank[4][:, 0:96],
                                 ACT.Sigmoid).then_inc(q_ready, 1)
            for b in range(4):
                through(min(chunk_of["q"][b] + 2, chunk_of["q"][3] + 1))
                if b == 3:
                    nsa_exp(0)
                sc.wait_ge(q_done, b + 2)
                nc.scalar.activation(qTf[:, 512 * b:512 * b + 512], bank[Q_BANK[b]][:, :],
                                     ACT.Copy).then_inc(q_ready, 1)
                if b == 0:
                    sc.wait_ge(phi_done, 3)
                    nc.scalar.activation(kcmp[:, :, :].rearrange("p g n -> p (g n)"),
                                         bank[7][:, 64:64 + GROUPS * NCMP], ACT.Copy)
                    nc.scalar.activation(vcmp[:, :], bank[7][0:NCMP, P:2 * P], ACT.Copy).then_inc(kv_act, 1)

            def nsa_evac(i):
                sc.wait_ge(p_turned, i + 1)
                if i >= 2:
                    sc.wait_ge(pv_done, i - 1)
                nc.scalar.activation(pt[:, i % 2, 384:768], bank[5][:, 0:384], ACT.Copy)
                nc.scalar.activation(pt[0:NCMP, i % 2, 768 + P:1024], bank[5][0:NCMP, 384:512],
                                     ACT.Copy).then_inc(pt_act, 1)

            def out_hi(pv, dst, src):
                sc.wait_ge(pv_done, pv)
                nc.scalar.activation(dst, src, ACT.Copy).then_inc(o_hi, 1)

            nsa_exp(1)
            for i in range(HEADS):
                nsa_evac(i)
                if i + 2 < HEADS:
                    nsa_exp(i + 2)
                if i % 2 == 0 and i:
                    out_hi(i, xn[0][:, i // 2 - 1, :], bank[6 + (i // 2 - 1) % 2][:, 0:S])
            out_hi(HEADS, xn[0][:, HEADS // 2 - 1, :], bank[7][:, 0:S])
            through(chunk_of["b_out"][2])

            sc.wait_ge(shifted, HEADS)
            mem_src = a["mem_2"][0].rearrange("(t p) n -> p t n", p=P)
            sc.dma_start(memraw, mem_src).then_inc(mem_loaded, 16)
            h_squares(FFN1)
            take_hi(FFN1)
            ffn_act(1)
            h_squares(MID)
            h_squares(IN2)
            sc.dma_start(gain_row[:, :], a["ln_f_2"].rearrange("(a n) -> a n", a=1)
                         .broadcast_to([P, D])).then_inc(last_gain_loaded, 16)
            take_hi(IN2)
            through(last_before(MID) + 3)

            squares(MEM, memraw, lambda t: sc.wait_ge(mem_loaded, 16))

            for b in range(4):
                through(chunk_of["ml_qk"][b] + 2)
                sc.wait_ge(in2_done, b + 1)
                nc.scalar.activation(u[:, 2 * b:2 * b + 2, PAD:PAD + S],
                                     bank[b][:, :].rearrange("p (f t) -> p f t", f=2),
                                     ACT.Copy).then_inc(in2_act, 1)
            through(chunk_of["ml_v"][1] + 2)
            for ft in range(KT):
                sc.wait_ge(conv4_done, ft + 1)
                nc.scalar.activation(v[:, ft, :], v[:, ft, :], ACT.Silu).then_inc(qk_ready, 1)
            through(chunk_of["ml_o"][1] + 2)
            sc.wait_ge(in2_done, 6)
            for t in range(TT):
                nc.scalar.activation(mlo[:, t, :], bank[6 + t][:, :], ACT.Sigmoid).then_inc(in2_act, 1)
            for b in range(4):
                through(chunk_of["fx_q"][0] + b + 2)
                sc.wait_ge(in2_done, 7 + b)
                nc.scalar.activation(qTf[:, 512 * b:512 * b + 512], bank[b][:, :], ACT.Copy).then_inc(in2_act, 1)
            through(chunk_of["rows"][0] + 3)
            take_hi(MEM)
            sc.wait_ge(rows_done, 1)
            nc.scalar.activation(row[:, 2:4, :], row[:, 2:4, :], ACT.Exp).then_inc(act_link, 1)
            through(chunk_of["xkv_k"][3])
            sc.wait_ge(rows_done, 2)
            nc.scalar.activation(row[:, 6:8, :], row[:, 4:6, :], ACT.Ln).then_inc(act_link, 1)
            def memory_evac(b):
                sc.wait_ge(xkv_done, b + 1)
                dst = memk[:, 2 * b:2 * b + 2, :].rearrange("p f t -> p (f t)") if b < 4 else \
                    memv[:, b % 2, 512 * (b // 2 - 2):512 * (b // 2 - 2) + 512]
                nc.scalar.activation(dst, bank[XKV_BANK[b]][:, :], ACT.Copy).then_inc(xkv_act, 1)

            for b in range(6):
                through((chunk_of["xkv_k"][b] if b < 4 else chunk_of["xkv_v"][1]) + 2)
                memory_evac(b)
            sc.wait_ge(rows_done, 4)
            nc.scalar.activation(expm[:, :, :], bank[7][:, 16:32].rearrange("p (t n) -> p t n", t=TT),
                                 ACT.Exp).then_inc(act_link, 1)

            def mlstm_exp(i):
                sc.wait_ge(ml_shift, i + 1)
                w = soft[:, i % 2, :]
                nc.scalar.activation(w[:, 0:S], w[:, 0:S], ACT.Exp, bias=rcol[:, 0, i:i + 1])
                nc.scalar.activation(w[:, S:3 * P], w[:, S:3 * P], ACT.Exp,
                                     bias=rcol[:, 1, i:i + 1]).then_inc(ml_exp, 1)

            mlstm_exp(0)
            mlstm_exp(1)
            through(chunk_of["out2"][1])
            memory_evac(6)
            memory_evac(7)
            mlstm_exp(2)
            mlstm_exp(3)
            sc.wait_ge(ml_copied, MLH + 1)
            nc.scalar.activation(mlsq, num[:, :, 0:MLD], ACT.Square).then_inc(act_link, 1)

            def fx_exp(i):
                n, s = HEADS + i, soft[:, i % 3, :]
                sc.wait_ge(shifted, n + 1)
                nc.scalar.activation(s[:, 0:P], s[:, 0:P], ACT.Exp, scale=-1.0, bias=nmax[:, i % 2, 0:1],
                                     accum_out=rsum[:, i % 2, 0:1])
                nc.scalar.activation(s[:, P:3 * P], s[:, P:3 * P], ACT.Exp, scale=-1.0,
                                     bias=nmax[:, i % 2, 1:2],
                                     accum_out=rsum[:, i % 2, 1:2]).then_inc(exp_done, 1)

            def fx_evac(i):
                n = HEADS + i
                sc.wait_ge(p_turned, n + 1)
                if i < 2:
                    sc.wait_ge(ml_num, MLH)
                else:
                    sc.wait_ge(pv_done, n - 1)
                nc.scalar.activation(pt[:, i % 2, 0:3 * P], bank[6 + i % 2][:, 0:3 * P],
                                     ACT.Copy).then_inc(pt_act, 1)

            fx_exp(0)
            fx_exp(1)
            for i in range(FXH):
                fx_evac(i)
                if i + 2 < FXH:
                    fx_exp(i + 2)
                if i % 2 == 0 and i:
                    out_hi(HEADS + i, xn[0][:, 3 + i // 2, :], bank[1 + 2 * ((i // 2 - 1) % 2)][:, 0:S])
            out_hi(HEADS + FXH, xn[0][:, KT - 1, :], bank[3][:, 0:S])
            for t in range(TT):
                sc.wait_ge(ml_turned, t + 1)
                nc.scalar.activation(xn[0][:, 0:MLH, tok(t)], bank[4 + t][:, :].rearrange("p (h c) -> p h c", h=MLH),
                                     ACT.Copy).then_inc(o_hi, 1)

            h_squares(CROSS)
            take_hi(CROSS)
            def x_exp(i):
                n = HEADS + FXH + i
                sc.wait_ge(shifted, n + 1)
                for t in range(TT):
                    x = nc.scalar.activation(soft[:, i % 2, S * t:S * t + S], bank[4 + i % 2][:, S * t:S * t + S],
                                             ACT.Exp, scale=XSCALE, bias=nmax[:, i % 2, 2 + t:3 + t],
                                             accum_out=rsum[:, i % 2, t:t + 1])
                x.then_inc(exp_done, 1)

            for b in range(4):
                through(chunk_of["xq"][b] + 2)
                if b == 3:
                    x_exp(0)
                    x_exp(1)
                sc.wait_ge(q_done, 6 + b)
                nc.scalar.activation(qTf[:, 512 * b:512 * b + 512], bank[b][:, :], ACT.Copy).then_inc(q_ready, 1)

            def x_evac(i):
                n = HEADS + FXH + i
                sc.wait_ge(p_turned, n + 1)
                if i >= 2:
                    sc.wait_ge(pv_done, n - 1)
                nc.scalar.activation(pt[:, i % 2, 0:512], bank[6 + i % 2][:, :], ACT.Copy).then_inc(pt_act, 1)

            def x_out_hi(i):
                out_hi(HEADS + FXH + i + 1, xn[0][:, 2 * i:2 * i + 2, :].rearrange("p f t -> p (f t)"), bank[i][:, :])

            for i in range(XH):
                x_evac(i)
                if i + 2 < XH:
                    x_exp(i + 2)
                if i:
                    x_out_hi(i - 1)
            x_out_hi(XH - 1)

            h_squares(FF)
            take_hi(FF)
            for g in range(D_FF // S):
                through(chunk_of["ff_in"][g] + 2)
                n = UP0["ff"] + g
                sc.wait_ge(up_done, n + 1)
                nc.scalar.activation(softf[:, 512 * (g % 3):512 * (g % 3) + 512], bank[g % 4][:, :],
                                     ACT.Relu).then_inc(gate_act, 1)
                sc.wait_ge(glu_done, n + 1)
                if g >= 2:
                    sc.wait_ge(*freed[chunk_of["ff_out"][g - 2]])
                nc.scalar.activation(ffa[0][:, 2 * (g % 2):2 * (g % 2) + 2, :].rearrange("p f t -> p (f t)"),
                                     ptf[:, 512 * (g % 4):512 * (g % 4) + 512], ACT.Copy).then_inc(ffa_hi, 1)
            h_squares(LAST)

        @block.vector
        def _(ve):
            links = [0]

            def link(x):
                links[0] += 1
                x.then_inc(dve_link, 1)
                ve.wait_ge(dve_link, links[0])

            def less_hi(dst, src, hi):
                return nc.vector.tensor_tensor(dst, src, hi.bitcast(F32), ALU.subtract)

            def split(c, m):
                if c in by_pool:
                    return
                ve.wait_ge(split_hi, m + 1)
                n, (hi, lo) = used_cols[c], split_slot[m % SPLITS]
                less_hi(lo[:, 0:n], raw[c % RAWS][:, 0:n], hi[:, 0:n]).then_inc(split_lo, 1)

            through = splitter(split)

            def take(k, which=0):
                name, off = gains[k][which]
                for n in range(4):
                    ve.wait_ge(xn_hi, xn_before[k] + 4 * which + n + 1)
                    for kt in (2 * n, 2 * n + 1):
                        g = col[name] + off + kt
                        x = nc.vector.scalar_tensor_tensor(
                            out=xn[1][:, kt, :], in0=bank[n][:, S * (kt % 2):S * (kt % 2) + S],
                            scalar=vecT[:, g:g + 1], in1=xn[0][:, kt, :].bitcast(F32),
                            op0=ALU.mult, op1=ALU.subtract)
                    x.then_inc(xn_ready, 1)

            def add(k):
                last = last_before(k)
                through(last + 1)
                for n, (t, c) in enumerate(ends(k)):
                    if t and c == (0 if k in (NSA, MID, LAST) else 1):
                        through(last + 2)
                    ve.wait_ge(acc_done, 4 * residuals.index(k) + n + 1)
                    part = h[:, t, 512 * c:512 * c + 512]
                    x = nc.vector.tensor_tensor(part, part, bank[4 + 2 * t + c][:, :], ALU.add)
                    if c == 1:
                        x.then_inc(h_ready, 1)

            nc.vector.memset(gate_bias[:, :], 0.0).then_inc(pads_zero, 1)
            nc.vector.memset(u[:, :, 0:PAD], 0.0).then_inc(pads_zero, 1)
            ve.wait_ge(pre_turned, 1)
            nc.vector.tensor_copy(vecT[:, :], bank[4][:, 0:P]).then_inc(pre_copied, 1)
            ve.wait_ge(pre_copied, 1)
            through(0)
            take(CONV)

            def glu_pw1(ft):
                through(chunk_of["pw1"][ft] + 2)
                ve.wait_ge(gate_act, ft + 1)
                b = col["a_pw1_b"] + ft
                nc.vector.scalar_tensor_tensor(
                    out=u[:, ft, PAD:PAD + S], in0=bank[ft % 4][:, 0:S], scalar=vecT[:, b:b + 1],
                    in1=softf[:, S * (ft % 4):S * (ft % 4) + S], op0=ALU.add, op1=ALU.mult).then_inc(glu_done, 1)

            glu_pw1(0)
            ve.wait_ge(pre_turned, 2)
            nc.vector.tensor_copy(tapT[:, :, :].rearrange("p k c -> p (k c)"),
                                  bank[5][:, 0:KT * (TAPS + TAPS2)]).then_inc(pre_copied, 1)
            ve.wait_ge(pre_turned, 3)
            nc.vector.tensor_copy(posT[:, :, :].rearrange("p b l -> p (b l)"), bank[6][:, 0:64]).then_inc(pre_copied, 1)
            glu_pw1(1)
            ve.wait_ge(pre_copied, 3)
            tasks = [lambda ft=ft: glu_pw1(ft) for ft in range(2, KT)]
            tasks += [lambda j=j: through(chunk_of["pw2"][j]) for j in range(3)]
            ve.wait_ge(glu_done, 2)
            taps_done, tap_done = 0, {}
            for fts in ((0, 1), (2, 3, SHARED)):
                for j in range(TAPS):
                    if j % 4 == 3 and tasks:
                        tasks.pop(0)()
                    if SHARED in fts and j == SHARED_TAPS:
                        fts = fts[:-1]
                    for f, ft in enumerate(fts):
                        tap, dst, src = tapT[:, ft, j:j + 1], v[:, ft, :], u[:, ft, j:j + S]
                        b = col["a_dw_b"] + ft
                        if j == 0:
                            ve.wait_ge(glu_done, ft + 1)
                            x = nc.vector.tensor_scalar(dst, src, tap, vecT[:, b:b + 1], ALU.mult, ALU.add)
                        else:
                            ve.wait_ge(conv_link, tap_done[ft])
                            x = nc.vector.scalar_tensor_tensor(out=dst, in0=src, scalar=tap, in1=dst,
                                                               op0=ALU.mult, op1=ALU.add)
                        if j == TAPS - 1:
                            x.then_inc(conv_dve, 1)
                        else:
                            taps_done += 1
                            tap_done[ft] = taps_done
                            x.then_inc(conv_link, 1)
            ve.wait_ge(diag_used, 1 + max(g for g in range(len(groups)) if groups[g][0] == SHARED))
            ve.wait_ge(conv_link, tap_done[SHARED])
            nc.vector.tensor_tensor(v[:, SHARED, :], v[:, SHARED, :], bank[SHARED][:, 0:S],
                                    ALU.add).then_inc(conv_dve, 1)
            for task in tasks:
                task()

            ve.wait_ge(stat_done, 1)
            for j in range(2):
                part = v[:, 4 * j:4 * j + 4, :]
                nc.vector.tensor_tensor(part, part, bank[0][:, 0:S].unsqueeze(1).broadcast_to([P, 4, S]),
                                        ALU.subtract).then_inc(centred, 1)
            for j in range(2):
                ve.wait_ge(squared, j + 1)
                x = nc.vector.tensor_tensor(actf[:, D * j:D * j + 512], actf[:, D * j:D * j + 512],
                                            actf[:, D * j + 512:D * j + D], ALU.add)
                if j == 0:
                    x.then_inc(halved, 1)
            ve.wait_ge(halved, 1)
            link(x)
            link(nc.vector.tensor_tensor(actf[:, 0:512], actf[:, 0:512], actf[:, D:D + 512], ALU.add))
            nc.vector.tensor_tensor(actf[:, 0:S], actf[:, 0:S], actf[:, S:2 * S], ALU.add).then_inc(squares_summed, 1)
            ve.wait_ge(std_ready, 1)
            link(nc.vector.reciprocal(softf[:, S:2 * S], softf[:, 0:S]))
            def normalise(g):
                part = v[:, 2 * g:2 * g + 2, :]
                nc.vector.tensor_tensor(part, part, softf[:, S:2 * S].unsqueeze(1).broadcast_to([P, 2, S]),
                                        ALU.mult).then_inc(normed, 1)

            def silu_halves(g):
                ve.wait_ge(silu_ready, 2 * g + 2)
                part = (slice(None), slice(2 * g, 2 * g + 2))
                nc.vector.tensor_copy(xn[0][part], v[part]).then_inc(silu_hi, 1)
                ve.wait_ge(silu_hi, g + 1)
                less_hi(xn[1][part], v[part], xn[0][part]).then_inc(silu_lo, 1)

            normalise(0)
            normalise(1)
            for g in range(4):
                silu_halves(g)
                if g + 2 < 4:
                    normalise(g + 2)

            def norm(k):
                add(k)
                take(k)
                through(last_before(k) + 3)

            def glu(which):
                stage = f"ffn{which}"
                for ft in range(FT):
                    through(chunk_of[stage + "_in"][ft] + 2)
                    n, b = UP0[stage] + ft, slice(S * (ft % 4), S * (ft % 4) + S)
                    ve.wait_ge(gate_act, n + 1)
                    nc.vector.tensor_tensor(ptf[:, b], bank[ft % 4][:, S:2 * S], softf[:, b],
                                            ALU.mult).then_inc(glu_done, 1)
                    ve.wait_ge(ffa_hi, FT * which + ft + 1)
                    less_hi(ffa[1][:, ft % 4, :], ptf[:, b], ffa[0][:, ft % 4, :]).then_inc(ffa_ready, 1)

            norm(FFN0)
            glu(0)
            norm(NSA)

            ve.wait_ge(kv_done, 1)
            ve.wait_ge(window_zero, 1)
            for b in range(2):
                kv = bank[4][:, S * b:S * b + S].rearrange("p (n l) -> p l n", l=16)
                for part in range(2):
                    ls = slice(16 * part, 16 * part + 16)
                    for g in range(GROUPS):
                        half = slice(DH * g, DH * g + DH)
                        nc.vector.tensor_tensor(window[half, b, ls, g, :], kv[half, :, part:part + NCMP],
                                                posT[half, b, ls].unsqueeze(2).broadcast_to([DH, 16, NCMP]),
                                                ALU.add).then_inc(window_ready, 1)
            ve.wait_ge(kv_done, 3)
            take(NSA, 1)
            through(chunk_of["q"][0])
            for half in range(2):
                nc.vector.tensor_copy(k2[DH * half:DH * half + DH, 0, :, :].rearrange("p b k -> p (b k)"),
                                      bank[5][0:DH, :]).then_inc(kv_dve, 1)
            through(chunk_of["q"][1])
            nc.vector.tensor_copy(vtok[:, :, :, :].rearrange("p t b c -> p (t b c)"),
                                  bank[6][:, :]).then_inc(kv_dve, 1)
            through(chunk_of["q"][2])
            ve.wait_ge(q_ready, 1)
            ve.wait_ge(consts_built, 9)
            link(nc.vector.tensor_scalar(gates[:, 0, 0:HEADS], gates[:, 0, 0:HEADS], valid[:, 0:1], None, ALU.mult))
            gate_of = gates[:, :, :].rearrange("p t (b h) -> p t b h", b=3)
            through(chunk_of["q"][3] + 1)

            def nsa_shift(i):
                ve.wait_ge(score_done, i + 1)
                ve.wait_ge(bias_built, i + 1)
                if i >= 3:
                    ve.wait_ge(p_turned, i - 2)
                for n, piece in enumerate(NSA_PIECES):
                    t, branch = n // 3, n % 3
                    if branch == 0:
                        src, bias = bank[i % 2][:, piece], biases[:, i, 3 * P + 16 * t:3 * P + 16 * t + NCMP]
                    elif t == 0:
                        src, bias = bank[i % 2][:, piece], biases[:, i, 0:P]
                    else:
                        src, bias = bank[2 + i % 2][:, S * (branch - 1):S * branch], biases[:, i, P:3 * P]
                    x = nc.vector.tensor_tensor_reduce(out=soft[:, i % 3, piece], in0=src, in1=bias,
                                                       scale=-DH ** -0.5, scalar=3e38, op0=ALU.add, op1=ALU.min,
                                                       accum_out=nmax[:, i % 2, n:n + 1])
                x.then_inc(shifted, 1)

            def nsa_inverse(i):
                ve.wait_ge(exp_done, i + 1)
                nc.vector.reciprocal(rcol[:, 0, 0:6], rsum[:, i % 2, :]).then_inc(inverse_ready, 1)

            def nsa_coef(i):
                ve.wait_ge(inverse_ready, i + 1)
                nc.vector.tensor_tensor(coef[:, i % 2, :].rearrange("p (t n) -> p t n", t=TT),
                                        rcol[:, 0, 0:6].rearrange("p (t n) -> p t n", t=TT),
                                        gate_of[:, :, :, i], ALU.mult).then_inc(coef_ready, 1)

            def nsa_weigh(i):
                ve.wait_ge(coef_ready, i + 1)
                for n, piece in enumerate(NSA_PIECES):
                    x = nc.vector.tensor_scalar(soft[:, i % 3, piece], soft[:, i % 3, piece], coef[:, i % 2, n:n + 1],
                                                None, ALU.mult)
                x.then_inc(weighed, 1)

            def nsa_evac(i):
                ve.wait_ge(p_turned, i + 1)
                if i >= 2:
                    ve.wait_ge(pv_done, i - 1)
                nc.vector.tensor_copy(pt[:, i % 2, 0:384], bank[4][:, 0:384])
                nc.vector.tensor_copy(pt[0:NCMP, i % 2, 768:768 + P], bank[4][0:NCMP, 384:512]).then_inc(pt_dve, 1)

            def nsa_out(ft):
                ve.wait_ge(o_hi, ft + 1)
                less_hi(xn[1][:, ft, :], bank[6 + ft % 2][:, 0:S], xn[0][:, ft, :]).then_inc(o_ready, 1)

            nsa_shift(0)
            nsa_shift(1)
            nsa_inverse(0)
            nsa_coef(0)
            for i in range(HEADS):
                nsa_weigh(i)
                if i + 2 < HEADS:
                    nsa_shift(i + 2)
                if i + 1 < HEADS:
                    nsa_inverse(i + 1)
                nsa_evac(i)
                if i + 1 < HEADS:
                    nsa_coef(i + 1)
                if i % 2 and i > 1:
                    nsa_out(i // 2 - 1)
            nsa_out(HEADS // 2 - 1)
            through(chunk_of["b_out"][2])

            norm(FFN1)
            glu(1)
            add(MID)
            ve.wait_ge(gains_loaded, 32)
            for t in range(TT):
                ve.wait_ge(rstd_ready, TT * MID + t + 1)
                nc.vector.scalar_tensor_tensor(out=h[:, t, :], in0=h[:, t, :],
                                               scalar=rstd[:, TT * MID + t:TT * MID + t + 1], in1=gain_row[:, :],
                                               op0=ALU.mult, op1=ALU.mult).then_inc(h_ready, 1)
            take(IN2)
            through(last_before(MID) + 3)
            before = links[0]
            for group in range(2):
                through(chunk_of["ml_qk"][2 * group + 1] + 2)
                ve.wait_ge(in2_act, 2 * group + 2)
                for j in range(TAPS2):
                    for f in range(4):
                        ft = 4 * group + f
                        src = u[:, ft, PAD - TAPS2 + 1 + j:PAD - TAPS2 + 1 + j + S]
                        tap = tapT[:, ft, TAPS + j:TAPS + j + 1]
                        if j == 0:
                            b = col["ml_conv_b_2"] + ft
                            x = nc.vector.tensor_scalar(v[:, ft, :], src, tap, vecT[:, b:b + 1], ALU.mult, ALU.add)
                        else:
                            ve.wait_ge(dve_link, before + 12 * group + 4 * (j - 1) + f + 1)
                            x = nc.vector.scalar_tensor_tensor(out=v[:, ft, :], in0=src, scalar=tap, in1=v[:, ft, :],
                                                               op0=ALU.mult, op1=ALU.add)
                        x.then_inc(conv4_done if j == TAPS2 - 1 else dve_link, 1)
            links[0] = before + 24
            through(chunk_of["ml_v"][1] + 2)
            ve.wait_ge(in2_done, 5)
            for t in range(TT):
                nc.vector.memset(mlv[:, t, :, MLD:MLV], 1.0)
                nc.vector.tensor_copy(mlv[:, t, :, 0:MLD],
                                      bank[4 + t][:, :].rearrange("p (h c) -> p h c", h=MLH)).then_inc(in2_dve, 1)

            through(chunk_of["ml_o"][1] + 2)
            ve.wait_ge(in2_act, 6)
            for t in range(TT):
                nc.vector.tensor_tensor(mlo[:, t, :], mlo[:, t, :], gain_ml[:, :], ALU.mult)
            through(chunk_of["fx_v"][1] + 2)
            ve.wait_ge(in2_done, 11)
            for t in range(TT):
                nc.vector.tensor_copy(fxv[:, t, :], bank[4 + t][:, :]).then_inc(in2_dve, 1)
            through(chunk_of["rows"][0] + 2)
            ve.wait_ge(in2_done, 12)
            nc.vector.tensor_copy(gtok[:, :, :].rearrange("p t c -> p (t c)"),
                                  bank[6][:, 0:32]).then_inc(gates_copied, 1)
            through(chunk_of["rows"][0] + 3)
            take(MEM)

            ve.wait_ge(in2_done, 13)
            ve.wait_ge(small_loaded, 16 * 6)
            for b in range(2):
                x = nc.vector.tensor_scalar(row[:, b, :], bank[6][0:FXH, S * b:S * b + S], gate_bias[:, b:b + 1],
                                            None, ALU.add)
            link(x)
            nc.vector.scalar_tensor_tensor(out=row[:, 2:4, :], in0=row[:, 0:2, :], scalar=-1.0, in1=row[:, 0:2, :],
                                           op0=ALU.mult, op1=ALU.min).then_inc(rows_done, 1)
            through(chunk_of["xkv_k"][3])
            ve.wait_ge(act_link, 1)
            nc.vector.tensor_scalar(row[:, 4:6, :], row[:, 2:4, :], 1.0, None, ALU.add).then_inc(rows_done, 1)
            ve.wait_ge(act_link, 2)
            link(nc.vector.scalar_tensor_tensor(out=row[:, 4:6, :], in0=row[:, 4:6, :], scalar=1.0,
                                                in1=row[:, 2:4, :], op0=ALU.subtract, op1=ALU.subtract))
            link(nc.vector.tensor_tensor(row[:, 6:8, :], row[:, 6:8, :], row[:, 4:6, :], ALU.subtract))
            link(nc.vector.scalar_tensor_tensor(out=row[:, 2:4, :], in0=row[:, 0:2, :], scalar=0.0,
                                                in1=row[:, 6:8, :], op0=ALU.min, op1=ALU.subtract))
            one = ones[0:FXH, 0:1].broadcast_to([FXH, S])
            for b in range(2):
                x = nc.vector.tensor_tensor_scan(row[:, 4 + b, :], one, row[:, 2 + b, :], 0.0, ALU.mult, ALU.add)
            link(x)
            nc.vector.tensor_scalar(row[:, 0, :], row[:, 4, :], -float(DH) ** 0.5, None, ALU.mult)
            link(nc.vector.scalar_tensor_tensor(out=row[:, 1, :], in0=bank[7][0:FXH, 0:S], scalar=gate_bias[:, 2:3],
                                                in1=row[:, 5, :], op0=ALU.add, op1=ALU.subtract))
            link(nc.vector.tensor_tensor_scan(row[:, 6, :], one, row[:, 1, :], 0.0, ALU.mult, ALU.max))
            nc.vector.tensor_scalar(row[:, 7, :], row[:, 6, :], -1.0, None, ALU.mult)
            nc.vector.scalar_tensor_tensor(out=row[:, 2, :], in0=row[:, 5, :], scalar=-1.0, in1=row[:, 6, :],
                                           op0=ALU.mult, op1=ALU.subtract).then_inc(rows_done, 1)
            through(chunk_of["xkv_v"][3])
            ve.wait_ge(cols_turned, 1)
            nc.vector.tensor_copy(rcol[:, :, :], bank[7][:, 0:16].rearrange("p (t n) -> p t n", t=TT)
                                  ).then_inc(rows_done, 1)

            def ml_shifted(i):
                ve.wait_ge(ml_score, i + 1)
                ve.wait_ge(consts_built, 9)
                w, m = soft[:, i % 2, :], bank[1 + 2 * (i % 2)]
                nc.vector.tensor_tensor(w[:, 0:S], m[:, 0:S], causalT[:, 0:S], ALU.add)
                nc.vector.tensor_tensor(w[:, S:3 * P], m[:, P:S], causalT[:, S:3 * P], ALU.add).then_inc(ml_shift, 1)

            def ml_weighed(i):
                ve.wait_ge(ml_exp, i + 1)
                if i >= 2:
                    ve.wait_ge(ml_num, i - 1)
                nc.vector.scalar_tensor_tensor(out=pt[:, i % 2, 0:3 * P], in0=bank[2 * (i % 2)][:, 0:3 * P],
                                               scalar=MLD ** -0.5, in1=soft[:, i % 2, 0:3 * P],
                                               op0=ALU.mult, op1=ALU.mult).then_inc(ml_weight, 1)

            numv = num.rearrange("p (t h) c -> p t h c", t=TT)

            def ml_take(i):
                ve.wait_ge(ml_num, i + 1)
                nc.vector.tensor_copy(numv[:, :, i, :], bank[4 + i % 2][:, 0:TT * MLV]
                                      .rearrange("p (t c) -> p t c", t=TT)).then_inc(ml_copied, 1)

            ml_shifted(0)
            ml_shifted(1)
            through(chunk_of["out2"][1])
            for i in range(MLH):
                ml_weighed(i)
                if i + 2 < MLH:
                    ml_shifted(i + 2)
                if i:
                    ml_take(i - 1)
            ml_take(MLH - 1)
            ve.wait_ge(act_link, 3)
            ve.wait_ge(ml_copied, MLH)
            d = num[:, :, MLD]
            link(nc.vector.scalar_tensor_tensor(out=den[:, 0, :], in0=d, scalar=-1.0, in1=d, op0=ALU.mult, op1=ALU.max))
            link(nc.vector.tensor_tensor(den[:, 1, :].rearrange("p (t h) -> p t h", t=TT),
                                         den[:, 0, :].rearrange("p (t h) -> p t h", t=TT),
                                         expm[:, :, 0:MLH], ALU.max))
            link(nc.vector.reciprocal(den[:, 2, :], den[:, 1, :]))
            nc.vector.tensor_tensor(num[:, :, 0:MLD], num[:, :, 0:MLD],
                                    den[:, 2, :].unsqueeze(2).broadcast_to([P, 8, MLD]), ALU.mult
                                    ).then_inc(ml_copied, 1)

            def fx_shift(i):
                n = HEADS + i
                ve.wait_ge(score_done, n + 1)
                if i >= 3:
                    ve.wait_ge(p_turned, n - 2)
                s, b = soft[:, i % 3, :], bank[2 * (i % 2)]
                nc.vector.tensor_tensor_reduce(out=s[:, 0:P], in0=b[:, 0:P], in1=causal[:, 0:P],
                                               scale=-DH ** -0.5, scalar=3e38, op0=ALU.add, op1=ALU.min,
                                               accum_out=nmax[:, i % 2, 0:1])
                nc.vector.tensor_tensor_reduce(out=s[:, P:3 * P], in0=b[:, P:3 * P], in1=causal[:, P:3 * P],
                                               scale=-DH ** -0.5, scalar=3e38, op0=ALU.add, op1=ALU.min,
                                               accum_out=nmax[:, i % 2, 1:2]).then_inc(shifted, 1)

            def row_weigh(n, i, pieces, buffer):
                ve.wait_ge(exp_done, n + 1)
                link(nc.vector.reciprocal(coef[:, i % 2, 0:2], rsum[:, i % 2, 0:2]))
                for t, piece in enumerate(pieces):
                    x = nc.vector.tensor_scalar(soft[:, buffer, piece], soft[:, buffer, piece],
                                                coef[:, i % 2, t:t + 1], None, ALU.mult)
                x.then_inc(weighed, 1)

            def fx_out(j):
                ve.wait_ge(o_hi, HEADS // 2 + j + 1)
                less_hi(xn[1][:, 4 + j, :], bank[1 + 2 * (j % 2)][:, 0:S], xn[0][:, 4 + j, :]).then_inc(o_ready, 1)

            def fx_weigh(i):
                row_weigh(HEADS + i, i, (slice(0, P), slice(P, 3 * P)), i % 3)

            fx_shift(0)
            fx_shift(1)
            for i in range(FXH):
                fx_weigh(i)
                if i + 2 < FXH:
                    fx_shift(i + 2)
                if i % 2 and i > 1:
                    fx_out(i // 2 - 1)
                if i == 1:
                    ve.wait_ge(act_link, 4)
                    nc.vector.tensor_reduce(den[:, 3, :], mlsq, AX.X, ALU.add).then_inc(ml_sq, 1)
                if i == 4:
                    ve.wait_ge(ml_rstd, 1)
                    link(nc.vector.tensor_tensor(num[:, :, 0:MLD], num[:, :, 0:MLD],
                                                 den[:, 5, :].unsqueeze(2).broadcast_to([P, 8, MLD]), ALU.mult))
                    for t in range(TT):
                        nc.vector.tensor_tensor(numv[:, t, :, 0:MLD], numv[:, t, :, 0:MLD],
                                                mlo[:, t, :].rearrange("p (h c) -> p h c", h=MLH),
                                                ALU.mult).then_inc(ml_out, 1)
            fx_out(FXH // 2 - 1)
            for t in range(TT):
                ve.wait_ge(o_hi, HEADS // 2 + FXH // 2 + t + 1)
                less_hi(xn[1][:, 0:MLH, tok(t)], bank[4 + t][:, :].rearrange("p (h c) -> p h c", h=MLH),
                        xn[0][:, 0:MLH, tok(t)]).then_inc(ml_ready, 1)

            norm(CROSS)
            through(chunk_of["xo"][1])

            def x_shift(i):
                ve.wait_ge(score_done, HEADS + FXH + i + 1)
                link(nc.vector.tensor_reduce(nmax[:, i % 2, 0:2], bank[4 + i % 2][:, :]
                                             .rearrange("p (t m) -> p t m", t=TT), AX.X, ALU.max, negate=True))
                nc.vector.tensor_scalar(nmax[:, i % 2, 2:4], nmax[:, i % 2, 0:2], XSCALE, None,
                                        ALU.mult).then_inc(shifted, 1)

            def x_out(i):
                ve.wait_ge(o_hi, HEADS // 2 + FXH // 2 + TT + i + 1)
                less_hi(xn[1][:, 2 * i:2 * i + 2, :].rearrange("p f t -> p (f t)"), bank[i][:, :],
                        xn[0][:, 2 * i:2 * i + 2, :].rearrange("p f t -> p (f t)")).then_inc(o_ready, 1)

            def x_weigh(i):
                row_weigh(HEADS + FXH + i, i, (slice(0, S), slice(S, 2 * S)), i % 2)

            x_shift(0)
            x_shift(1)
            x_weigh(0)
            for i in range(XH):
                if i + 1 < XH:
                    x_weigh(i + 1)
                if i + 2 < XH:
                    x_shift(i + 2)
                if i:
                    x_out(i - 1)
            x_out(XH - 1)

            norm(FF)
            for g in range(D_FF // S):
                through(chunk_of["ff_in"][g] + 2)
                n, b = UP0["ff"] + g, slice(512 * (g % 4), 512 * (g % 4) + 512)
                ve.wait_ge(gate_act, n + 1)
                nc.vector.scalar_tensor_tensor(out=ptf[:, b], in0=bank[g % 4][:, :], scalar=0.0,
                                               in1=softf[:, 512 * (g % 3):512 * (g % 3) + 512],
                                               op0=ALU.max, op1=ALU.mult).then_inc(glu_done, 1)
                f = (slice(None), slice(2 * (g % 2), 2 * (g % 2) + 2))
                ve.wait_ge(ffa_hi, 2 * FT + g + 1)
                less_hi(ffa[1][f].rearrange("p f t -> p (f t)"), ptf[:, b],
                        ffa[0][f].rearrange("p f t -> p (f t)")).then_inc(ffa_ready, 1)
            add(LAST)
            ve.wait_ge(last_gain_loaded, 16)
            for t in range(TT):
                ve.wait_ge(rstd_ready, TT * LAST + t + 1)
                nc.vector.scalar_tensor_tensor(out=scaled[:, t, :], in0=h[:, t, :],
                                               scalar=rstd[:, TT * LAST + t:TT * LAST + t + 1], in1=gain_row[:, :],
                                               op0=ALU.mult, op1=ALU.mult).then_inc(out_ready, 1)

        @block.tensor
        def _(te):
            mm = nc.tensor.matmul

            turn_of = [0]

            def weights(stage, n, k, unsplit=False):
                c = chunk_of[stage][n]
                assert c == turn_of[0]
                turn_of[0] += 1
                if not is_split[c]:
                    te.wait_ge(raw_loaded[c % RAWS], loads_through(c))
                    return c, raw[c % RAWS]
                te.wait_ge(*lo_count(c))
                return c, [kn(s, used_cols[c] // k, k) for s in split_slot[nth[c] % SPLITS]]

            def used(c, x):
                x.then_inc(freed[c][0], 1)

            def mm3(dst, left, right, start, stop):
                mm(dst, left[0], right[0], start=start, stop=False)
                mm(dst, left[0], right[1], start=False, stop=False)
                return mm(dst, left[1], right[0], start=False, stop=stop)

            def part(pair, *index):
                return [x[index] for x in pair]

            ALL = slice(None)

            def turn(k, src=h):
                idx = turning.index(k)
                for t in range(TT):
                    te.wait_ge(root_diag_ready, TT * idx + t + 1)
                    for kt in range(KT):
                        x = mm(bank[kt // 2][:, S * (kt % 2) + P * t:S * (kt % 2) + P * t + P],
                               src[:, t, P * kt:P * kt + P], root_diag[:, t, :], start=True, stop=True)
                        if t == TT - 1 and kt % 2:
                            x.then_inc(turned, 1)

            def features(dst, w, c0, ready=None):
                for kt in range(KT):
                    if ready is not None and kt % 2 == 0:
                        te.wait_ge(xn_ready, ready + kt // 2 + 1)
                    x = mm3(dst, part(w, ALL, kt, slice(c0, c0 + P)), part(xn, ALL, kt, ALL),
                            kt == 0, kt == KT - 1)
                return x

            def tokens(dst, w, cols, t, k0=0, k1=KT, first=True, ready=None):
                for kt in range(k0, k1):
                    if ready:
                        te.wait_ge(*ready(kt))
                    x = mm3(dst, part(xn, ALL, kt, tok(t)), part(w, ALL, kt - k0, cols),
                            kt == 0 and first, kt == KT - 1)
                return x

            def feature_pair(stage, n, b, before=None, ready=None):
                c, w = weights(stage, n, KT)
                if before:
                    te.wait_ge(*before)
                for j in range(2):
                    x = features(bank[b][:, S * j:S * j + S], w, P * j, ready if j == 0 else None)
                used(c, x)

            def by_token(stage, n, b0, b1, each=None):
                for half in range(2):
                    c, w = weights(stage, n + half, 4)
                    for t, b in enumerate((b0, b1)):
                        x = tokens(bank[b][:, :], w, ALL, t, 4 * half, 4 * half + 4)
                        if half and each:
                            x.then_inc(each, 1)
                    if not (half and each):
                        used(c, x)

            def residual_product(stage, bias=False, ready=None, free=None):
                for col_half in range(2):
                    for half in range(2):
                        c, w = weights(stage, 2 * col_half + half, 4)
                        for t in range(TT):
                            dst = bank[4 + 2 * t + col_half][:, :]
                            if t and free and col_half == half == 0:
                                te.wait_ge(*free)
                            if bias and half == 0:
                                mm(dst, ones[0:1, :], pw2_row[0:1, 512 * col_half:512 * col_half + 512],
                                   start=True, stop=False)
                            x = tokens(dst, w, ALL, t, 4 * half, 4 * half + 4, first=not bias,
                                       ready=ready if col_half == 0 and t == 0 else None)
                            if half:
                                x.then_inc(acc_done, 1)
                        if half == 0:
                            used(c, x)

            def down(stage, g, count, ready):
                c, w = weights(stage, g, 2)
                te.wait_ge(ffa_ready, ready)
                for t in range(TT):
                    for half in range(2):
                        for q in range(2):
                            kt = 2 * g + q
                            x = mm3(bank[4 + 2 * t + half][:, :], part(ffa, ALL, kt % 4, tok(t)),
                                    part(w, ALL, q, slice(512 * half, 512 * half + 512)),
                                    kt == 0, kt == count - 1)
                        if kt == count - 1:
                            x.then_inc(acc_done, 1)
                if 2 * g + 2 < count:
                    used(c, x)

            te.wait_ge(consts_built, 1)
            te.wait_ge(vecs_loaded, 16 * len(act_loads))
            te.wait_ge(vecs_loaded_pool, 16 * len(pool_loads))
            te.wait_ge(vecs_loaded_sp, 16 * len(sp_loads))
            nc.tensor.transpose(bank[4][:, 0:P], vecs, ident[:, :]).then_inc(pre_turned, 1)
            turn(CONV)

            def turn_taps():
                te.wait_ge(taps_loaded, 16 * len(tap_loads))
                m = TAPS + TAPS2
                for k in range(KT):
                    x = nc.tensor.transpose(bank[5][:, m * k:m * k + m], taps[:, P * k:P * k + P], ident[0:m, 0:m])
                x.then_inc(pre_turned, 1)
                for b in range(2):
                    x = nc.tensor.transpose(bank[6][:, 32 * b:32 * b + 32], pos[:, P * b:P * b + P], ident[0:32, 0:32])
                x.then_inc(pre_turned, 1)

            for ft in range(KT):
                feature_pair("pw1", ft, ft % 4, (glu_done, ft - 3) if ft >= 4 else None,
                             xn_before[CONV] if ft == 0 else None)
                if ft == 0:
                    turn_taps()

            def mean(ft, dst, src, stage):
                x = mm(dst, mean_w[:, :], src, start=ft == 0, stop=ft == KT - 1)
                if ft == KT - 1:
                    x.then_inc(stat_done, 1)

            te.wait_ge(pads_zero, 2)
            te.wait_ge(consts_built, 9)
            for g, (ft, js) in enumerate(groups):
                te.wait_ge(glu_done, ft + 1)
                te.wait_ge(diag_built, g + 1)
                for q, j in enumerate(js):
                    x = mm(bank[ft][:, 0:S], diag[:, g % NDIAG, q, :], u[:, ft, j:j + S],
                           start=j == pe_taps[ft][0], stop=j == TAPS - 1)
                x.then_inc(diag_used, 1)
            te.wait_ge(glu_done, KT)
            order = list(range(SHARED + 1, KT)) + list(range(SHARED + 1))
            for n, ft in enumerate(order):
                if ft > SHARED:
                    te.wait_ge(conv_out, ft - SHARED)
                else:
                    te.wait_ge(conv_dve, ft + 1)
                x = mm(bank[0][:, 0:S], mean_w[:, :], v[:, ft, :], start=n == 0, stop=n == KT - 1)
            x.then_inc(stat_done, 1)
            te.wait_ge(squares_summed, 1)
            mm(bank[1][:, 0:S], mean_w[:, :], actf[:, 0:S], start=True, stop=True).then_inc(stat_done, 1)
            te.wait_ge(small_loaded, 16 * 6)
            residual_product("pw2", bias=True, ready=lambda kt: (silu_lo, kt // 2 + 1))

            def ffn(k, which):
                stage = f"ffn{which}"
                turn(k)
                for g in range(FC + 1):
                    if g < FC:
                        for ft in (2 * g, 2 * g + 1):
                            feature_pair(stage + "_in", ft, ft % 4,
                                         (glu_done, UP0[stage] + ft - 3) if ft >= 4 else None,
                                         xn_before[k] if ft == 0 else None)
                    if g:
                        down(stage + "_out", g - 1, FT, FT * which + 2 * g)

            ffn(FFN0, 0)

            turn(NSA)
            feature_pair("kv", 0, 4, ready=xn_before[NSA])
            feature_pair("kv", 1, 5)
            c, w = weights("kv", 2, KT)
            for t in range(TT):
                x = tokens(bank[6][:, S * t:S * t + S], w, ALL, t)
            used(c, x)
            te.wait_ge(window_ready, 8)
            for b in range(2):
                c, w = weights("phi", b, 1)
                w = w[:, :].rearrange("p (l e) -> p l e", e=DH)
                for l in range(32):
                    x = mm(bank[7][0:DH, 2 * NCMP * b:2 * NCMP * b + 2 * NCMP], w[:, l, :],
                           window[:, b, l, :, :].rearrange("p g n -> p (g n)"), start=l == 0, stop=l == 31)
                used(c, x)
            def nsa_score(i):
                if i >= 2:
                    te.wait_ge(shifted, i - 1)
                e, g = slice(DH * (i % 2), DH * (i % 2) + DH), i // (HEADS // GROUPS)
                x, y = bank[i % 2], bank[2 + i % 2]
                q0, q1 = qT[e, i // 2, 0:P], qT[e, i // 2, P:S]
                mm(x[:, 0:2 * P], q0, k2[e, g, :, 0:P], start=True, stop=True)
                mm(x[:, 256:271], q0, kcmp[e, g, :], start=True, stop=True)
                mm(x[:, 272:287], q1, kcmp[e, g, :], start=True, stop=True)
                mm(y[:, :], q1, k2[e, g, :, :].rearrange("p b k -> p (b k)"), start=True,
                   stop=True).then_inc(score_done, 1)

            te.wait_ge(xn_ready, xn_before[NSA] + 8)
            c, w = weights("gates", 0, KT)
            for t in range(TT):
                x = tokens(bank[4][:, 48 * t:48 * t + 48], w, ALL, t)
            used(c, x)
            for b in range(4):
                if b == 3:
                    te.wait_ge(q_ready, 3)
                    te.wait_ge(kv_act, 4)
                    te.wait_ge(kv_dve, 3)
                    nsa_score(0)
                    nsa_score(1)
                if b == 2:
                    te.wait_ge(q_ready, 1)
                feature_pair("q", b, Q_BANK[b])
                if b == 0:
                    te.wait_ge(kv_act, 3)
                    te.wait_ge(small_loaded, 16 * 6)
                    for e in range(2):
                        mm(bank[7][DH * e:DH * e + DH, 64:64 + GROUPS * NCMP], phi2[:, 0, :], hid[:, 0, :],
                           start=True, stop=True)
                    for g in range(GROUPS):
                        x = mm(bank[7][0:NCMP, P + DH * g:P + DH * g + DH],
                               hid[:, 1, NCMP * g:NCMP * g + NCMP], phi2[:, 1, :], start=True, stop=True)
                    x.then_inc(phi_done, 1)

            def nsa_turn(i):
                te.wait_ge(weighed, i + 1)
                if i:
                    te.wait_ge(pt_dve, i)
                    te.wait_ge(pt_act, i)
                s = soft[:, i % 3, :]
                turns = [(4, 0, 0), (4, P, 288), (4, 2 * P, 416), (5, 0, 128), (5, P, 544), (5, 2 * P, 672)]
                for b, at, src in turns:
                    nc.tensor.transpose(bank[b][:, at:at + P], s[:, src:src + P], ident[:, :])
                for t in range(TT):
                    x = nc.tensor.transpose(bank[4 + t][0:NCMP, 384:512],
                                            s[:, 256 + 16 * t:256 + 16 * t + NCMP], ident[:, :])
                x.then_inc(p_turned, 1)

            def nsa_pv(i):
                te.wait_ge(pt_dve, i + 1)
                te.wait_ge(pt_act, i + 1)
                ft, g = i // 2, i // (HEADS // GROUPS)
                if i % 2 == 0 and ft >= 2:
                    te.wait_ge(o_ready, ft - 1)
                dst = bank[6 + ft % 2][DH * (i % 2):DH * (i % 2) + DH, 0:S]
                d = slice(DH * g, DH * g + DH)
                for b in range(2):
                    mm(dst, vtok[:, 0, b, d], pt[:, i % 2, 384 * b:384 * b + S], start=b == 0, stop=False)
                    mm(dst[:, P:S], vtok[:, 1, b, d], pt[:, i % 2, 384 * b + S:384 * b + 384], start=False, stop=False)
                mm(dst, vcmp[:, d], pt[0:NCMP, i % 2, 768:1024], start=False, stop=True).then_inc(pv_done, 1)

            te.wait_ge(q_ready, 5)
            for i in range(HEADS):
                if i + 2 < HEADS:
                    nsa_score(i + 2)
                nsa_turn(i)
                if i:
                    nsa_pv(i - 1)
            nsa_pv(HEADS - 1)
            residual_product("b_out", ready=lambda kt: (o_ready, kt + 1), free=(o_ready, HEADS // 2 - 1))

            ffn(FFN1, 1)

            turn(IN2)
            for b in range(4):
                feature_pair("ml_qk", b, b, ready=xn_before[IN2] if b == 0 else None)
            by_token("ml_v", 0, 4, 5)
            by_token("ml_o", 0, 6, 7)
            for b in range(4):
                feature_pair("fx_q" if b < 2 else "fx_k", b % 2, b, (in2_act, b + 1))
            te.wait_ge(in2_dve, 2)
            by_token("fx_v", 0, 4, 5)
            te.wait_ge(in2_act, 6)
            c, w = weights("rows", 0, KT)
            for t in range(TT):
                x = tokens(bank[6][:, 16 * t:16 * t + 16], w, ALL, t)
            used(c, x)
            te.wait_ge(in2_act, 10)
            turn(MEM, memraw)
            te.wait_ge(gates_copied, 1)
            for dst, c0 in ((bank[6][0:FXH, 0:S], 8), (bank[6][0:FXH, S:2 * S], 4), (bank[7][0:FXH, 0:S], 0)):
                for t in range(TT):
                    x = nc.tensor.transpose(dst[:, tok(t)], gtok[:, t, c0:c0 + 8], ident[:, :])
            x.then_inc(in2_done, 1)
            for b in range(4):
                feature_pair("xkv_k", b, XKV_BANK[b], ready=xn_before[MEM] if b == 0 else None)
            te.wait_ge(in2_dve, 4)
            by_token("xkv_v", 0, XKV_BANK[4], XKV_BANK[5], each=xkv_done)
            te.wait_ge(rows_done, 3)
            for b, r in enumerate((1, 2)):
                for t in range(TT):
                    x = nc.tensor.transpose(bank[7][:, 16 * b + 8 * t:16 * b + 8 * t + 8], row[:, r, tok(t)],
                                            ident[0:FXH, 0:FXH])
            x.then_inc(cols_turned, 1)

            def all_rows(i):
                return ident[0:FXH, i:i + 1].broadcast_to([FXH, P])

            def mlstm_score(i):
                if i >= 2:
                    te.wait_ge(ml_weight, i - 1)
                s, m = bank[2 * (i % 2)], bank[1 + 2 * (i % 2)]
                mm(m[:, 0:S], all_rows(i), row[:, 7, :], start=True, stop=True)
                mm(s[:, 0:S], v[:, 4 + i, 0:P], v[:, i, :], start=True, stop=True)
                mm(s[:, S:3 * P], v[:, 4 + i, P:S], v[:, i, P:S], start=True, stop=True).then_inc(ml_score, 1)

            def mlstm_pv(i):
                te.wait_ge(ml_weight, i + 1)
                if i >= 2:
                    te.wait_ge(ml_copied, i - 1)
                dst, p = bank[4 + i % 2], pt[:, i % 2, :]
                mm(dst[:, 0:MLV], p[:, 0:P], mlv[:, 0, i, :], start=True, stop=True)
                mm(dst[:, MLV:2 * MLV], p[:, P:S], mlv[:, 0, i, :], start=True, stop=False)
                mm(dst[:, MLV:2 * MLV], p[:, S:3 * P], mlv[:, 1, i, :], start=False, stop=True).then_inc(ml_num, 1)

            te.wait_ge(xkv_act, 4)
            te.wait_ge(qk_ready, KT)
            mlstm_score(0)
            mlstm_score(1)
            te.wait_ge(xkv_act, 5)
            by_token("xkv_v", 2, XKV_BANK[6], XKV_BANK[7], each=xkv_done)
            te.wait_ge(xkv_act, 8)
            for i in range(MLH):
                if i + 2 < MLH:
                    mlstm_score(i + 2)
                mlstm_pv(i)

            def fx_score(i):
                n = HEADS + i
                if i < 2:
                    te.wait_ge(ml_weight, MLH)
                else:
                    te.wait_ge(shifted, n - 1)
                e, j = slice(DH * (i % 2), DH * (i % 2) + DH), i // 2
                s = bank[2 * (i % 2)]
                for t, cols, keys in ((0, slice(0, P), slice(0, P)), (1, slice(P, 3 * P), slice(0, S))):
                    mm(s[:, cols], qT[e, j, tok(t)], qT[e, 4 + j, keys], start=True, stop=False)
                    x = mm(s[:, cols], all_rows(i), row[:, 0, keys], start=False, stop=True)
                x.then_inc(score_done, 1)

            def fx_turn(i):
                n = HEADS + i
                te.wait_ge(weighed, n + 1)
                if i >= 2:
                    te.wait_ge(pt_act, n - 1)
                else:
                    te.wait_ge(act_link, 3)
                    te.wait_ge(rows_done, 4)
                for q in range(3):
                    x = nc.tensor.transpose(bank[6 + i % 2][:, P * q:P * q + P],
                                            soft[:, i % 3, P * q:P * q + P], ident[:, :])
                x.then_inc(p_turned, 1)

            def fx_pv(i):
                n, j = HEADS + i, i // 2
                te.wait_ge(pt_act, n + 1)
                if i % 2 == 0 and j >= 2:
                    te.wait_ge(o_ready, HEADS // 2 + j - 1)
                dst = bank[1 + 2 * (j % 2)][DH * (i % 2):DH * (i % 2) + DH, :]
                d = slice(DH * i, DH * i + DH)
                mm(dst[:, 0:S], fxv[:, 0, d], pt[:, i % 2, 0:S], start=True, stop=False)
                mm(dst[:, P:S], fxv[:, 1, d], pt[:, i % 2, S:3 * P], start=False, stop=True).then_inc(pv_done, 1)

            fx_score(0)
            fx_score(1)
            for i in range(FXH):
                if i + 2 < FXH:
                    fx_score(i + 2)
                fx_turn(i)
                if i:
                    fx_pv(i - 1)
            fx_pv(FXH - 1)
            te.wait_ge(ml_out, TT)
            for t in range(TT):
                for i in range(MLH):
                    x = nc.tensor.transpose(bank[4 + t][:, P * i:P * i + P], num[:, MLH * t + i, 0:MLD], ident[:, :])
                x.then_inc(ml_turned, 1)
            residual_product("out2", ready=lambda kt: (ml_ready, TT) if kt < MLH else (o_ready, HEADS // 2 + kt - 3))

            turn(CROSS)
            def x_score(i):
                if i >= 2:
                    te.wait_ge(exp_done, HEADS + FXH + i - 1)
                for t in range(TT):
                    for k in range(2):
                        x = mm(bank[4 + i % 2][:, S * t:S * t + S], qT[:, 2 * i + k, tok(t)],
                               memk[:, 2 * i + k, :], start=k == 0, stop=k == 1)
                x.then_inc(score_done, 1)

            for b in range(4):
                if b == 3:
                    te.wait_ge(q_ready, 7)
                    x_score(0)
                    x_score(1)
                feature_pair("xq", b, b, ready=xn_before[CROSS] if b == 0 else None)

            def x_turn(i):
                n = HEADS + FXH + i
                te.wait_ge(weighed, n + 1)
                if i >= 2:
                    te.wait_ge(pt_act, n - 1)
                for k in range(2):
                    for t in range(TT):
                        x = nc.tensor.transpose(bank[6 + i % 2][:, S * k + P * t:S * k + P * t + P],
                                                soft[:, i % 2, S * t + P * k:S * t + P * k + P], ident[:, :])
                x.then_inc(p_turned, 1)

            def x_pv(i):
                te.wait_ge(pt_act, HEADS + FXH + i + 1)
                for half in range(2):
                    at = S * i + P * half
                    for k in range(2):
                        x = mm(bank[i][:, S * half:S * half + S], memv[:, k, at:at + P],
                               pt[:, i % 2, S * k:S * k + S], start=k == 0, stop=k == 1)
                x.then_inc(pv_done, 1)

            te.wait_ge(q_ready, 9)
            for i in range(XH):
                if i + 2 < XH:
                    x_score(i + 2)
                x_turn(i)
                if i:
                    x_pv(i - 1)
            x_pv(XH - 1)
            residual_product("xo", ready=lambda kt: (o_ready, HEADS // 2 + FXH // 2 + kt // 2 + 1))

            turn(FF)
            for g in range(D_FF // S + 1):
                if g < D_FF // S:
                    feature_pair("ff_in", g, g % 4, (glu_done, UP0["ff"] + g - 3) if g >= 4 else None,
                                 xn_before[FF] if g == 0 else None)
                if g:
                    down("ff_out", g - 1, D_FF // P, 2 * FT + g)



_INS = ["x", "a_norm", "a_pw1_w", "a_pw1_b", "a_dw_w", "a_dw_b", "a_ln_g", "a_ln_b", "a_pw2_w", "a_pw2_b",
        "kv_norm", "w_kv", "cmp_pos_k", "cmp_pos_v", "phi_k_w1", "phi_k_w2", "phi_v_w1", "phi_v_w2", "b_norm",
        "b_w_in", "b_w_out", "ffn_norm", "ffn_w_in", "ffn_w_out", "final_norm", "mem_2", "ln1_2", "w_in_2",
        "ml_conv_w_2", "ml_conv_b_2", "ml_b_i_2", "ml_b_f_2", "ml_norm_2", "fx_b_f_2", "w_out_2", "ln_x_2",
        "ln_mem_2", "w_xq_2", "w_xkv_2", "w_xo_2", "ln2_2", "w_ff1_2", "w_ff2_2", "ln_f_2"]


def kernel(**inputs):
    import numpy as np
    import concourse.bacc as bacc
    from concourse.bass_utils import run_bass_kernel_spmd

    nc = bacc.Bacc("TRN2", target_bir_lowering=False, num_devices=1)
    arrays, aps = {}, {}
    for name in _INS:
        arrays[f"in_{name}"] = np.ascontiguousarray(inputs[name])
        aps[name] = nc.dram_tensor(f"in_{name}", arrays[f"in_{name}"].shape, F32, kind="ExternalInput").ap()
    out = nc.dram_tensor("out", (1, S, D), F32, kind="ExternalOutput").ap()
    build_kernel(nc, aps, out)
    result = run_bass_kernel_spmd(nc, [arrays], core_ids=[0])
    return result.results[0]["out"]
```
